# Optimizing a Trainium2 kernel written in Bass

```python
import jax, jax.numpy as jnp
from jax import lax
import numpy as np

D_MODEL = 1024
BATCH = 1
SEQ = 1024
DEPTH = 1
DEC_BATCH = 8
DEC_SEQ = 4
PAST_LEN = 4096
PAGE_SIZE = 128

MIX_WIDTH = D_MODEL
NSA_WIDTH = MIX_WIDTH // 2
POOL_WIDTH = MIX_WIDTH - NSA_WIDTH
HEAD_DIM = 64
N_HEADS = NSA_WIDTH // HEAD_DIM
N_KV_HEADS = 2
GROUP = N_HEADS // N_KV_HEADS
ROPE_DIM = HEAD_DIM // 4
ROPE_THETA = 500000.0
CMP_BLOCK = 32
CMP_STRIDE = 16
CMP_HIDDEN = 256
SLC_BLOCK = 64
TOPK_BLOCKS = 16
WINDOW = 512
Q_BLOCK = 128
POOL_WINDOWS = (2, 4, 8, 16)
POOL_GROUP_WIDTH = POOL_WIDTH // len(POOL_WINDOWS)
POOL_STATE = max(POOL_WINDOWS) - 1
D_FF = 2816
RMS_EPS = 1e-6
FORCE_SCORE = 1e4
NEG_INF = -1e30
ATTN_SCALE = HEAD_DIM ** -0.5

KV_WIDTH = 2 * N_KV_HEADS * HEAD_DIM
OFF_KV_CMP = NSA_WIDTH
OFF_KV_SLC = OFF_KV_CMP + KV_WIDTH
OFF_KV_WIN = OFF_KV_SLC + KV_WIDTH
OFF_GATE = OFF_KV_WIN + KV_WIDTH
OFF_POOL = OFF_GATE + 3 * N_HEADS
IN_WIDTH = OFF_POOL + POOL_WIDTH

kernel_name = 'nsa_pool_macaron_hybrid_step'

def rmsnorm(x, g):
    x32 = x.astype(jnp.float32)
    y = x32 * lax.rsqrt(jnp.mean(x32 * x32, axis=-1, keepdims=True) + RMS_EPS)
    return (y * g.astype(jnp.float32)).astype(x.dtype)

def swiglu_ffn(x, g, w_gate, w_up, w_down):
    h = rmsnorm(x, g)
    return (jax.nn.silu(h @ w_gate) * (h @ w_up)) @ w_down

def rope(x, pos):
    half = ROPE_DIM // 2
    inv = jnp.power(ROPE_THETA, -jnp.arange(half, dtype=jnp.float32) / half)
    ang = pos.astype(jnp.float32)[:, None] * inv[None, :]
    cos = jnp.cos(ang)[:, None, :].astype(x.dtype)
    sin = jnp.sin(ang)[:, None, :].astype(x.dtype)
    x1 = x[..., :half]
    x2 = x[..., half:ROPE_DIM]
    return jnp.concatenate([x1 * cos - x2 * sin, x1 * sin + x2 * cos, x[..., ROPE_DIM:]], axis=-1)

def masked_softmax(s, mask):
    s = jnp.where(mask, s, NEG_INF)
    m = jnp.max(s, axis=-1, keepdims=True)
    e = jnp.where(mask, jnp.exp(s - m), 0.0)
    return e / jnp.maximum(jnp.sum(e, axis=-1, keepdims=True), 1e-30)

def pad_rows(x, mult):
    pad = (-x.shape[1]) % mult
    return jnp.pad(x, [(0, 0), (0, pad)] + [(0, 0)] * (x.ndim - 2))

def in_project(h, w_in, pos):
    B, T, _ = h.shape
    z = h @ w_in
    q = rope(z[..., :OFF_KV_CMP].reshape(B, T, N_HEADS, HEAD_DIM), pos)

    def kv(off):
        r = z[..., off:off + KV_WIDTH].reshape(B, T, 2, N_KV_HEADS, HEAD_DIM)
        return jnp.stack([rope(r[:, :, 0], pos), r[:, :, 1]], axis=2)

    gates = jax.nn.sigmoid(z[..., OFF_GATE:OFF_POOL].astype(jnp.float32)).astype(h.dtype)
    gates = gates.reshape(B, T, N_HEADS, 3)
    u = z[..., OFF_POOL:]
    return q, kv(OFF_KV_CMP), kv(OFF_KV_SLC), kv(OFF_KV_WIN), gates, u

def cmp_chunk_proj(k, w1):
    B, T, G, D = k.shape
    chunks = k.reshape(B, T // CMP_STRIDE, CMP_STRIDE, G, D)
    w = w1.reshape(CMP_BLOCK // CMP_STRIDE, CMP_STRIDE, D, CMP_HIDDEN)
    return jnp.einsum('bcsgd,hsdf->bcghf', chunks, w)

def cmp_blocks(proj, w1, w2, pe):
    n_slots = CMP_BLOCK // CMP_STRIDE
    n_blk = proj.shape[1] - n_slots + 1
    acc = sum(proj[:, h:h + n_blk, :, h] for h in range(n_slots))
    bias = pe.reshape(-1) @ w1
    return jax.nn.gelu(acc + bias) @ w2

def compress_kv(row_list, cmpw):
    w_k1, w_k2, pe_k, w_v1, w_v2, pe_v = cmpw

    def one(i, w1, w2, pe):
        proj = jnp.concatenate([cmp_chunk_proj(r[:, :, i], w1) for r in row_list], axis=1)
        return cmp_blocks(proj, w1, w2, pe)

    return one(0, w_k1, w_k2, pe_k), one(1, w_v1, w_v2, pe_v)

def compressed_attention(q, kc, vc, q_pos):
    B, T = q.shape[:2]
    n_blk = kc.shape[1]
    qg = q.reshape(B, T, N_KV_HEADS, GROUP, HEAD_DIM)
    s = jnp.einsum('btgrd,bngd->bgrtn', qg, kc).astype(jnp.float32) * ATTN_SCALE
    blk_end = jnp.arange(n_blk) * CMP_STRIDE + CMP_BLOCK - 1
    p = masked_softmax(s, blk_end[None, :] <= q_pos[:, None])
    o = jnp.einsum('bgrtn,bngd->btgrd', p.astype(vc.dtype), vc).reshape(B, T, N_HEADS, HEAD_DIM)
    return o, jnp.sum(p, axis=2)

def select_blocks(p_grp, q_pos, n_slc):
    n_cmp = p_grp.shape[-1]
    c0 = jnp.arange(n_cmp)[:, None] * CMP_STRIDE
    s0 = jnp.arange(n_slc)[None, :] * SLC_BLOCK
    overlap = jnp.clip(jnp.minimum(c0 + CMP_BLOCK, s0 + SLC_BLOCK) - jnp.maximum(c0, s0), 0, None)
    agg = (overlap / CMP_BLOCK).astype(jnp.float32)
    p_slc = jnp.einsum('bgtn,nj->bgtj', p_grp, agg)
    cur = (q_pos // SLC_BLOCK)[:, None]
    j = jnp.arange(n_slc)[None, :]
    forced = (j == 0) | (j == cur) | (j == cur - 1)
    score = jnp.where(forced, FORCE_SCORE, jnp.where(j <= cur, p_slc, NEG_INF))
    _, idx = lax.top_k(score, min(TOPK_BLOCKS, n_slc))
    return idx.astype(jnp.int32)

def selected_core(q, kg, vg, idx, q_pos):
    Q = q.shape[0]
    s = jnp.einsum('qgrd,gqkpd->gqrkp', q, kg).astype(jnp.float32) * ATTN_SCALE
    G_, _, R_, K_, P_ = s.shape
    kpos = idx[..., None] * SLC_BLOCK + jnp.arange(SLC_BLOCK)
    mask = (kpos <= q_pos[None, :, None, None]).reshape(G_, Q, 1, K_ * P_)
    p = masked_softmax(s.reshape(G_, Q, R_, K_ * P_), mask).reshape(s.shape)
    o = jnp.einsum('gqrkp,gqkpd->qgrd', p.astype(vg.dtype), vg)
    return o.reshape(Q, N_HEADS, HEAD_DIM)

def selected_prompt(q, kv_slc, idx, pos):
    B, S = q.shape[:2]
    qb_len = min(Q_BLOCK, S)
    nqb = S // qb_len
    kvb = kv_slc.reshape(B, S // SLC_BLOCK, SLC_BLOCK, 2, N_KV_HEADS, HEAD_DIM)
    qs = q.reshape(B * nqb, qb_len, N_KV_HEADS, GROUP, HEAD_DIM)
    ib = idx.reshape(B, N_KV_HEADS, nqb, qb_len, -1).transpose(0, 2, 1, 3, 4)
    ib = ib.reshape(B * nqb, N_KV_HEADS, qb_len, -1)
    pb = jnp.broadcast_to(pos.reshape(1, nqb, qb_len), (B, nqb, qb_len)).reshape(B * nqb, qb_len)
    bi = jnp.repeat(jnp.arange(B, dtype=jnp.int32), nqb)
    gi = jnp.arange(N_KV_HEADS)[:, None, None]

    def body(args):
        qb, ibk, pq, b = args
        blk = kvb[b, ibk, :, :, gi]
        return selected_core(qb, blk[..., 0, :], blk[..., 1, :], ibk, pq)

    o = lax.map(body, (qs, ib, pb, bi))
    return o.reshape(B, S, N_HEADS, HEAD_DIM)

def selected_sample(q, cache_kv_slc, kv_new, page_table, idx, q_pos):
    DB, DS = q.shape[:2]
    past_len = page_table.shape[1] * PAGE_SIZE
    npb = past_len // SLC_BLOCK
    bpp = PAGE_SIZE // SLC_BLOCK
    pool = cache_kv_slc.reshape(-1, bpp, SLC_BLOCK, 2, N_KV_HEADS, HEAD_DIM)
    newb = pad_rows(kv_new, SLC_BLOCK).reshape(DB, -1, SLC_BLOCK, 2, N_KV_HEADS, HEAD_DIM)
    nnb = newb.shape[1]
    bi = jnp.arange(DB)[:, None, None, None]
    gi = jnp.arange(N_KV_HEADS)[None, :, None, None]
    jp = jnp.minimum(idx, npb - 1)
    phys = page_table[bi, jp // bpp]
    past_blk = pool[phys, jp % bpp, :, :, gi]
    jn = jnp.clip(idx - npb, 0, nnb - 1)
    new_blk = newb[bi, jn, :, :, gi]
    blk = jnp.where((idx >= npb)[..., None, None, None], new_blk, past_blk)
    qs = q.reshape(DB, DS, N_KV_HEADS, GROUP, HEAD_DIM)
    return jax.vmap(selected_core, in_axes=(0, 0, 0, 0, None))(
        qs, blk[..., 0, :], blk[..., 1, :], idx, q_pos)

def window_core(q, kv, q_pos, k_pos):
    B, Q = q.shape[:2]
    qg = q.reshape(B, Q, N_KV_HEADS, GROUP, HEAD_DIM)
    s = jnp.einsum('bqgrd,bkgd->bgrqk', qg, kv[:, :, 0]).astype(jnp.float32) * ATTN_SCALE
    diff = q_pos[:, None] - k_pos[None, :]
    mask = (diff >= 0) & (diff <= WINDOW) & (k_pos[None, :] >= 0)
    p = masked_softmax(s, mask)
    o = jnp.einsum('bgrqk,bkgd->bqgrd', p.astype(kv.dtype), kv[:, :, 1])
    return o.reshape(B, Q, N_HEADS, HEAD_DIM)

def window_prompt(q, kv_win):
    B, S = q.shape[:2]
    qb_len = min(Q_BLOCK, S)
    nqb = S // qb_len
    kvp = jnp.pad(kv_win, ((0, 0), (WINDOW, 0), (0, 0), (0, 0), (0, 0)))

    def body(n):
        start = n * qb_len
        qb = lax.dynamic_slice_in_dim(q, start, qb_len, axis=1)
        kb = lax.dynamic_slice_in_dim(kvp, start, WINDOW + qb_len, axis=1)
        q_pos = start + jnp.arange(qb_len)
        k_pos = start - WINDOW + jnp.arange(WINDOW + qb_len)
        return window_core(qb, kb, q_pos, k_pos)

    o = lax.map(body, jnp.arange(nqb))
    return o.transpose(1, 0, 2, 3, 4).reshape(B, S, N_HEADS, HEAD_DIM)

def pool_mixer(u_ext, pos_ext, n_out, w_pool, pool_scale):
    T = u_ext.shape[1]
    u32 = u_ext.astype(jnp.float32)
    cs = jnp.pad(jnp.cumsum(u32, axis=1), ((0, 0), (1, 0), (0, 0)))
    t = jnp.arange(T - n_out, T)
    pos = pos_ext[T - n_out:]
    outs = []
    for g, w in enumerate(POOL_WINDOWS):
        c0, c1 = g * POOL_GROUP_WIDTH, (g + 1) * POOL_GROUP_WIDTH
        lo = jnp.maximum(t + 1 - w, 0)
        win_sum = cs[:, t + 1, c0:c1] - cs[:, lo, c0:c1]
        cnt = jnp.minimum(w, pos + 1).astype(jnp.float32)[None, :, None]
        d = (win_sum / cnt - u32[:, T - n_out:, c0:c1]).astype(u_ext.dtype)
        outs.append(d @ w_pool[g])
    return jnp.concatenate(outs, axis=-1) * pool_scale

def merge_heads(o_c, o_s, o_w, gates, pool_out, w_out):
    B, T = o_c.shape[:2]
    o = gates[..., 0:1] * o_c + gates[..., 1:2] * o_s + gates[..., 2:3] * o_w
    return jnp.concatenate([o.reshape(B, T, NSA_WIDTH), pool_out], axis=-1) @ w_out

def prompt_mixer(h, pos, w_in, cmpw, w_pool, pool_scale, w_out):
    S = h.shape[1]
    q, kv_c, kv_s, kv_w, gates, u = in_project(h, w_in, pos)
    kc, vc = compress_kv([pad_rows(kv_c, CMP_STRIDE)], cmpw)
    o_c, p_grp = compressed_attention(q, kc, vc, pos)
    idx = select_blocks(p_grp, pos, -(-S // SLC_BLOCK))
    o_s = selected_prompt(q, kv_s, idx, pos)
    o_w = window_prompt(q, kv_w)
    pool_out = pool_mixer(u, pos, S, w_pool, pool_scale)
    out = merge_heads(o_c, o_s, o_w, gates, pool_out, w_out)
    new = (kv_c, kv_s, kv_w[:, S - min(WINDOW, S):], u[:, S - POOL_STATE:])
    return out, new

def sample_mixer(h, pos, cache_kv_cmp, cache_kv_slc, page_table, st_win, st_pool,
                 w_in, cmpw, w_pool, pool_scale, w_out):
    DB, DS = h.shape[:2]
    past_len = page_table.shape[1] * PAGE_SIZE
    q, kv_c, kv_s, kv_w, gates, u = in_project(h, w_in, pos)
    past_c = cache_kv_cmp[page_table].reshape(DB, past_len, 2, N_KV_HEADS, HEAD_DIM)
    kc, vc = compress_kv([past_c, pad_rows(kv_c, CMP_STRIDE)], cmpw)
    o_c, p_grp = compressed_attention(q, kc, vc, pos)
    idx = select_blocks(p_grp, pos, -(-(past_len + DS) // SLC_BLOCK))
    o_s = selected_sample(q, cache_kv_slc, kv_s, page_table, idx, pos)
    wb = st_win.shape[1]
    win_ext = jnp.concatenate([st_win, kv_w], axis=1)
    o_w = window_core(q, win_ext, pos, past_len - wb + jnp.arange(wb + DS))
    ps = st_pool.shape[1]
    pool_ext = jnp.concatenate([st_pool, u], axis=1)
    pool_out = pool_mixer(pool_ext, past_len - ps + jnp.arange(ps + DS), DS, w_pool, pool_scale)
    out = merge_heads(o_c, o_s, o_w, gates, pool_out, w_out)
    new = (kv_c, kv_s, win_ext[:, DS:], pool_ext[:, DS:])
    return out, new

def setup_inputs(seed: int = 0) -> dict:
    key = jax.random.key(seed)
    ks = jax.random.split(key, 32)
    n_pages = PAST_LEN // PAGE_SIZE
    n_used = DEC_BATCH * n_pages
    n_phys = n_used + (n_used + 3) // 4

    def nrm(k, shape, scale):
        return jax.random.normal(k, shape, jnp.float32) * scale

    def gain(k, shape):
        return 1.0 + 0.05 * jax.random.normal(k, shape, jnp.float32)

    kv_shape = (DEPTH, n_phys, PAGE_SIZE, 2, N_KV_HEADS, HEAD_DIM)
    page_table = jax.random.permutation(ks[4], n_phys)[:n_used].reshape(DEC_BATCH, n_pages).astype(jnp.int32)
    return {
        'x_prompt': nrm(ks[0], (BATCH, SEQ, D_MODEL), 1.0),
        'x_sample': nrm(ks[1], (DEC_BATCH, DEC_SEQ, D_MODEL), 1.0),
        'cache_kv_cmp': nrm(ks[2], kv_shape, 1.0),
        'cache_kv_slc': nrm(ks[3], kv_shape, 1.0),
        'page_table': page_table,
        'state_kv_win': nrm(ks[5], (DEPTH, DEC_BATCH, min(WINDOW, PAST_LEN), 2, N_KV_HEADS, HEAD_DIM), 1.0),
        'state_pool': nrm(ks[6], (DEPTH, DEC_BATCH, POOL_STATE, POOL_WIDTH), 1.0),
        'n_ffn1': gain(ks[7], (DEPTH, D_MODEL)),
        'w_ffn1_gate': nrm(ks[8], (DEPTH, D_MODEL, D_FF), D_MODEL ** -0.5),
        'w_ffn1_up': nrm(ks[9], (DEPTH, D_MODEL, D_FF), D_MODEL ** -0.5),
        'w_ffn1_down': nrm(ks[10], (DEPTH, D_FF, D_MODEL), D_FF ** -0.5),
        'n_mix': gain(ks[11], (DEPTH, D_MODEL)),
        'w_in': nrm(ks[12], (DEPTH, D_MODEL, IN_WIDTH), D_MODEL ** -0.5),
        'w_cmp_k1': nrm(ks[13], (DEPTH, CMP_BLOCK * HEAD_DIM, CMP_HIDDEN), (CMP_BLOCK * HEAD_DIM) ** -0.5),
        'w_cmp_k2': nrm(ks[14], (DEPTH, CMP_HIDDEN, HEAD_DIM), CMP_HIDDEN ** -0.5),
        'pe_cmp_k': nrm(ks[15], (DEPTH, CMP_BLOCK, HEAD_DIM), 0.1),
        'w_cmp_v1': nrm(ks[16], (DEPTH, CMP_BLOCK * HEAD_DIM, CMP_HIDDEN), (CMP_BLOCK * HEAD_DIM) ** -0.5),
        'w_cmp_v2': nrm(ks[17], (DEPTH, CMP_HIDDEN, HEAD_DIM), CMP_HIDDEN ** -0.5),
        'pe_cmp_v': nrm(ks[18], (DEPTH, CMP_BLOCK, HEAD_DIM), 0.1),
        'w_pool': nrm(ks[19], (DEPTH, len(POOL_WINDOWS), POOL_GROUP_WIDTH, POOL_GROUP_WIDTH), POOL_GROUP_WIDTH ** -0.5),
        'pool_scale': gain(ks[20], (DEPTH, POOL_WIDTH)),
        'w_out': nrm(ks[21], (DEPTH, MIX_WIDTH, D_MODEL), MIX_WIDTH ** -0.5),
        'n_ffn2': gain(ks[22], (DEPTH, D_MODEL)),
        'w_ffn2_gate': nrm(ks[23], (DEPTH, D_MODEL, D_FF), D_MODEL ** -0.5),
        'w_ffn2_up': nrm(ks[24], (DEPTH, D_MODEL, D_FF), D_MODEL ** -0.5),
        'w_ffn2_down': nrm(ks[25], (DEPTH, D_FF, D_MODEL), D_FF ** -0.5),
        'n_final': gain(ks[26], (D_MODEL,)),
    }

def reference(x_prompt, x_sample, cache_kv_cmp, cache_kv_slc, page_table, state_kv_win, state_pool,
              n_ffn1, w_ffn1_gate, w_ffn1_up, w_ffn1_down, n_mix, w_in,
              w_cmp_k1, w_cmp_k2, pe_cmp_k, w_cmp_v1, w_cmp_v2, pe_cmp_v,
              w_pool, pool_scale, w_out, n_ffn2, w_ffn2_gate, w_ffn2_up, w_ffn2_down, n_final):
    seq = x_prompt.shape[1]
    dec_seq = x_sample.shape[1]
    past_len = page_table.shape[1] * PAGE_SIZE
    pos_p = jnp.arange(seq, dtype=jnp.int32)
    pos_s = past_len + jnp.arange(dec_seq, dtype=jnp.int32)
    xp, xs = x_prompt, x_sample
    st_p = ([], [], [], [])
    st_s = ([], [], [], [])
    for l in range(DEPTH):
        ffn1 = (n_ffn1[l], w_ffn1_gate[l], w_ffn1_up[l], w_ffn1_down[l])
        ffn2 = (n_ffn2[l], w_ffn2_gate[l], w_ffn2_up[l], w_ffn2_down[l])
        cmpw = (w_cmp_k1[l], w_cmp_k2[l], pe_cmp_k[l], w_cmp_v1[l], w_cmp_v2[l], pe_cmp_v[l])
        xp = xp + 0.5 * swiglu_ffn(xp, *ffn1)
        xs = xs + 0.5 * swiglu_ffn(xs, *ffn1)
        mix_p, new_p = prompt_mixer(rmsnorm(xp, n_mix[l]), pos_p, w_in[l], cmpw,
                                    w_pool[l], pool_scale[l], w_out[l])
        mix_s, new_s = sample_mixer(rmsnorm(xs, n_mix[l]), pos_s, cache_kv_cmp[l], cache_kv_slc[l],
                                    page_table, state_kv_win[l], state_pool[l], w_in[l], cmpw,
                                    w_pool[l], pool_scale[l], w_out[l])
        xp = xp + mix_p
        xs = xs + mix_s
        xp = xp + 0.5 * swiglu_ffn(xp, *ffn2)
        xs = xs + 0.5 * swiglu_ffn(xs, *ffn2)
        for lst, a in zip(st_p, new_p):
            lst.append(a)
        for lst, a in zip(st_s, new_s):
            lst.append(a)
    y_prompt = rmsnorm(xp, n_final)
    y_sample = rmsnorm(xs, n_final)
    new_kv_cmp_prompt = jnp.stack(st_p[0])
    new_kv_slc_prompt = jnp.stack(st_p[1])
    new_kv_win_prompt = jnp.stack(st_p[2])
    new_pool_prompt = jnp.stack(st_p[3])
    new_kv_cmp_sample = jnp.stack(st_s[0])
    new_kv_slc_sample = jnp.stack(st_s[1])
    new_kv_win_sample = jnp.stack(st_s[2])
    new_pool_sample = jnp.stack(st_s[3])
    return (y_prompt, y_sample, new_kv_cmp_prompt, new_kv_slc_prompt, new_kv_win_prompt, new_pool_prompt,
            new_kv_cmp_sample, new_kv_slc_sample, new_kv_win_sample, new_pool_sample)


_drawn_inputs = setup_inputs


def setup_inputs(seed=0):
    import zlib

    import numpy as np

    out = dict(_drawn_inputs(seed))
    spreads = {}
    factors = {'cache_kv_cmp': 2.855,
     'cache_kv_slc': 3.316,
     'n_ffn1': 2.701,
     'pe_cmp_k': 8.0,
     'pe_cmp_v': 3.224,
     'n_ffn2': 3.301,
     'pool_scale': 4.015}
    for name, (base, spread) in spreads.items():
        noise = np.random.default_rng([zlib.crc32(name.encode()), seed]).standard_normal(out[name].shape)
        drawn = base * np.exp(spread * noise) if base else spread * noise
        out[name] = __import__('jax').numpy.asarray(drawn.astype(out[name].dtype))
    for name, factor in factors.items():
        out[name] = (out[name] * factor).astype(out[name].dtype)
    return out
```

```python
from contextlib import ExitStack

import numpy as np

import concourse.bass as bass
from concourse import mybir

F32 = mybir.dt.float32
F32R = mybir.dt.float32r
I32 = mybir.dt.int32
ACT = mybir.ActivationFunctionType
ALU = mybir.AluOpType
AX = mybir.AxisListType

P = 128
BANK = 512
D_MODEL, SEQ, DEC_BATCH, DEC_SEQ = 1024, 1024, 8, 4
PAST_LEN, PAGE, WINDOW = 4096, 128, 512
N_SAMPLE = DEC_BATCH * DEC_SEQ
T = SEQ + N_SAMPLE
CHUNKS = 3
CH = T // CHUNKS
KT = D_MODEL // P
TT = SEQ // P + 1
D_FF = 2816
FT = D_FF // P
HD, N_HEADS, N_KV, GROUP = 64, 8, 2, 4
NSA_WIDTH, POOL_WIDTH, KV_WIDTH = 512, 512, 256
OFF_CMP, OFF_SLC, OFF_WIN, OFF_GATE = 512, 768, 1024, 1280
OFF_POOL = OFF_GATE + 3 * N_HEADS
IN_WIDTH = OFF_POOL + POOL_WIDTH
CMP_STRIDE, CMP_HIDDEN, CMP_BLOCK = 16, 256, 32
SLC_BLOCK = 64
POOL_WINDOWS = (2, 4, 8, 16)
POOL_STATE = 15
SCALE = HD ** -0.5
EPS = 1e-6
NEG = -1e30


class Order:

    def __init__(self, sem):
        self.sem, self.n = sem, 0

    def did(self, instruction):
        instruction.then_inc(self.sem, 1)
        self.n += 1
        return instruction

    def wait(self, engine):
        engine.wait_ge(self.sem, self.n)


class Mem:

    def __init__(self, nc):
        self.nc, self.serial, self.stage_sems = nc, 0, []

    def sem(self, name):
        self.stage_sems.append(self.lasting_sem(name))
        return self.stage_sems[-1]

    def lasting_sem(self, name):
        self.serial += 1
        return self.nc.alloc_semaphore(name=f"{name}_{self.serial}")

    def end_stage(self):
        self.nc.clear_and_free_semaphores(self.stage_sems)
        self.nc.all_engine_barrier()
        self.stage_sems = []

    def sb(self, stack, name, shape, dt=F32):
        self.serial += 1
        return stack.enter_context(self.nc.sbuf_tensor(f"{name}_{self.serial}", shape, dt))

    def ps(self, stack, name, shape=(P, BANK)):
        self.serial += 1
        return stack.enter_context(self.nc.psum_tensor(f"{name}_{self.serial}", list(shape), F32))


def product3(pe, out, w_hi, w_lo, x_hi, x_lo, first, last):
    pe.matmul(out, w_hi, x_hi, start=first, stop=False)
    pe.matmul(out, w_hi, x_lo, start=False, stop=False)
    return pe.matmul(out, w_lo, x_hi, start=False, stop=last)


def chunk(c):
    return slice(c * CH, (c + 1) * CH)


class Norm:

    def __init__(self, mem, scope, K, name, split=True):
        self.K = K
        self.sq = mem.sb(scope, name + "_sq", [P, KT, CH])
        self.var = mem.sb(scope, name + "_var", [P, CH])
        self.rms = mem.sb(scope, name + "_rms", [P, CH])
        self.inv = mem.sb(scope, name + "_inv", [P, CH])
        self.tmp = mem.sb(scope, name + "_tmp", [P, CH])
        self.gain = mem.sb(scope, name + "_gain", [P, KT])
        self.h = self.sq
        self.split = split
        self.gain_in = mem.sem(name + "_gain_in")
        self.sq_done = mem.sem(name + "_sq_done")
        self.sum_done = mem.sem(name + "_sum_done")
        self.var_done = mem.sem(name + "_var_done")
        self.rms_done = mem.sem(name + "_rms_done")
        self.h_done = mem.sem(name + "_h_done")
        self.hi_done = mem.sem(name + "_hi_done")
        self.dve_step = mem.sem(name + "_dve_step")
        self.ready = mem.sem(name + "_ready")

    def load(self, sp, gain):
        sp.dma_start(self.gain[:], gain).then_inc(self.gain_in, 16)

    def scalar(self, act, xT, h_hi):
        for c in range(CHUNKS):
            if c:
                act.wait_ge(self.ready, c)
            act.activation(self.sq[:], xT[:, :, chunk(c)], ACT.Square).then_inc(self.sq_done, 1)
            act.wait_ge(self.var_done, c + 1)
            act.activation(self.rms[:], self.var[:], ACT.Sqrt).then_inc(self.rms_done, 1)
            if self.split:
                act.wait_ge(self.h_done, c + 1)
                act.activation(h_hi[:, :, chunk(c)], self.h[:], ACT.Copy).then_inc(self.hi_done, 1)

    def tensor(self, pe, bank):
        for c in range(CHUNKS):
            pe.wait_ge(self.sq_done, c + 1)
            if c:
                pe.wait_ge(self.var_done, c)
            for k in range(KT):
                mm = pe.matmul(bank[:, 0:CH], self.K["ones"][:], self.sq[:, k, :],
                               start=(k == 0), stop=(k == KT - 1))
            mm.then_inc(self.sum_done, 1)

    def vector(self, dve, xT, bank, h_hi, h_lo, K):
        step = Order(self.dve_step)
        dve.wait_ge(self.gain_in, 16)
        for c in range(CHUNKS):
            dve.wait_ge(self.sum_done, c + 1)
            dve.tensor_scalar(self.var[:], bank[:, 0:CH], 1.0 / D_MODEL, EPS, ALU.mult,
                              ALU.add).then_inc(self.var_done, 1)
            dve.wait_ge(self.var_done, c + 1)
            dve.wait_ge(self.rms_done, c + 1)
            step.did(dve.reciprocal(self.inv[:], self.rms[:]))
            step.wait(dve)
            step.did(dve.tensor_tensor(self.tmp[:], self.inv[:], self.inv[:], ALU.mult))
            step.wait(dve)
            step.did(dve.tensor_tensor(self.tmp[:], self.tmp[:], self.var[:], ALU.mult))
            step.wait(dve)
            step.did(dve.tensor_scalar(self.tmp[:], self.tmp[:], -0.5, 1.5, ALU.mult, ALU.add))
            step.wait(dve)
            step.did(dve.tensor_tensor(self.inv[:], self.inv[:], self.tmp[:], ALU.mult))
            step.wait(dve)
            for k in range(KT):
                out = self.h[:, k, :] if self.split else h_hi[:, k, chunk(c)]
                last = dve.scalar_tensor_tensor(out, xT[:, k, chunk(c)], self.gain[:, k:k + 1],
                                                self.inv[:], ALU.mult, ALU.mult)
            if not self.split:
                last.then_inc(self.ready, 1)
                continue
            last.then_inc(self.h_done, 1)
            dve.wait_ge(self.hi_done, c + 1)
            dve.tensor_tensor(h_lo[:, :, chunk(c)], self.h[:], h_hi[:, :, chunk(c)].bitcast(F32),
                              ALU.subtract).then_inc(self.ready, 1)


def stage_load_x(nc, mem, K, xT, x_prompt, x_sample, copies, copied):
    with ExitStack() as scope:
        x_in = mem.sb(scope, "x_in", [P, TT, D_MODEL])
        banks = [mem.ps(scope, f"xbank{i}") for i in range(4)]
        landed = [mem.sem(f"x_landed{t}") for t in range(TT)]
        turned, taken = mem.sem("x_turned"), mem.sem("x_taken")

        with nc.Block() as block:
            @block.gpsimd
            def _(pool):
                for target, source in copies:
                    pool.dma_start(target, source).then_inc(copied, 16)

            @block.sync
            def _(sp):
                for t in range(TT):
                    if t < TT - 1:
                        sp.dma_start(x_in[:, t, :], x_prompt[t * P:(t + 1) * P, :]).then_inc(landed[t], 16)
                    else:
                        sp.dma_start(x_in[0:N_SAMPLE, t, :], x_sample).then_inc(landed[t], 16)

            @block.tensor
            def _(pe):
                for t in range(TT):
                    n = P if t < TT - 1 else N_SAMPLE
                    pe.wait_ge(landed[t], 16)
                    for half in range(2):
                        u = 2 * t + half
                        if u >= 4:
                            pe.wait_ge(taken, u - 3)
                        for k in range(4):
                            tr = pe.transpose(banks[u % 4][:, k * P:k * P + n],
                                              x_in[0:n, t, (4 * half + k) * P:(4 * half + k + 1) * P],
                                              K["ident"][0:n, 0:n])
                        tr.then_inc(turned, 1)

            @block.vector
            def _(dve):
                for t in range(TT):
                    n = P if t < TT - 1 else N_SAMPLE
                    for half in range(2):
                        u = 2 * t + half
                        dve.wait_ge(turned, u + 1)
                        dve.tensor_copy(
                            xT[:, 4 * half:4 * half + 4, t * P:t * P + n],
                            banks[u % 4][:, :].rearrange("p (k n) -> p k n", k=4)[:, :, 0:n],
                        ).then_inc(taken, 1)


def stage_ffn(nc, mem, K, xT, gain, w_gate, w_up, w_down, name):
    PAIRS = FT // 2
    wg_v = w_gate.rearrange("(k p) (f n) -> p k f n", p=P, n=P)
    wu_v = w_up.rearrange("(k p) (f n) -> p k f n", p=P, n=P)
    wd_v = w_down.rearrange("(f p) n -> p f n", p=P)
    with ExitStack() as scope:
        h_hi = mem.sb(scope, name + "_h_hi", [P, KT, T], F32R)
        h_lo = mem.sb(scope, name + "_h_lo", [P, KT, T], F32R)
        with ExitStack() as norm_scope:
            norm = Norm(mem, norm_scope, K, name)
        wd_hi = mem.sb(scope, name + "_wd_hi", [P, 2, D_MODEL], F32R)
        wd_lo = mem.sb(scope, name + "_wd_lo", [P, 2, D_MODEL], F32R)
        act_up = mem.sb(scope, name + "_act_up", [P, CH])
        gu_raw = [mem.sb(scope, f"{name}_gu_raw{s}", [P, 2, KT, P]) for s in range(2)]
        gu_hi = [mem.sb(scope, f"{name}_gu_hi{s}", [P, 2, KT, P], F32R) for s in range(2)]
        gu_lo = [mem.sb(scope, f"{name}_gu_lo{s}", [P, 2, KT, P], F32R) for s in range(2)]
        wd_raw = mem.sb(scope, name + "_wd_raw", [P, 2, D_MODEL])
        a_hi = mem.sb(scope, name + "_a_hi", [P, 2, T], F32R)
        a_lo = mem.sb(scope, name + "_a_lo", [P, 2, T], F32R)
        act_gate = mem.sb(scope, name + "_act_gate", [P, 2, CH])
        gate_bank = [mem.ps(scope, f"{name}_gate{i}") for i in range(2)]
        up_bank = [mem.ps(scope, f"{name}_up{i}") for i in range(2)]
        down_bank = [mem.ps(scope, f"{name}_down{i}") for i in range(4)]
        sum_bank = down_bank[0]

        gu_landed = [mem.sem(f"{name}_gu_landed{s}") for s in range(2)]
        gu_hi_done = [mem.sem(f"{name}_gu_hi_done{s}") for s in range(2)]
        gu_split = [mem.sem(f"{name}_gu_split{s}") for s in range(2)]
        wd_landed, wd_hi_done = mem.sem(name + "_wd_landed"), mem.sem(name + "_wd_hi_done")
        wd_split = mem.sem(name + "_wd_split")
        gate_done, up_done = mem.sem(name + "_gate_done"), mem.sem(name + "_up_done")
        silu_done, pair_free = mem.sem(name + "_silu_done"), mem.sem(name + "_pair_free")
        a_ready, dve_step = mem.sem(name + "_a_ready"), mem.sem(name + "_dve_step2")
        down_done, down_free = mem.sem(name + "_down_done"), mem.sem(name + "_down_free")
        UNITS = 2 * CHUNKS
        DOWNS = KT * CHUNKS

        with nc.Block() as block:
            @block.sync
            def _(sp):
                norm.load(sp, gain)

                def load_gu(s, i, tile):
                    sp.wait_ge(gu_split[s], i)
                    sp.dma_start(gu_raw[s][:, 0], wg_v[:, :, tile, :]).then_inc(gu_landed[s], 16)
                    sp.dma_start(gu_raw[s][:, 1], wu_v[:, :, tile, :]).then_inc(gu_landed[s], 16)

                def pair(i, last):
                    load_gu(1, i, 2 * i + 1)
                    sp.wait_ge(wd_split, i)
                    sp.dma_start(wd_raw[:], wd_v[:, bass.ds(2 * i, 2), :]).then_inc(wd_landed, 16)
                    if not last:
                        load_gu(0, i + 1, 2 * i + 2)

                load_gu(0, 0, 0)
                with sp.Fori(0, PAIRS - 1) as i:
                    pair(i, False)
                pair(PAIRS - 1, True)

            @block.scalar
            def _(act):
                def high_gu(s, i, first=False):
                    act.wait_ge(gu_landed[s], 32 * i + 32)
                    if not first:
                        act.wait_ge(up_done, UNITS * i if s else UNITS * i - CHUNKS)
                    act.activation(gu_hi[s][:], gu_raw[s][:], ACT.Copy).then_inc(gu_hi_done[s], 1)

                def silu(i, s, c):
                    u = UNITS * i + CHUNKS * s + c
                    b = (CHUNKS * s + c) % 2
                    act.wait_ge(gate_done, u + 1)
                    act.wait_ge(pair_free, u + 1)
                    act.activation(act_gate[:, b, :], gate_bank[b][:, 0:CH], ACT.Silu).then_inc(silu_done, 1)

                def pair(i, last):
                    high_gu(1, i)
                    for c in range(CHUNKS):
                        silu(i, 0, c)
                    act.wait_ge(wd_landed, 16 * i + 16)
                    act.wait_ge(down_done, DOWNS * i)
                    act.activation(wd_hi[:], wd_raw[:], ACT.Copy).then_inc(wd_hi_done, 1)
                    if not last:
                        high_gu(0, i + 1)
                    for c in range(CHUNKS):
                        silu(i, 1, c)

                high_gu(0, 0, True)
                norm.scalar(act, xT, h_hi)
                with act.Fori(0, PAIRS - 1) as i:
                    pair(i, False)
                pair(PAIRS - 1, True)

            @block.vector
            def _(dve):
                dve.sem_inc(pair_free, 2)
                dve.sem_inc(down_free, 4)

                def low_gu(s, i):
                    dve.wait_ge(gu_hi_done[s], i + 1)
                    dve.tensor_tensor(gu_lo[s][:], gu_raw[s][:], gu_hi[s][:].bitcast(F32),
                                      ALU.subtract).then_inc(gu_split[s], 1)

                low_gu(0, 0)
                norm.vector(dve, xT, sum_bank, h_hi, h_lo, K)

                def multiply(i, s, c):
                    u = UNITS * i + CHUNKS * s + c
                    b = (CHUNKS * s + c) % 2
                    dve.wait_ge(silu_done, u + 1)
                    dve.wait_ge(up_done, u + 1)
                    dve.wait_ge(a_ready, u)
                    dve.tensor_tensor(act_up[:], act_gate[:, b, :], up_bank[b][:, 0:CH],
                                      ALU.mult).then_inc(pair_free, 1)
                    dve.wait_ge(pair_free, u + 3)
                    dve.tensor_copy(a_hi[:, s, chunk(c)], act_up[:]).then_inc(dve_step, 1)
                    dve.wait_ge(dve_step, u + 1)
                    dve.tensor_tensor(a_lo[:, s, chunk(c)], act_up[:], a_hi[:, s, chunk(c)].bitcast(F32),
                                      ALU.subtract).then_inc(a_ready, 1)

                def pair(i, last):
                    low_gu(1, i)
                    for c in range(CHUNKS):
                        multiply(i, 0, c)
                    dve.wait_ge(wd_hi_done, i + 1)
                    dve.tensor_tensor(wd_lo[:], wd_raw[:], wd_hi[:].bitcast(F32),
                                      ALU.subtract).then_inc(wd_split, 1)
                    if not last:
                        low_gu(0, i + 1)
                    for c in range(CHUNKS):
                        multiply(i, 1, c)
                    dve.wait_ge(down_free, DOWNS * i + 4)
                    for c in range(CHUNKS):
                        for m in range(KT):
                            n = KT * c + m
                            dve.wait_ge(down_done, DOWNS * i + n + 1)
                            dve.scalar_tensor_tensor(xT[:, m, chunk(c)], down_bank[n % 4][:, 0:CH], 0.5,
                                                     xT[:, m, chunk(c)], ALU.mult,
                                                     ALU.add).then_inc(down_free, 1)

                with dve.Fori(0, PAIRS - 1) as i:
                    pair(i, False)
                pair(PAIRS - 1, True)

            @block.tensor
            def _(pe):
                norm.tensor(pe, sum_bank)

                def gate_up(i, s, c):
                    u = UNITS * i + CHUNKS * s + c
                    b = (CHUNKS * s + c) % 2
                    pe.wait_ge(pair_free, u + 1)
                    for j, (bank, done) in enumerate(((gate_bank[b], gate_done), (up_bank[b], up_done))):
                        for k in range(KT):
                            mm = product3(pe, bank[:, 0:CH], gu_hi[s][:, j, k, :], gu_lo[s][:, j, k, :],
                                          h_hi[:, k, chunk(c)], h_lo[:, k, chunk(c)], k == 0, k == KT - 1)
                        mm.then_inc(done, 1)

                def pair(i, first):
                    for s in range(2):
                        pe.wait_ge(gu_split[s], i + 1)
                        for c in range(CHUNKS):
                            if first and s == 0:
                                pe.wait_ge(norm.ready, c + 1)
                            gate_up(i, s, c)
                    pe.wait_ge(wd_split, i + 1)
                    for c in range(CHUNKS):
                        pe.wait_ge(a_ready, UNITS * i + CHUNKS + c + 1)
                        for m in range(KT):
                            n = KT * c + m
                            pe.wait_ge(down_free, DOWNS * i + n + 1)
                            for s in range(2):
                                mm = product3(pe, down_bank[n % 4][:, 0:CH],
                                              wd_hi[:, s, m * P:(m + 1) * P], wd_lo[:, s, m * P:(m + 1) * P],
                                              a_hi[:, s, chunk(c)], a_lo[:, s, chunk(c)], s == 0, s == 1)
                            mm.then_inc(down_done, 1)

                pair(0, True)
                with pe.Fori(1, PAIRS) as i:
                    pair(i, False)


def stage_compress(nc, mem, K, pages, source, n_pages_seq, n_seq, chunks, w1, w2, pe_cols,
                   kc_out, vc_out, name, spare=None):
    HALVES = max(1, chunks // P)
    R = min(chunks, P)
    W = chunks + 2
    SLOTS = CMP_BLOCK // CMP_STRIDE
    NF = CMP_HIDDEN // P
    UNITS = HALVES * KT // 2
    ALL = n_seq * 2
    VT = max(1, chunks // P)
    with ExitStack() as scope:
        raw = [mem.sb(scope, f"{name}_raw{h}", [P, CMP_STRIDE * KV_WIDTH]) if h == 0 or spare is None else spare
               for h in range(2)]
        w1_hi = [mem.sb(scope, f"{name}_w1_hi{j}", [P, SLOTS * KT, CMP_HIDDEN], F32R) for j in range(2)]
        w1_lo = [mem.sb(scope, f"{name}_w1_lo{j}", [P, SLOTS * KT, CMP_HIDDEN], F32R) for j in range(2)]
        w2_sb = mem.sb(scope, name + "_w2", [P, 2, NF, HD])
        pe_sb = mem.sb(scope, name + "_pe", [P, 2, SLOTS * KT])
        bias = mem.sb(scope, name + "_bias", [P, 2 * NF])
        x_hi = [mem.sb(scope, f"{name}_x_hi{j}", [P, KT, N_KV, W], F32R) for j in range(2)]
        x_lo = [mem.sb(scope, f"{name}_x_lo{j}", [P, KT, N_KV, W], F32R) for j in range(2)]
        packed = [mem.sb(scope, f"{name}_packed{i}", [P, N_KV, CMP_STRIDE, HD]) for i in range(2)]
        hidden = [mem.sb(scope, f"{name}_hidden{j}", [P, NF, N_KV, chunks]) for j in range(2)]
        turn_bank = [mem.ps(scope, f"{name}_turn{i}") for i in range(2)]
        hid_bank = [mem.ps(scope, f"{name}_hid{i}") for i in range(NF)]
        out_bank = [mem.ps(scope, f"{name}_out{i}") for i in range(2)]

        w_landed, w_hi_done = mem.sem(name + "_w_landed"), mem.sem(name + "_w_hi_done")
        w_split, bias_sum = mem.sem(name + "_w_split"), mem.sem(name + "_bias_sum")
        bias_done, zeroed = mem.sem(name + "_bias_done"), mem.sem(name + "_zeroed")
        raw_landed = [mem.sem(f"{name}_raw_landed{h}") for h in range(HALVES)]
        packed_done = [mem.sem(f"{name}_packed_done{i}") for i in range(2)]
        turned = [mem.sem(f"{name}_turned{j}") for j in range(2)]
        x_hi_done = [mem.sem(f"{name}_x_hi_done{j}") for j in range(2)]
        x_ready = [mem.sem(f"{name}_x_ready{j}") for j in range(2)]
        hid_done, gelu_done = mem.sem(name + "_hid_done"), mem.sem(name + "_gelu_done")
        out_done, out_taken = mem.sem(name + "_out_done"), mem.sem(name + "_out_taken")
        LOADS = R // 8 if pages is not None else 1


        def pack_slot(j, h):
            return (j * HALVES + h) % 2

        def packs(b, j, h):
            return 2 * b + j + 1 if HALVES == 2 else b + 1

        with nc.Block() as block:
            @block.sync
            def _(sp):
                for j in range(2):
                    sp.dma_start(raw[j][:, :].rearrange("p (k f) -> p k f", f=CMP_HIDDEN),
                                 w1[j].rearrange("(k p) f -> p k f", p=P)).then_inc(w_landed, 16)
                    sp.dma_start(w2_sb[:, j], w2[j].rearrange("(k p) n -> p k n", p=P)).then_inc(w_landed, 16)
                    sp.dma_start(pe_sb[:, j], pe_cols[j]).then_inc(w_landed, 16)

                def load(b, again):
                    for h in range(HALVES):
                        if again:
                            sp.wait_ge(packed_done[pack_slot(1, h)], packs(b - 1, 1, h))
                        if pages is None:
                            sp.dma_start(raw[h][0:R, :], source).then_inc(raw_landed[h], 16)
                            continue
                        for q in range(LOADS):
                            page = sp.value_load(pages[0:1, bass.ds(b * n_pages_seq + LOADS * h + q, 1)],
                                                 min_val=0, max_val=source.shape[0] - 1)
                            sp.dma_start(raw[h][8 * q:8 * q + 8, :],
                                         source[bass.ds(page, 1)].rearrange("a c n -> (a c) n")
                                         ).then_inc(raw_landed[h], 16)

                sp.wait_ge(w_split, 2)
                sp.wait_ge(bias_sum, 1)
                load(0, False)
                if n_seq > 1:
                    with sp.Fori(1, n_seq) as b:
                        load(b, True)

            @block.scalar
            def _(act):
                act.wait_ge(w_landed, 96)
                for j in range(2):
                    act.activation(w1_hi[j][:], raw[j][:, :].rearrange("p (k f) -> p k f", f=CMP_HIDDEN),
                                   ACT.Copy).then_inc(w_hi_done, 1)

                def pack(b, j, h, first=False):
                    act.wait_ge(raw_landed[h], 16 * LOADS * (b + 1))
                    if j == 1 and HALVES == 2:
                        act.wait_ge(turned[0], UNITS * b + 4 * (h + 1))
                    elif not first:
                        act.wait_ge(turned[1], UNITS * (b - 1) + 4 * (h + 1))
                    i = pack_slot(j, h)
                    rows = raw[h][0:R, :].rearrange("p (s j g d) -> p j g s d", s=CMP_STRIDE, j=2, g=N_KV)
                    act.activation(packed[i][0:R], rows[:, j], ACT.Copy).then_inc(packed_done[i], 1)

                def high_x(b, j, t):
                    h, q = divmod(t, KT // 2)
                    act.wait_ge(turned[j], UNITS * b + t + 1)
                    bank = turn_bank[(UNITS * j + t) % 2]
                    act.activation(x_hi[j][:, 2 * q:2 * q + 2, :, h * R:h * R + R],
                                   bank[:, 0:4 * R].rearrange("p (k g n) -> p k g n", k=2, g=2),
                                   ACT.Copy).then_inc(x_hi_done[j], 1)

                def gelu(b, j, f):
                    u = 2 * NF * b + NF * j + f
                    act.wait_ge(hid_done, u + 1)
                    act.activation(hidden[j][:, f], hid_bank[f][:, 0:2 * chunks].rearrange("p (g n) -> p g n", g=2),
                                   ACT.Gelu_apprx_tanh,
                                   bias=bias[:, NF * j + f:NF * j + f + 1]).then_inc(gelu_done, 1)

                def slot(highs, pack_next, gelu_now):
                    for u in highs[:len(highs) // 2]:
                        high_x(*u)
                    if pack_next is not None:
                        pack(*pack_next)
                    for u in highs[len(highs) // 2:]:
                        high_x(*u)
                    gelu(*gelu_now)

                def sequence(b, last):
                    span = [range(f * UNITS // 2, (f + 1) * UNITS // 2) for f in range(NF)]
                    slot([(b, 1, t) for t in span[0]], (b, 1, 1) if HALVES == 2 else None, (b, 0, 0))
                    slot([(b, 1, t) for t in span[1]], None if last else (b + 1, 0, 0), (b, 0, 1))
                    slot([] if last else [(b + 1, 0, t) for t in span[0]],
                         None if last else (b + 1, 0, 1), (b, 1, 0))
                    slot([] if last else [(b + 1, 0, t) for t in span[1]],
                         None if last else (b + 1, 1, 0), (b, 1, 1))

                for h in range(HALVES):
                    pack(0, 0, h, True)
                for t in range(UNITS):
                    high_x(0, 0, t)
                pack(0, 1, 0, HALVES == 1)
                act.wait_ge(bias_done, 1)
                if n_seq > 1:
                    with act.Fori(0, n_seq - 1) as b:
                        sequence(b, False)
                sequence(n_seq - 1, True)

            @block.vector
            def _(dve):
                for j in range(2):
                    for x in (x_hi[j], x_lo[j]):
                        z = dve.memset(x[:, :, :, chunks:W].bitcast(F32), 0.0)
                z.then_inc(zeroed, 1)
                for j in range(2):
                    dve.wait_ge(w_hi_done, j + 1)
                    dve.tensor_tensor(w1_lo[j][:], raw[j][:, :].rearrange("p (k f) -> p k f", f=CMP_HIDDEN),
                                      w1_hi[j][:].bitcast(F32), ALU.subtract).then_inc(w_split, 1)
                dve.wait_ge(bias_sum, 1)
                dve.tensor_copy(bias[:], out_bank[0][:, 0:2 * NF]).then_inc(bias_done, 1)

                def low_x(b, j, t):
                    h, q = divmod(t, KT // 2)
                    dve.wait_ge(x_hi_done[j], UNITS * b + t + 1)
                    bank = turn_bank[(UNITS * j + t) % 2]
                    out = x_lo[j][:, 2 * q:2 * q + 2, :, h * R:h * R + R]
                    dve.tensor_tensor(out, bank[:, 0:4 * R].rearrange("p (k g n) -> p k g n", k=2, g=2),
                                      x_hi[j][:, 2 * q:2 * q + 2, :, h * R:h * R + R].bitcast(F32),
                                      ALU.subtract).then_inc(x_ready[j], 1)

                def take(b, j):
                    dve.wait_ge(out_done, 2 * b + j + 1)
                    if j == 0:
                        dve.tensor_copy(kc_out[:, bass.ds(b, 1), :].rearrange("p a n -> p (a n)"),
                                        out_bank[0][:, 0:chunks]).then_inc(out_taken, 1)
                    else:
                        dve.tensor_copy(vc_out[0:R, bass.ds(b, 1), :, :].rearrange("p a t n -> p (a t n)"),
                                        out_bank[1][0:R, 0:VT * P]).then_inc(out_taken, 1)

                def sequence(b, last):
                    for t in range(UNITS):
                        low_x(b, 1, t)
                    take(b, 0)
                    if not last:
                        for t in range(UNITS):
                            low_x(b + 1, 0, t)
                    take(b, 1)

                for t in range(UNITS):
                    low_x(0, 0, t)
                if n_seq > 1:
                    with dve.Fori(0, n_seq - 1) as b:
                        sequence(b, False)
                sequence(n_seq - 1, True)

            @block.tensor
            def _(pe):
                pe.wait_ge(w_landed, 96)
                for j in range(2):
                    for f in range(NF):
                        for k in range(SLOTS * KT):
                            mm = pe.matmul(out_bank[0][:, NF * j + f:NF * j + f + 1],
                                           raw[j][:, k * CMP_HIDDEN + f * P:k * CMP_HIDDEN + (f + 1) * P],
                                           pe_sb[:, j, k:k + 1], start=(k == 0), stop=(k == SLOTS * KT - 1))
                mm.then_inc(bias_sum, 1)
                pe.wait_ge(zeroed, 1)

                def turn(b, j, t):
                    h, q = divmod(t, KT // 2)
                    if q == 0:
                        pe.wait_ge(packed_done[pack_slot(j, h)], packs(b, j, h))
                    if t >= 2:
                        pe.wait_ge(x_ready[j], UNITS * b + t - 1)
                    elif j == 1:
                        pe.wait_ge(x_ready[0], UNITS * (b + 1))
                    elif type(b) is not int or b:
                        pe.wait_ge(x_ready[1], UNITS * b)
                    rows = packed[pack_slot(j, h)][0:R].rearrange("p g (k s) d -> p g k (s d)", s=2)
                    bank = turn_bank[(UNITS * j + t) % 2]
                    for k in range(2):
                        for g in range(N_KV):
                            tr = pe.transpose(bank[:, (2 * k + g) * R:(2 * k + g + 1) * R],
                                              rows[:, g, 2 * q + k, :], K["ident"][0:R, 0:R])
                    tr.then_inc(turned[j], 1)

                def hidden_of(b, j, f, turns):
                    pe.wait_ge(x_ready[j], UNITS * (b + 1))
                    if j == 1:
                        pe.wait_ge(gelu_done, 2 * NF * b + f + 1)
                    elif type(b) is not int or b:
                        pe.wait_ge(gelu_done, 2 * NF * b - NF + f + 1)
                    n = 0
                    for slot in range(SLOTS):
                        for k in range(KT):
                            w = slot * KT + k
                            mm = product3(pe, hid_bank[f][:, 0:2 * chunks],
                                          w1_hi[j][:, w, f * P:(f + 1) * P], w1_lo[j][:, w, f * P:(f + 1) * P],
                                          x_hi[j][:, k, :, slot:slot + chunks],
                                          x_lo[j][:, k, :, slot:slot + chunks],
                                          w == 0, w == SLOTS * KT - 1)
                            if w % (SLOTS * KT // max(1, UNITS // 2)) == 0 and n < len(turns):
                                turn(*turns[n])
                                n += 1
                    mm.then_inc(hid_done, 1)

                def second(b, j):
                    pe.wait_ge(gelu_done, 2 * NF * b + NF * (j + 1))
                    bank = out_bank[j]
                    if type(b) is int and b == 0:
                        if j == 0:
                            pe.wait_ge(bias_done, 1)
                    else:
                        pe.wait_ge(out_taken, 2 * b - 1 + j)
                    for g in range(N_KV):
                        if j == 0:
                            for f in range(NF):
                                mm = pe.matmul(bank[g * HD:(g + 1) * HD, 0:chunks], w2_sb[:, 0, f, :],
                                               hidden[0][:, f, g, :], start=(f == 0), stop=(f == NF - 1))
                        else:
                            for v in range(VT):
                                for f in range(NF):
                                    mm = pe.matmul(bank[0:R, v * P + g * HD:v * P + (g + 1) * HD],
                                                   hidden[1][:, f, g, v * R:(v + 1) * R], w2_sb[:, 1, f, :],
                                                   start=(f == 0), stop=(f == NF - 1))
                    mm.then_inc(out_done, 1)

                def sequence(b, last):
                    for j in range(2):
                        for f in range(NF):
                            span = range(f * UNITS // 2, (f + 1) * UNITS // 2)
                            turns = [(b, 1, t) for t in span] if j == 0 else \
                                [] if last else [(b + 1, 0, t) for t in span]
                            hidden_of(b, j, f, turns)
                        second(b, j)

                for t in range(UNITS):
                    turn(0, 0, t)
                if n_seq > 1:
                    sequence(0, False)
                    if n_seq > 2:
                        with pe.Fori(1, n_seq - 1) as b:
                            sequence(b, False)
                sequence(n_seq - 1, True)


def stage_in_project(nc, mem, K, xT, gain, w_in, z, z_sample, uT, outs):
    ZG = 4
    ZN = OFF_POOL // ZG
    UG, UN = 2, POOL_WIDTH // 2
    with ExitStack() as scope:
        h_hi = mem.sb(scope, "in_h_hi", [P, KT, T], F32R)
        h_lo = mem.sb(scope, "in_h_lo", [P, KT, T], F32R)
        with ExitStack() as norm_scope:
            norm = Norm(mem, norm_scope, K, "in")
        w_hi = mem.sb(scope, "in_w_hi", [P, KT, ZN], F32R)
        w_lo = mem.sb(scope, "in_w_lo", [P, KT, ZN], F32R)
        w_raw = mem.sb(scope, "in_w_raw", [P, KT, ZN])
        rot = [mem.sb(scope, f"in_rot{i}", [P, TT, 4, 8]) for i in range(4)]
        banks = [mem.ps(scope, f"in_bank{i}") for i in range(4)]
        w_landed, w_hi_done, w_split = mem.sem("in_w_landed"), mem.sem("in_w_hi_done"), mem.sem("in_w_split")
        z_done, z_taken, u_done, u_taken = (mem.sem("in_z_done"), mem.sem("in_z_taken"),
                                            mem.sem("in_u_done"), mem.sem("in_u_taken"))
        padded, rotated, gated, out_sem = (mem.sem("in_padded"), mem.sem("in_rotated"),
                                           mem.sem("in_gated"), mem.sem("in_out"))
        rope_step = mem.sem("in_rope_step")
        w_view = w_in.rearrange("(k p) n -> p k n", p=P)

        with nc.Block() as block:
            @block.sync
            def _(sp):
                norm.load(sp, gain)
                sp.dma_start(outs["x"], xT[:]).then_inc(out_sem, 16)

                def load(i, start, n):
                    sp.wait_ge(w_split, i)
                    sp.dma_start(w_raw[:, :, 0:n], w_view[:, :, bass.ds(start, n)]).then_inc(w_landed, 16)

                with sp.Fori(0, ZG) as i:
                    load(i, ZN * i, ZN)
                for i in range(UG):
                    load(ZG + i, OFF_POOL + UN * i, UN)
                sp.wait_ge(rotated, 1)
                sp.wait_ge(z_taken, ZG * TT)
                for key, off in (("cmp", OFF_CMP), ("slc", OFF_SLC), ("win", OFF_WIN)):
                    first = 0 if key != "win" else (SEQ - WINDOW) // P
                    sp.dma_start(outs[key + "_prompt"].rearrange("(t p) n -> p t n", p=P),
                                 z[:, first:TT - 1, off:off + KV_WIDTH]).then_inc(out_sem, 16)
                    if key != "win":
                        sp.dma_start(outs[key + "_sample"], z[0:N_SAMPLE, TT - 1, off:off + KV_WIDTH]
                                     ).then_inc(out_sem, 16)
                sp.dma_start(z_sample[:], z[0:N_SAMPLE, TT - 1, :]).then_inc(out_sem, 16)
                sp.wait_ge(out_sem, 16 * 7)

            @block.scalar
            def _(act):
                norm.scalar(act, xT, h_hi)

                def high(i, n, used):
                    act.wait_ge(w_landed, 16 * i + 16)
                    used()
                    act.activation(w_hi[:, :, 0:n], w_raw[:, :, 0:n], ACT.Copy).then_inc(w_hi_done, 1)

                act.wait_ge(padded, 1)

                def z_group(i):
                    high(i, ZN, lambda: act.wait_ge(z_done, TT * i))
                    for t in range(TT):
                        act.wait_ge(z_done, TT * i + t + 1)
                        rows = slice(0, P) if t < TT - 1 else slice(P - N_SAMPLE, P)
                        n = P if t < TT - 1 else N_SAMPLE
                        act.activation(z[0:n, t, bass.ds(ZN * i, ZN)], banks[t % 4][rows, 0:ZN],
                                       ACT.Copy).then_inc(z_taken, 1)

                with act.Fori(0, ZG) as i:
                    z_group(i)
                high(ZG, UN, lambda: act.wait_ge(z_done, TT * ZG))
                act.wait_ge(z_taken, ZG * TT)
                act.activation(z[:, :, OFF_GATE:OFF_POOL], z[:, :, OFF_GATE:OFF_POOL],
                               ACT.Sigmoid).then_inc(gated, 1)
                for m in range(2 * UG):
                    if m == 2:
                        high(ZG + 1, UN, lambda: act.wait_ge(u_done, 2 * CHUNKS))
                    for c in range(CHUNKS):
                        n = CHUNKS * m + c
                        act.wait_ge(u_done, n + 1)
                        act.activation(uT[:, m, chunk(c)], banks[n % 4][:, 0:CH], ACT.Copy).then_inc(u_taken, 1)

            @block.vector
            def _(dve):
                norm.vector(dve, xT, banks[0], h_hi, h_lo, K)
                dve.memset(z[:, TT - 1, :], 0.0).then_inc(padded, 1)

                def low(i, n):
                    dve.wait_ge(w_hi_done, i + 1)
                    dve.tensor_tensor(w_lo[:, :, 0:n], w_raw[:, :, 0:n], w_hi[:, :, 0:n].bitcast(F32),
                                      ALU.subtract).then_inc(w_split, 1)

                with dve.Fori(0, ZG) as i:
                    low(i, ZN)
                low(ZG, UN)
                dve.wait_ge(z_taken, ZG * TT)
                step = Order(rope_step)
                for n, (off, heads) in enumerate(((0, 4), (4 * HD, 4), (OFF_CMP, 2), (OFF_SLC, 2), (OFF_WIN, 2))):
                    if n == 2:
                        low(ZG + 1, UN)
                    view = z[:, :, off:off + heads * HD].rearrange("p t (h d) -> p t h d", d=HD)
                    x1, x2 = view[:, :, :, 0:8], view[:, :, :, 8:16]
                    cos = K["cos"][:].unsqueeze(2).to_broadcast([P, TT, heads, 8])
                    sin = K["sin"][:].unsqueeze(2).to_broadcast([P, TT, heads, 8])
                    r = [x[:, :, 0:heads, :] for x in rot]
                    step.wait(dve)
                    for out, a, b in ((r[0], x1, cos), (r[1], x2, sin), (r[2], x1, sin), (r[3], x2, cos)):
                        step.did(dve.tensor_tensor(out, a, b, ALU.mult))
                    step.wait(dve)
                    step.did(dve.tensor_tensor(x1, r[0], r[1], ALU.subtract))
                    step.did(dve.tensor_tensor(x2, r[2], r[3], ALU.add))
                step.wait(dve)
                dve.engine_nop().then_inc(rotated, 1)

            @block.tensor
            def _(pe):
                norm.tensor(pe, banks[0])

                with pe.Fori(0, ZG) as i:
                    pe.wait_ge(w_split, i + 1)
                    pe.wait_ge(norm.ready, CHUNKS)
                    for t in range(TT):
                        pe.wait_ge(z_taken, TT * i + t - 3 if t > 3 else TT * i)
                        last = t == TT - 1
                        tokens = slice(T - P, T) if last else slice(t * P, (t + 1) * P)
                        for k in range(KT):
                            mm = product3(pe, banks[t % 4][:, 0:ZN], h_hi[:, k, tokens], h_lo[:, k, tokens],
                                          w_hi[:, k, :], w_lo[:, k, :], k == 0, k == KT - 1)
                        mm.then_inc(z_done, 1)
                for m in range(2 * UG):
                    if m % 2 == 0:
                        pe.wait_ge(w_split, ZG + m // 2 + 1)
                    w = slice((m % 2) * P, (m % 2) * P + P)
                    for c in range(CHUNKS):
                        n = CHUNKS * m + c
                        if n < 4:
                            pe.wait_ge(z_taken, ZG * TT)
                        else:
                            pe.wait_ge(u_taken, n - 3)
                        for k in range(KT):
                            mm = product3(pe, banks[n % 4][:, 0:CH], w_hi[:, k, w], w_lo[:, k, w],
                                          h_hi[:, k, chunk(c)], h_lo[:, k, chunk(c)], k == 0, k == KT - 1)
                        mm.then_inc(u_done, 1)


def stage_pool(nc, mem, K, uT, mix, state_pool, w_pool, pool_scale, out_prompt, out_sample):
    ROWS = POOL_STATE + N_SAMPLE
    EXT = POOL_STATE + DEC_SEQ
    with ExitStack() as scope:
        state = mem.sb(scope, "pl_state", [P, POOL_WIDTH])
        w_sb = mem.sb(scope, "pl_w", [P, 4, P])
        scale = mem.sb(scope, "pl_scale", [P, 4])
        rows = mem.sb(scope, "pl_rows", [P, POOL_WIDTH])
        prompt = [mem.sb(scope, f"pl_prompt{i}", [P, POOL_STATE + SEQ]) for i in range(3)]
        sample = [mem.sb(scope, f"pl_sample{i}", [P, DEC_BATCH, EXT]) for i in range(3)]
        diff = mem.sb(scope, "pl_diff", [P, T])
        state_bank, row_bank = mem.ps(scope, "pl_state_bank"), mem.ps(scope, "pl_row_bank")
        banks = [mem.ps(scope, f"pl_bank{i}") for i in range(CHUNKS)]
        landed, turned, rows_taken, out_sem = (mem.sem("pl_landed"), mem.sem("pl_turned"),
                                               mem.sem("pl_rows_taken"), mem.sem("pl_out"))
        dve_step, diff_ready, map_done, map_taken = (mem.sem("pl_dve_step"), mem.sem("pl_diff_ready"),
                                                     mem.sem("pl_map_done"), mem.sem("pl_map_taken"))

        with nc.Block() as block:
            @block.sync
            def _(sp):
                sp.dma_start(state[0:DEC_BATCH * POOL_STATE, :],
                             state_pool.rearrange("b s n -> (b s) n")).then_inc(landed, 16)
                sp.dma_start(w_sb[:], w_pool.rearrange("g p n -> p g n")).then_inc(landed, 16)
                sp.dma_start(scale[:], pool_scale).then_inc(landed, 16)
                sp.wait_ge(rows_taken, 1)
                sp.dma_start(out_prompt, rows[0:POOL_STATE, :]).then_inc(out_sem, 16)
                for b in range(DEC_BATCH):
                    r = POOL_STATE + b * DEC_SEQ
                    sp.dma_start(out_sample[b, POOL_STATE - DEC_SEQ:POOL_STATE, :],
                                 rows[r:r + DEC_SEQ, :]).then_inc(out_sem, 16)
                sp.wait_ge(out_sem, 16 * (1 + DEC_BATCH))

            @block.tensor
            def _(pe):
                pe.wait_ge(landed, 48)
                n = DEC_BATCH * POOL_STATE
                for g in range(4):
                    pe.transpose(state_bank[:, g * P:g * P + n], state[0:n, g * P:(g + 1) * P], K["ident"][0:n, 0:n])
                    tr = pe.transpose(row_bank[0:ROWS, g * P:(g + 1) * P], uT[:, g, T - ROWS:T], K["ident"][:])
                tr.then_inc(turned, 1)
                for g in range(4):
                    pe.wait_ge(diff_ready, g + 1)
                    if g:
                        pe.wait_ge(map_taken, CHUNKS * g)
                    for c in range(CHUNKS):
                        pe.matmul(banks[c][:, 0:CH], w_sb[:, g, :], diff[:, chunk(c)], start=True,
                                  stop=True).then_inc(map_done, 1)

            @block.scalar
            def _(act):
                act.wait_ge(turned, 1)
                act.activation(rows[0:ROWS, :], row_bank[0:ROWS, :], ACT.Copy).then_inc(rows_taken, 1)
                act.wait_ge(landed, 48)
                for g in range(4):
                    for c in range(CHUNKS):
                        act.wait_ge(map_done, CHUNKS * g + c + 1)
                        act.activation(mix[:, KT // 2 + g, chunk(c)], banks[c][:, 0:CH], ACT.Copy,
                                       scale=scale[:, g:g + 1]).then_inc(map_taken, 1)

            @block.vector
            def _(dve):
                step = Order(dve_step)
                dve.wait_ge(turned, 1)
                for g, w in enumerate(POOL_WINDOWS):
                    step.wait(dve)
                    if g == 0:
                        step.did(dve.memset(prompt[0][:, 0:POOL_STATE], 0.0))
                    step.did(dve.tensor_copy(prompt[0][:, POOL_STATE:], uT[:, g, 0:SEQ]))
                    n = DEC_BATCH * POOL_STATE
                    step.did(dve.tensor_copy(sample[0][:, :, 0:POOL_STATE],
                                             state_bank[:, g * P:g * P + n].rearrange("p (b s) -> p b s", b=DEC_BATCH)))
                    step.did(dve.tensor_copy(sample[0][:, :, POOL_STATE:],
                                             uT[:, g, SEQ:T].rearrange("p (b s) -> p b s", b=DEC_BATCH)))
                    step.wait(dve)
                    reach, at = 1, 0
                    while reach < w:
                        to = 2 if at == 1 else 1
                        lo = 2 * reach - 1
                        step.did(dve.tensor_tensor(prompt[to][:, lo:], prompt[at][:, lo:],
                                                   prompt[at][:, lo - reach:POOL_STATE + SEQ - reach], ALU.add))
                        step.did(dve.tensor_tensor(sample[to][:, :, lo:], sample[at][:, :, lo:],
                                                   sample[at][:, :, lo - reach:EXT - reach], ALU.add))
                        step.wait(dve)
                        reach, at = 2 * reach, to
                    if g:
                        dve.wait_ge(map_done, CHUNKS * g)
                    step.did(dve.scalar_tensor_tensor(diff[:, 0:SEQ], prompt[at][:, POOL_STATE:], 1.0 / w,
                                                      prompt[0][:, POOL_STATE:], ALU.mult, ALU.subtract))
                    step.did(dve.scalar_tensor_tensor(
                        diff[:, SEQ:T].rearrange("p (b s) -> p b s", b=DEC_BATCH), sample[at][:, :, POOL_STATE:],
                        1.0 / w, sample[0][:, :, POOL_STATE:], ALU.mult, ALU.subtract))
                    step.wait(dve)
                    step.did(dve.tensor_tensor(prompt[at][:, POOL_STATE:POOL_STATE + 16],
                                               prompt[at][:, POOL_STATE:POOL_STATE + 16], K["inv_count"][:, g, :], ALU.mult))
                    step.wait(dve)
                    step.did(dve.tensor_tensor(diff[:, 0:16], prompt[at][:, POOL_STATE:POOL_STATE + 16],
                                               prompt[0][:, POOL_STATE:POOL_STATE + 16], ALU.subtract))
                    step.wait(dve)
                    dve.engine_nop().then_inc(diff_ready, 1)


def stage_attend_prompt(nc, mem, K, z, kcp, vcp, mixT):
    QT = SEQ // P
    WT = WINDOW // P
    NB = SEQ // CMP_STRIDE - 1
    WIN0, CMP0 = SEQ, SEQ + (WT + 1) * P
    PW = CMP0 + 64
    LEAD = 12

    def win_tiles(qt):
        return list(range(max(0, qt - WT + 1), qt + 1)) + ([qt - WT] if qt >= WT else [])

    def value_units(qt):
        return ([(t * P, P, (0, t)) for t in range(qt + 1)]
                + [(WIN0 + i * P, P, (1, t)) for i, t in enumerate(win_tiles(qt))]
                + [(CMP0, NB, None)])

    UNITS = [len(value_units(q)) for q in range(QT)]
    PER_GROUP = LEAD + sum(UNITS)
    assert PER_GROUP % 2 == 0

    with ExitStack() as scope:
        q_rows = mem.sb(scope, "at_q_rows", [P, QT, GROUP, HD])
        k_rows = mem.sb(scope, "at_k_rows", [P, 2, QT, HD])
        values = mem.sb(scope, "at_values", [P, 2, QT, HD])
        vc_rows = mem.sb(scope, "at_vc_rows", [P, HD])
        kc = mem.sb(scope, "at_kc", [HD, N_KV, SEQ // CMP_STRIDE])
        qT = mem.sb(scope, "at_qT", [HD, GROUP, SEQ])
        kT = mem.sb(scope, "at_kT", [HD, 2, SEQ])
        probs = [mem.sb(scope, f"at_probs{i}", [P, GROUP, PW]) for i in range(2)]
        neg_max = mem.sb(scope, "at_neg_max", [P, 2, GROUP, 3])
        sums = mem.sb(scope, "at_sums", [P, 2, GROUP, 3])
        factor = mem.sb(scope, "at_factor", [P, GROUP, 3])
        turned_sb = [mem.sb(scope, f"at_turned{i}", [P, BANK]) for i in range(2)]
        slc_bank = mem.ps(scope, "at_slc_bank", (P, 2 * BANK))
        win_bank = mem.ps(scope, "at_win_bank", (P, 2 * BANK))
        turn_bank = [mem.ps(scope, f"at_turn_bank{i}") for i in range(2)]
        out_bank = [mem.ps(scope, f"at_out_bank{i}") for i in range(2)]

        kc_ready, q_copied, kv_copied = mem.sem("at_kc_ready"), mem.sem("at_q_copied"), mem.sem("at_kv_copied")
        turned, taken, pv_done = mem.sem("at_turned"), mem.sem("at_taken"), mem.sem("at_pv_done")
        scored = [mem.sem(f"at_scored{i}") for i in range(2)]
        maxed = [mem.sem(f"at_maxed{i}") for i in range(2)]
        exped = [mem.sem(f"at_exped{i}") for i in range(2)]
        p_ready, out_done, out_taken = mem.sem("at_p_ready"), mem.sem("at_out_done"), mem.sem("at_out_taken")
        dve_step = mem.sem("at_dve_step")
        STEPS = QT * 3 + 1

        def unit_base(qt):
            return LEAD + sum(UNITS[:qt])

        def quarter(qt, r):
            n = UNITS[qt]
            return range(n * r // GROUP, n * (r + 1) // GROUP)

        with nc.Block() as block:
            @block.scalar
            def _(act):
                with act.Fori(0, N_KV) as g:
                    act.wait_ge(taken, PER_GROUP * g)
                    act.wait_ge(turned, PER_GROUP * g)
                    act.activation(q_rows[:], z[:, 0:QT, bass.ds(g * GROUP * HD, GROUP * HD)].rearrange(
                        "p t (r d) -> p t r d", r=GROUP), ACT.Copy, scale=SCALE).then_inc(q_copied, 1)
                    for n in range(QT):
                        act.wait_ge(turned, PER_GROUP * g + n + 1)
                        act.activation(qT[:, :, n * P:(n + 1) * P],
                                       turn_bank[n % 2][0:HD, :].rearrange("p (r n) -> p r n", r=GROUP),
                                       ACT.Copy).then_inc(taken, 1)
                    for n in range(QT, LEAD):
                        b, half = divmod(n - QT, 2)
                        act.wait_ge(turned, PER_GROUP * g + n + 1)
                        act.activation(kT[:, b, half * BANK:(half + 1) * BANK], turn_bank[n % 2][0:HD, :],
                                       ACT.Copy).then_inc(taken, 1)
                    for qt in range(QT + 1):
                        for r in range(GROUP):
                            if qt < QT:
                                n = GROUP * qt + r
                                nm, sm, p = neg_max[:, qt % 2, r], sums[:, qt % 2, r], probs[qt % 2][:, r]
                                act.wait_ge(maxed[0], GROUP * QT * g + n + 1)
                                act.activation(p[:, 0:(qt + 1) * P], slc_bank[:, 0:(qt + 1) * P], ACT.Exp,
                                               bias=nm[:, 1:2], accum_out=sm[:, 1:2]).then_inc(exped[0], 1)
                                act.wait_ge(maxed[1], GROUP * QT * g + n + 1)
                                w = len(win_tiles(qt)) * P
                                act.activation(p[:, WIN0:WIN0 + w], win_bank[:, 0:w], ACT.Exp,
                                               bias=nm[:, 2:3], accum_out=sm[:, 2:3])
                                act.activation(p[:, CMP0:CMP0 + NB], win_bank[:, (WT + 1) * P:(WT + 1) * P + NB],
                                               ACT.Exp, bias=nm[:, 0:1],
                                               accum_out=sm[:, 0:1]).then_inc(exped[1], 1)
                            if qt > 0:
                                for u in quarter(qt - 1, r):
                                    n = unit_base(qt - 1) + u
                                    rows = value_units(qt - 1)[u][1]
                                    act.wait_ge(turned, PER_GROUP * g + n + 1)
                                    if n - LEAD >= 2:
                                        act.wait_ge(pv_done, (PER_GROUP - LEAD) * g + n - LEAD - 1)
                                    act.activation(turned_sb[n % 2][0:rows, :], turn_bank[n % 2][0:rows, :],
                                                   ACT.Copy).then_inc(taken, 1)

            @block.vector
            def _(dve):
                for g in range(N_KV):
                    k = dve.tensor_copy(kc[:, g, :], kcp[g * HD:(g + 1) * HD, :])
                k.then_inc(kc_ready, 1)
                with dve.Fori(0, N_KV) as g:
                    dve.wait_ge(turned, PER_GROUP * g)
                    dve.wait_ge(pv_done, (PER_GROUP - LEAD) * g)
                    for b, off in enumerate((OFF_SLC, OFF_WIN)):
                        dve.tensor_copy(k_rows[:, b], z[:, 0:QT, bass.ds(off + g * HD, HD)])
                        dve.tensor_copy(values[:, b], z[:, 0:QT, bass.ds(off + N_KV * HD + g * HD, HD)])
                    dve.tensor_copy(vc_rows[0:NB], vcp[0:NB, bass.ds(g * HD, HD)]).then_inc(kv_copied, 1)
                    for qt in range(QT + 1):
                        if qt < QT:
                            for r in range(GROUP):
                                n = GROUP * qt + r
                                nm = neg_max[:, qt % 2, r]
                                dve.wait_ge(scored[0], GROUP * QT * g + n + 1)
                                dve.tensor_reduce(nm[:, 1:2], slc_bank[:, 0:(qt + 1) * P], AX.X, ALU.max,
                                                  negate=True).then_inc(maxed[0], 1)
                                dve.wait_ge(scored[1], GROUP * QT * g + n + 1)
                                dve.tensor_reduce(nm[:, 2:3], win_bank[:, 0:len(win_tiles(qt)) * P], AX.X,
                                                  ALU.max, negate=True)
                                dve.tensor_reduce(nm[:, 0:1], win_bank[:, (WT + 1) * P:(WT + 1) * P + NB], AX.X,
                                                  ALU.max, negate=True).then_inc(maxed[1], 1)
                            for i in range(2):
                                dve.wait_ge(exped[i], GROUP * QT * g + GROUP * (qt + 1))
                            dve.tensor_scalar(factor[:], sums[:, qt % 2], 1e-30, None, ALU.max).then_inc(dve_step, 1)
                            dve.wait_ge(dve_step, STEPS * g + 3 * qt + (1 if qt else 0) + 1)
                            dve.reciprocal(factor[:], factor[:]).then_inc(dve_step, 1)
                            dve.wait_ge(dve_step, STEPS * g + 3 * qt + (1 if qt else 0) + 2)
                            dve.tensor_tensor(factor[:], factor[:], z[:, qt, bass.ds(OFF_GATE + g * 3 * GROUP, 3 * GROUP)]
                                              .rearrange("p (r b) -> p r b", b=3), ALU.mult).then_inc(dve_step, 1)
                            dve.wait_ge(dve_step, STEPS * g + 3 * qt + (1 if qt else 0) + 3)
                            if qt == 0:
                                dve.tensor_scalar(factor[:, :, 0:1], factor[:, :, 0:1], K["has_block"][:], None,
                                                  ALU.mult).then_inc(dve_step, 1)
                                dve.wait_ge(dve_step, STEPS * g + 4)
                            for r in range(GROUP):
                                p = probs[qt % 2][:, r]
                                w = len(win_tiles(qt)) * P
                                for b, lo, n in ((1, 0, (qt + 1) * P), (2, WIN0, w), (0, CMP0, NB)):
                                    last = dve.tensor_scalar(p[:, lo:lo + n], p[:, lo:lo + n],
                                                             factor[:, r, b:b + 1], None, ALU.mult)
                            last.then_inc(p_ready, 1)
                        if qt > 0:
                            dve.wait_ge(out_done, QT * g + qt)
                            for r in range(GROUP):
                                half = slice((r % 2) * HD, (r % 2 + 1) * HD)
                                last = dve.tensor_copy(
                                    mixT[half, bass.ds(2 * g + r // 2, 1), (qt - 1) * P:qt * P],
                                    out_bank[(qt - 1) % 2][0:HD, r * P:(r + 1) * P].unsqueeze(1))
                            last.then_inc(out_taken, 1)

            @block.tensor
            def _(pe):
                pe.wait_ge(kc_ready, 1)

                def free_turn_bank(g, n):
                    if n >= 2:
                        pe.wait_ge(taken, PER_GROUP * g + n - 1)
                    else:
                        pe.wait_ge(taken, PER_GROUP * g)
                    pe.nop(nofuse=True)

                def scores(g, qt, r):
                    n = GROUP * qt + r
                    q = qT[:, r, qt * P:(qt + 1) * P]
                    pe.wait_ge(exped[0], GROUP * QT * g + n)
                    for lo in range(0, (qt + 1) * P, BANK):
                        hi = min(lo + BANK, (qt + 1) * P)
                        diagonal = hi == (qt + 1) * P
                        mm = pe.matmul(slc_bank[:, lo:hi], q, kT[:, 0, lo:hi], start=True, stop=not diagonal)
                        if diagonal:
                            mm = pe.matmul(slc_bank[:, hi - P:hi], K["ident16"][:], K["diagonal"][:],
                                           start=False, stop=True)
                    mm.then_inc(scored[0], 1)
                    pe.wait_ge(exped[1], GROUP * QT * g + n)
                    first = max(0, qt - WT + 1)
                    w = (qt + 1 - first) * P
                    pe.matmul(win_bank[:, 0:w], q, kT[:, 1, first * P:(qt + 1) * P], start=True, stop=False)
                    pe.matmul(win_bank[:, w - P:w], K["ident16"][:], K["diagonal"][:], start=False, stop=True)
                    if qt >= WT:
                        pe.matmul(win_bank[:, BANK:BANK + P], q, kT[:, 1, (qt - WT) * P:(qt - WT + 1) * P],
                                  start=True, stop=False)
                        pe.matmul(win_bank[:, BANK:BANK + P], K["ident16"][:], K["edge"][:], start=False, stop=True)
                    c = (WT + 1) * P
                    pe.matmul(win_bank[:, c:c + NB], q, kc[:, bass.ds(g, 1), 0:NB].rearrange("p a n -> p (a n)"),
                              start=True, stop=False)
                    at = (SEQ - P) // CMP_STRIDE - qt * (P // CMP_STRIDE)
                    pe.matmul(win_bank[:, c:c + NB], K["ident16"][:], K["blocks"][:, at:at + NB], start=False,
                              stop=True).then_inc(scored[1], 1)

                def value_product(g, qt, u):
                    n = unit_base(qt) + u
                    _, rows, source = value_units(qt)[u]
                    pe.wait_ge(taken, PER_GROUP * g + n + 1)
                    if u == 0 and qt >= 2:
                        pe.wait_ge(out_taken, QT * g + qt - 1)
                    elif u == 0:
                        pe.wait_ge(out_taken, QT * g)
                    pe.nop(nofuse=True)
                    v = vc_rows[0:rows, :] if source is None else values[:, source[0], source[1], :]
                    mm = pe.matmul(out_bank[qt % 2][0:HD, :], v, turned_sb[n % 2][0:rows, :],
                                   start=(u == 0), stop=(u == UNITS[qt] - 1))
                    mm.then_inc(pv_done, 1)
                    if u == UNITS[qt] - 1:
                        pe.wait_ge(pv_done, (PER_GROUP - LEAD) * g + n - LEAD + 1)
                        pe.nop().then_inc(out_done, 1)

                with pe.Fori(0, N_KV) as g:
                    pe.wait_ge(q_copied, g + 1)
                    for n in range(QT):
                        free_turn_bank(g, n)
                        for r in range(GROUP):
                            tr = pe.transpose(turn_bank[n % 2][0:HD, r * P:(r + 1) * P], q_rows[:, n, r, :],
                                              K["ident"][:])
                        tr.then_inc(turned, 1)
                    pe.wait_ge(kv_copied, g + 1)
                    for n in range(QT, LEAD):
                        b, half = divmod(n - QT, 2)
                        free_turn_bank(g, n)
                        for i in range(4):
                            tr = pe.transpose(turn_bank[n % 2][0:HD, i * P:(i + 1) * P],
                                              k_rows[:, b, 4 * half + i, :], K["ident"][:])
                        tr.then_inc(turned, 1)
                    pe.wait_ge(taken, PER_GROUP * g + LEAD)
                    pending = None
                    for qt in range(QT + 1):
                        for r in range(GROUP):
                            if qt < QT:
                                scores(g, qt, r)
                            if qt > 0:
                                for u in quarter(qt - 1, r):
                                    lo, rows, _ = value_units(qt - 1)[u]
                                    n = unit_base(qt - 1) + u
                                    if u == 0:
                                        pe.wait_ge(p_ready, QT * g + qt)
                                    free_turn_bank(g, n)
                                    for h in range(GROUP):
                                        tr = pe.transpose(turn_bank[n % 2][0:rows, h * P:(h + 1) * P],
                                                          probs[(qt - 1) % 2][:, h, lo:lo + rows], K["ident"][:])
                                    tr.then_inc(turned, 1)
                                    if pending:
                                        value_product(g, *pending)
                                    pending = (qt - 1, u)
                    value_product(g, *pending)


def stage_attend_sample(nc, mem, K, z_s, pages, cache_slc, state_win, kc_dram, vc_dram, gates_dram, mixT):
    NP = PAST_LEN // PAGE
    HB = DEC_BATCH // 4
    NBLK = (PAST_LEN - CMP_BLOCK) // CMP_STRIDE + 1
    CB = PAST_LEN // CMP_STRIDE
    NSLC = PAST_LEN // SLC_BLOCK
    KG = NP // 4
    WT = WINDOW // P
    NEWP = N_SAMPLE
    UNITS = 8 + NP
    GROUPS = KG + 1
    with ExitStack() as scope:
        q_rows = mem.sb(scope, "as_q_rows", [N_SAMPLE, GROUP, N_KV, HD])
        q_diag = mem.sb(scope, "as_q_diag", [P, DEC_BATCH, N_KV, GROUP, DEC_SEQ])
        k_new = mem.sb(scope, "as_k_new", [P, 2, N_SAMPLE])
        kc = mem.sb(scope, "as_kc", [P, DEC_BATCH, CB])
        vc = mem.sb(scope, "as_vc", [P, DEC_BATCH, CB // P, P])
        state = [mem.sb(scope, f"as_state{i}", [P, 4, WT, KV_WIDTH]) for i in range(HB)]
        gate = mem.sb(scope, "as_gate", [P, HB, 3])
        k_page = [mem.sb(scope, f"as_k_page{i}", [P, 4, 4, P]) for i in range(2)]
        v_page = [mem.sb(scope, f"as_v_page{i}", [P, 4, 4, P]) for i in range(2)]
        kT = [mem.sb(scope, f"as_kT{i}", [P, BANK]) for i in range(2)]
        pT = [mem.sb(scope, f"as_pT{i}", [P, P]) for i in range(2)]
        p_cmp = mem.sb(scope, "as_p_cmp", [P, CB])
        p_cmp_gated = mem.sb(scope, "as_p_cmp_gated", [P, CB])
        p_win = mem.sb(scope, "as_p_win", [P, WINDOW + NEWP])
        p_slc = mem.sb(scope, "as_p_slc", [P, PAST_LEN + NEWP])
        grouped = mem.sb(scope, "as_grouped", [P, NSLC + 1, 4])
        score = [mem.sb(scope, f"as_score{i}", [P, NSLC + 1]) for i in range(2)]
        best = mem.sb(scope, "as_best", [P, 8])
        left_out = mem.sb(scope, "as_left_out", [P, NSLC])
        small = mem.sb(scope, "as_small", [P, 3, 3])
        out_rows = mem.sb(scope, "as_out_rows", [P, P])
        kt_bank = [mem.ps(scope, f"as_kt_bank{i}") for i in range(2)]
        s_bank = [mem.ps(scope, f"as_s_bank{i}") for i in range(2)]
        c_bank = mem.ps(scope, "as_c_bank")
        pt_bank = [mem.ps(scope, f"as_pt_bank{i}") for i in range(2)]
        out_bank = mem.ps(scope, "as_out_bank")

        gates_out, landed, gate_in = mem.sem("as_gates_out"), mem.sem("as_landed"), mem.sem("as_gate_in")
        state_landed = [mem.sem(f"as_state_landed{i}") for i in range(HB)]
        k_landed = [mem.sem(f"as_k_landed{i}") for i in range(2)]
        v_landed = [mem.sem(f"as_v_landed{i}") for i in range(2)]
        v_used = [mem.sem(f"as_v_used{i}") for i in range(2)]
        k_added = [mem.sem(f"as_k_added{i}") for i in range(2)]
        q_packed, q_turned, q_ready, kn_ready = (mem.sem("as_q_packed"), mem.sem("as_q_turned"),
                                                 mem.sem("as_q_ready"), mem.sem("as_kn_ready"))
        c_done, kt_turned, kt_taken, s_done = (mem.sem("as_c_done"), mem.sem("as_kt_turned"),
                                               mem.sem("as_kt_taken"), mem.sem("as_s_done"))
        s_group, s_added = mem.sem("as_s_group"), mem.sem("as_s_added")
        maxed, exped = mem.sem("as_maxed"), mem.sem("as_exped")
        c_normed, g_done, p_ready = mem.sem("as_c_normed"), mem.sem("as_g_done"), mem.sem("as_p_ready")
        pt_turned, pt_taken, pv_done = mem.sem("as_pt_turned"), mem.sem("as_pt_taken"), mem.sem("as_pv_done")
        out_copied, out_turned, out_taken = mem.sem("as_out_copied"), mem.sem("as_out_turned"), mem.sem("as_out_taken")
        dve_step = mem.sem("as_dve_step")

        with nc.Block() as block:
            @block.sync
            def _(sp):
                sp.dma_start(gates_dram, z_s[:, OFF_GATE:OFF_POOL]).then_inc(gates_out, 16)
                sp.dma_start(kc[:], kc_dram).then_inc(landed, 16)
                sp.dma_start(vc[:], vc_dram).then_inc(landed, 16)
                sp.wait_ge(gates_out, 16)
                for b in range(DEC_BATCH):
                    sp.dma_start(gate[32 * (b % 4):32 * (b % 4) + 32, b // 4, :],
                                 gates_dram[DEC_SEQ * b:DEC_SEQ * b + DEC_SEQ, :].rearrange("t (h c) -> h t c", c=3)
                                 ).then_inc(gate_in, 16)
                for hb in range(HB):
                    with sp.Fori(0, KG // 2) as i:
                        for s in range(2):
                            sp.wait_ge(k_added[s], KG // 2 * hb + i)
                            for b in range(4):
                                for j in range(4):
                                    page = sp.value_load(
                                        pages[0:1, bass.ds((4 * hb + b) * NP + 8 * i + 4 * s + j, 1)],
                                        min_val=0, max_val=cache_slc.shape[0] - 1)
                                    sp.dma_start(k_page[s][:, b, j, :],
                                                 cache_slc[bass.ds(page, 1), :, 0:P].rearrange("a t n -> (a t) n")
                                                 ).then_inc(k_landed[s], 16)

            @block.gpsimd
            def _(pool):
                for hb in range(HB):
                    for b in range(4):
                        pool.dma_start(state[hb][:, b], state_win[4 * hb + b].rearrange("(w p) n -> p w n", p=P)
                                       ).then_inc(state_landed[hb], 16)
                for hb in range(HB):
                    with pool.Fori(0, KG // 2) as i:
                        for s in range(2):
                            pool.wait_ge(v_used[s], KG // 2 * hb + i)
                            for b in range(4):
                                for j in range(4):
                                    page = pool.value_load(
                                        pages[0:1, bass.ds((4 * hb + b) * NP + 8 * i + 4 * s + j, 1)],
                                        min_val=0, max_val=cache_slc.shape[0] - 1)
                                    pool.dma_start(v_page[s][:, b, j, :],
                                                   cache_slc[bass.ds(page, 1), :, P:2 * P].rearrange("a t n -> (a t) n")
                                                   ).then_inc(v_landed[s], 16)

            @block.scalar
            def _(act):
                act.sem_inc(kt_taken, 2)
                act.sem_inc(pt_taken, 2)
                act.activation(q_rows[:], z_s[:, 0:NSA_WIDTH].rearrange("p (g r d) -> p r g d", g=N_KV, r=GROUP),
                               ACT.Copy, scale=SCALE).then_inc(q_packed, 1)
                act.wait_ge(q_turned, 2)
                act.activation(k_new[:], pt_bank[1][:, 0:2 * N_SAMPLE].rearrange("p (b n) -> p b n", b=2),
                               ACT.Copy).then_inc(kn_ready, 1)

                def take_kt(hb, g4, b):
                    n = 4 * (GROUPS * hb) + 4 * g4 + b
                    act.wait_ge(kt_turned, n + 1)
                    act.wait_ge(s_done, n + 1)
                    act.activation(kT[b % 2][:], kt_bank[b % 2][:], ACT.Copy).then_inc(kt_taken, 1)

                def take_pt(hb, n, i, rows):
                    act.wait_ge(pt_turned, UNITS * hb + n + 1)
                    act.wait_ge(pv_done, UNITS * hb + n + 1)
                    act.activation(pT[i][0:rows, :], pt_bank[i][0:rows, 0:P], ACT.Copy).then_inc(pt_taken, 1)

                for hb in range(HB):
                    act.wait_ge(maxed, 3 * hb + 1)
                    act.activation(p_cmp[:, 0:NBLK], c_bank[:, 0:NBLK], ACT.Exp, bias=small[:, 0, 0:1],
                                   accum_out=small[:, 1, 0:1]).then_inc(exped, 1)
                    for b in range(4):
                        take_kt(hb, 0, b)
                    act.wait_ge(maxed, 3 * hb + 2)
                    act.activation(p_win[:], p_win[:], ACT.Exp, bias=small[:, 0, 2:3],
                                   accum_out=small[:, 1, 2:3]).then_inc(exped, 1)
                    with act.Fori(0, KG // 2) as i:
                        for s in range(2):
                            for b in range(4):
                                take_kt(hb, 2 * i + s + 1, b)
                    for n in range(7):
                        take_pt(hb, n, n % 2, P if n != 6 else NEWP)
                    act.wait_ge(maxed, 3 * hb + 3)
                    act.activation(p_slc[:], p_slc[:], ACT.Exp, bias=small[:, 0, 1:2],
                                   accum_out=small[:, 1, 1:2]).then_inc(exped, 1)
                    take_pt(hb, 7, 1, NEWP)
                    with act.Fori(0, KG // 2) as i:
                        for n in range(8):
                            take_pt(hb, 8 + 8 * i + n, n % 2, P)
                    act.wait_ge(pv_done, UNITS * (hb + 1) + 2)
                    act.activation(out_rows[:], out_bank[:, 0:P], ACT.Copy).then_inc(out_copied, 1)

            @block.vector
            def _(dve):
                step = Order(dve_step)
                step.did(dve.memset(q_diag[:], 0.0))
                step.did(dve.memset(grouped[:, 0, :], 0.0))
                step.did(dve.memset(p_cmp[:, NBLK:CB], 0.0))
                step.wait(dve)
                dve.wait_ge(q_turned, 1)
                for g in range(N_KV):
                    half = slice(g * HD, (g + 1) * HD)
                    qd = dve.tensor_copy(q_diag[half, :, g].rearrange("p b r t -> p r b t"),
                                         pt_bank[0][half, 0:GROUP * N_SAMPLE].rearrange(
                                             "p (r b t) -> p r b t", r=GROUP, t=DEC_SEQ))
                qd.then_inc(q_ready, 1)
                dve.wait_ge(gate_in, 16 * DEC_BATCH)

                def factor(branch, hb, gated=True):
                    f = small[:, 2, branch:branch + 1]
                    step.did(dve.tensor_scalar(f, small[:, 1, branch:branch + 1], 1e-30, None, ALU.max))
                    step.wait(dve)
                    step.did(dve.reciprocal(f, f))
                    step.wait(dve)
                    if gated:
                        step.did(dve.tensor_tensor(f, f, gate[:, hb, branch:branch + 1], ALU.mult))
                        step.wait(dve)
                    return f

                for hb in range(HB):
                    dve.wait_ge(c_done, hb + 1)
                    if hb:
                        dve.wait_ge(pv_done, UNITS * hb + 2)
                    step.did(dve.tensor_tensor(p_win[:, WINDOW:], c_bank[:, CB + NEWP:CB + 2 * NEWP],
                                               K["new_mask"][:, hb, :], ALU.add))
                    step.did(dve.tensor_tensor(p_slc[:, PAST_LEN:], c_bank[:, CB:CB + NEWP],
                                               K["new_mask"][:, hb, :], ALU.add))
                    step.wait(dve)
                    dve.tensor_reduce(small[:, 0, 0:1], c_bank[:, 0:NBLK], AX.X, ALU.max,
                                      negate=True).then_inc(maxed, 1)
                    dve.wait_ge(exped, 3 * hb + 1)
                    f = factor(0, hb, False)
                    dve.tensor_scalar(p_cmp[:, 0:NBLK], p_cmp[:, 0:NBLK], f, None, ALU.mult).then_inc(c_normed, 1)
                    dve.wait_ge(c_normed, hb + 1)
                    step.did(dve.tensor_scalar(p_cmp_gated[:], p_cmp[:], gate[:, hb, 0:1], None, ALU.mult))
                    dve.wait_ge(s_group, GROUPS * hb + 1)
                    step.did(dve.tensor_tensor(p_win[:, 0:WINDOW], s_bank[0][:], K["win_mask"][:], ALU.add))
                    step.wait(dve)
                    dve.engine_nop().then_inc(s_added, 1)
                    dve.tensor_reduce(small[:, 0, 2:3], p_win[:], AX.X, ALU.max, negate=True).then_inc(maxed, 1)
                    dve.wait_ge(g_done, hb + 1)
                    step.did(dve.tensor_copy(grouped[:, 1:, :], pt_bank[0][:, 0:CB].rearrange("p (j c) -> p j c", c=4)))
                    step.wait(dve)
                    now, before = grouped[:, 1:, :], grouped[:, 0:NSLC, 3]
                    sc = score[0][:, 0:NSLC]
                    step.did(dve.tensor_tensor(sc, now[:, :, 0], now[:, :, 1], ALU.add))
                    step.wait(dve)
                    step.did(dve.tensor_tensor(sc, sc, now[:, :, 2], ALU.add))
                    step.wait(dve)
                    step.did(dve.scalar_tensor_tensor(sc, now[:, :, 3], 0.5, sc, ALU.mult, ALU.add))
                    step.wait(dve)
                    step.did(dve.scalar_tensor_tensor(sc, before, 0.5, sc, ALU.mult, ALU.add))
                    step.wait(dve)
                    step.did(dve.memset(score[0][:, 0:1], 1e4))
                    step.did(dve.memset(score[0][:, NSLC - 1:NSLC + 1], 1e4))
                    step.wait(dve)
                    for i in range(2):
                        step.did(dve.max(best[:], score[i][:]))
                        step.wait(dve)
                        step.did(dve.match_replace(score[1 - i][:], best[:], score[i][:], -1.0))
                        step.wait(dve)
                    step.did(dve.tensor_scalar(left_out[:], score[0][:, 0:NSLC], 0.0, NEG, ALU.is_ge, ALU.mult))
                    dve.wait_ge(exped, 3 * hb + 2)
                    f = factor(2, hb)
                    step.did(dve.tensor_scalar(p_win[:], p_win[:], f, None, ALU.mult))
                    step.wait(dve)
                    dve.engine_nop().then_inc(p_ready, 1)
                    with dve.Fori(0, KG // 2) as i:
                        for s in range(2):
                            dve.wait_ge(s_group, GROUPS * hb + 2 * i + s + 2)
                            mask = left_out[:, bass.ds(16 * i + 8 * s, 8)].unsqueeze(2).to_broadcast([P, 8, SLC_BLOCK])
                            dve.tensor_tensor(p_slc[:, bass.ds((8 * i + 4 * s) * P, BANK)].rearrange(
                                "p (j n) -> p j n", j=8), s_bank[1 - s][:].rearrange("p (j n) -> p j n", j=8),
                                mask, ALU.add).then_inc(k_added[s], 1)
                    for s in range(2):
                        dve.wait_ge(k_added[s], KG // 2 * (hb + 1))
                    dve.tensor_reduce(small[:, 0, 1:2], p_slc[:], AX.X, ALU.max, negate=True).then_inc(maxed, 1)
                    dve.wait_ge(exped, 3 * hb + 3)
                    f = factor(1, hb)
                    step.did(dve.tensor_scalar(p_slc[:], p_slc[:], f, None, ALU.mult))
                    step.wait(dve)
                    dve.engine_nop().then_inc(p_ready, 1)
                    dve.wait_ge(out_turned, hb + 1)
                    src = kt_bank[0][:, 0:P].rearrange("p (b g r t) -> p b g r t", b=4, g=N_KV, r=GROUP)
                    for g in range(N_KV):
                        for r in range(GROUP):
                            half = slice((r % 2) * HD, (r % 2 + 1) * HD)
                            at = SEQ + 16 * hb
                            last = dve.tensor_copy(
                                mixT[half, 2 * g + r // 2, at:at + 16].rearrange("p (b t) -> p b t", t=DEC_SEQ),
                                src[g * HD:(g + 1) * HD, :, g, r, :])
                    last.then_inc(out_taken, 1)

            @block.tensor
            def _(pe):
                pe.sem_inc(s_done, 2)
                pe.sem_inc(pv_done, 2)
                pe.wait_ge(q_packed, 1)
                for r in range(GROUP):
                    tr = pe.transpose(pt_bank[0][:, r * N_SAMPLE:(r + 1) * N_SAMPLE],
                                      q_rows[:, r].rearrange("p g d -> p (g d)"), K["ident"][0:N_SAMPLE, 0:N_SAMPLE])
                tr.then_inc(q_turned, 1)
                for i, off in enumerate((OFF_SLC, OFF_WIN)):
                    tr = pe.transpose(pt_bank[1][:, i * N_SAMPLE:(i + 1) * N_SAMPLE], z_s[:, off:off + P],
                                      K["ident"][0:N_SAMPLE, 0:N_SAMPLE])
                tr.then_inc(q_turned, 1)
                pe.wait_ge(landed, 32)
                pe.wait_ge(q_ready, 1)
                pe.wait_ge(kn_ready, 1)

                def queries(b):
                    return q_diag[:, b].rearrange("p g r t -> p (g r t)")

                def turn_keys(hb, g4, b, tiles):
                    n = 4 * GROUPS * hb + 4 * g4 + b
                    pe.wait_ge(kt_taken, n + 1)
                    for j in range(4):
                        tr = pe.transpose(kt_bank[b % 2][:, j * P:(j + 1) * P], tiles[j], K["ident"][:])
                    tr.then_inc(kt_turned, 1)

                def key_scores(hb, g4, b, bank):
                    n = 4 * GROUPS * hb + 4 * g4 + b
                    pe.wait_ge(kt_taken, n + 3)
                    mm = pe.matmul(bank[32 * b:32 * b + 32, :], queries(4 * hb + b), kT[b % 2][:], start=True, stop=True)
                    mm.then_inc(s_done, 1)
                    if b == 3:
                        pe.wait_ge(s_done, n + 3)
                        pe.nop().then_inc(s_group, 1)

                def key_group(hb, g4, bank, tiles):
                    for b in range(5):
                        if b < 4:
                            turn_keys(hb, g4, b, tiles(b))
                        if b > 0:
                            key_scores(hb, g4, b - 1, bank)

                def turn_probs(hb, n, i, source, rows, copied=None):
                    pe.wait_ge(pt_taken, UNITS * hb + n + 1)
                    pe.transpose(pt_bank[i][0:rows, 0:P], source, K["ident"][:]).then_inc(pt_turned, 1)

                def value_product(hb, n, i, rows, values, first=False, last=False):
                    pe.wait_ge(pt_taken, UNITS * hb + n + 3)
                    for b in range(4):
                        mm = pe.matmul(out_bank[32 * b:32 * b + 32, 0:P], pT[i][0:rows, 32 * b:32 * b + 32],
                                       values(b), start=first, stop=last)
                    mm.then_inc(pv_done, 1)

                for hb in range(HB):
                    if hb:
                        pe.wait_ge(s_added, hb)
                        pe.wait_ge(p_ready, 2 * hb)
                    for b in range(4):
                        rows = slice(32 * b, 32 * b + 32)
                        pe.matmul(c_bank[rows, 0:NBLK], queries(4 * hb + b), kc[:, 4 * hb + b, 0:NBLK],
                                  start=True, stop=True)
                        for i in range(2):
                            mm = pe.matmul(c_bank[rows, CB + i * NEWP:CB + (i + 1) * NEWP], queries(4 * hb + b),
                                           k_new[:, i, :], start=True, stop=True)
                    mm.then_inc(c_done, 1)
                    pe.wait_ge(state_landed[hb], 64)
                    if hb:
                        pe.wait_ge(k_added[1], KG // 2 * hb)
                        pe.wait_ge(out_taken, hb)
                    key_group(hb, 0, s_bank[0], lambda b: [state[hb][:, b, j, 0:P] for j in range(4)])
                    pe.wait_ge(c_normed, hb + 1)
                    if hb:
                        pe.wait_ge(pt_taken, UNITS * hb + 2)
                    pe.matmul(pt_bank[0][:, 0:CB], K["head_sum"][:], p_cmp[:], start=True, stop=True).then_inc(g_done, 1)
                    with pe.Fori(0, KG // 2) as i:
                        for s in range(2):
                            pe.wait_ge(k_landed[s], 256 * (KG // 2 * hb + i + 1))
                            if s == 0:
                                pe.wait_ge(k_added[0], KG // 2 * hb + i)
                            else:
                                pe.wait_ge(s_added, hb + 1)
                                pe.wait_ge(k_added[1], KG // 2 * hb + i)
                            key_group(hb, 2 * i + s + 1, s_bank[1 - s],
                                      lambda b, s=s: [k_page[s][:, b, j, :] for j in range(4)])
                    units = [(p_cmp_gated[:, i * P:(i + 1) * P], P, lambda b, i=i: vc[:, 4 * hb + b, i, :])
                             for i in range(2)]
                    units += [(p_win[:, i * P:(i + 1) * P], P, lambda b, i=i: state[hb][:, b, i, P:2 * P])
                              for i in range(WT)]
                    units += [(p_win[:, WINDOW:], NEWP, lambda b: z_s[:, OFF_WIN + P:OFF_WIN + 2 * P])]
                    units += [(p_slc[:, PAST_LEN:], NEWP, lambda b: z_s[:, OFF_SLC + P:OFF_SLC + 2 * P])]
                    pe.wait_ge(p_ready, 2 * hb + 1)
                    if hb:
                        pe.wait_ge(out_copied, hb)
                    for n in range(9):
                        if n == 7:
                            value_product(hb, 6, 0, NEWP, units[6][2])
                            pe.wait_ge(p_ready, 2 * hb + 2)
                        if n < 8:
                            turn_probs(hb, n, n % 2, units[n][0], units[n][1])
                        if n > 0 and n != 7:
                            value_product(hb, n - 1, (n - 1) % 2, units[n - 1][1], units[n - 1][2], n == 1)

                    def page_group(i, last):
                        for n in range(9):
                            s, j = divmod(n, 4)
                            if n < 8:
                                if j == 0:
                                    pe.wait_ge(v_landed[s], 256 * (KG // 2 * hb + i + 1))
                                turn_probs(hb, 8 + 8 * i + n, n % 2, p_slc[:, (8 * i + n) * P:(8 * i + n + 1) * P], P)
                            if n > 0:
                                s, j = divmod(n - 1, 4)
                                value_product(hb, 7 + 8 * i + n, (n - 1) % 2, P,
                                              lambda b: v_page[s][:, b, j, :], False, last and n == 8)
                                if j == 3:
                                    pe.wait_ge(pv_done, UNITS * hb + 8 + 8 * i + n + 2)
                                    pe.nop().then_inc(v_used[s], 1)
                    for i in range(KG // 2):
                        page_group(i, i == KG // 2 - 1)
                    pe.wait_ge(out_copied, hb + 1)
                    pe.transpose(kt_bank[0][:, 0:P], out_rows[:], K["ident"][:]).then_inc(out_turned, 1)


def stage_out_project(nc, mem, K, trunk, x_saved, w_out):
    mixT = xT = trunk
    w_view = w_out.rearrange("(k p) (m n) -> p m k n", p=P, n=P)
    with ExitStack() as scope:
        mix_hi = mem.sb(scope, "op_mix_hi", [P, KT, T], F32R)
        mix_lo = mem.sb(scope, "op_mix_lo", [P, KT, T], F32R)
        w_raw = [mem.sb(scope, f"op_w_raw{i}", [P, KT, P]) for i in range(2)]
        w_hi = [mem.sb(scope, f"op_w_hi{i}", [P, KT, P], F32R) for i in range(2)]
        w_lo = [mem.sb(scope, f"op_w_lo{i}", [P, KT, P], F32R) for i in range(2)]
        banks = [mem.ps(scope, f"op_bank{i}") for i in range(4)]
        x_in, w_landed = mem.sem("op_x_in"), [mem.sem(f"op_w_landed{i}") for i in range(2)]
        mix_hi_done, mix_split = mem.sem("op_mix_hi_done"), mem.sem("op_mix_split")
        w_hi_done, w_split = mem.sem("op_w_hi_done"), mem.sem("op_w_split")
        done, added = mem.sem("op_done"), mem.sem("op_added")

        with nc.Block() as block:
            @block.sync
            def _(sp):
                for m in range(KT):
                    if m >= 2:
                        sp.wait_ge(w_split, m - 1)
                    sp.dma_start(w_raw[m % 2][:], w_view[:, m]).then_inc(w_landed[m % 2], 16)
                    if m == 2:
                        sp.wait_ge(mix_split, CHUNKS)
                        sp.dma_start(xT[:], x_saved).then_inc(x_in, 16)

            @block.scalar
            def _(act):
                def high(m):
                    act.wait_ge(w_landed[m % 2], 16 * (m // 2) + 16)
                    if m >= 2:
                        act.wait_ge(done, CHUNKS * (m - 1))
                    act.activation(w_hi[m % 2][:], w_raw[m % 2][:], ACT.Copy).then_inc(w_hi_done, 1)

                high(0)
                for c in range(CHUNKS):
                    act.activation(mix_hi[:, :, chunk(c)], mixT[:, :, chunk(c)], ACT.Copy).then_inc(mix_hi_done, 1)
                for m in range(1, KT):
                    high(m)

            @block.vector
            def _(dve):
                def low(m):
                    dve.wait_ge(w_hi_done, m + 1)
                    dve.tensor_tensor(w_lo[m % 2][:], w_raw[m % 2][:], w_hi[m % 2][:].bitcast(F32),
                                      ALU.subtract).then_inc(w_split, 1)

                low(0)
                for c in range(CHUNKS):
                    dve.wait_ge(mix_hi_done, c + 1)
                    dve.tensor_tensor(mix_lo[:, :, chunk(c)], mixT[:, :, chunk(c)],
                                      mix_hi[:, :, chunk(c)].bitcast(F32), ALU.subtract).then_inc(mix_split, 1)
                dve.wait_ge(x_in, 16)
                for m in range(KT):
                    if m + 1 < KT:
                        low(m + 1)
                    for c in range(CHUNKS):
                        n = CHUNKS * m + c
                        dve.wait_ge(done, n + 1)
                        dve.tensor_tensor(xT[:, m, chunk(c)], xT[:, m, chunk(c)], banks[n % 4][:, 0:CH],
                                          ALU.add).then_inc(added, 1)

            @block.tensor
            def _(pe):
                for m in range(KT):
                    pe.wait_ge(w_split, m + 1)
                    for c in range(CHUNKS):
                        n = CHUNKS * m + c
                        if m == 0:
                            pe.wait_ge(mix_split, c + 1)
                        if n >= 4:
                            pe.wait_ge(added, n - 3)
                        for k in range(KT):
                            mm = product3(pe, banks[n % 4][:, 0:CH], w_hi[m % 2][:, k, :], w_lo[m % 2][:, k, :],
                                          mix_hi[:, k, chunk(c)], mix_lo[:, k, chunk(c)], k == 0, k == KT - 1)
                        mm.then_inc(done, 1)


def stage_finish(nc, mem, K, xT, gain, y_prompt, y_sample, states_copied, n_states_copied):
    with ExitStack() as scope:
        h = mem.sb(scope, "fin_h", [P, KT, T])
        y = [mem.sb(scope, f"fin_y{i}", [P, D_MODEL]) for i in range(3)]
        norm = Norm(mem, scope, K, "fin", split=False)
        banks = [mem.ps(scope, f"fin_bank{i}") for i in range(4)]
        sum_bank = mem.ps(scope, "fin_sum")
        turned, taken = mem.sem("fin_turned"), mem.sem("fin_taken")
        out_sem = [mem.sem(f"fin_out{i}") for i in range(3)]

        with nc.Block() as block:
            @block.sync
            def _(sp):
                norm.load(sp, gain)
                for t in range(TT):
                    sp.wait_ge(taken, 2 * t + 2)
                    target = y_prompt[t * P:(t + 1) * P, :] if t < TT - 1 else y_sample
                    n = P if t < TT - 1 else N_SAMPLE
                    sp.dma_start(target, y[t % 3][0:n, :]).then_inc(out_sem[t % 3], 16)
                sp.wait_ge(states_copied, n_states_copied)
                for i in range(3):
                    sp.wait_ge(out_sem[i], 16 * (TT // 3))

            @block.scalar
            def _(act):
                norm.scalar(act, xT, h)
                for t in range(TT):
                    n = P if t < TT - 1 else N_SAMPLE
                    if t >= 3:
                        act.wait_ge(out_sem[t % 3], 16 * (t // 3))
                    for half in range(2):
                        u = 2 * t + half
                        act.wait_ge(turned, u + 1)
                        act.activation(y[t % 3][0:n, half * BANK:(half + 1) * BANK], banks[u % 4][0:n, :],
                                       ACT.Copy).then_inc(taken, 1)

            @block.vector
            def _(dve):
                norm.vector(dve, xT, sum_bank, h, None, K)

            @block.tensor
            def _(pe):
                norm.tensor(pe, sum_bank)
                for t in range(TT):
                    n = P if t < TT - 1 else N_SAMPLE
                    pe.wait_ge(norm.ready, -(-(t * P + n) // CH))
                    for half in range(2):
                        u = 2 * t + half
                        if u >= 4:
                            pe.wait_ge(taken, u - 3)
                        for k in range(4):
                            tr = pe.transpose(banks[u % 4][0:n, k * P:(k + 1) * P],
                                              h[:, 4 * half + k, t * P:t * P + n], K["ident"][:])
                        tr.then_inc(turned, 1)


def stage_constants(nc, mem, targets, narrow=()):
    landed = mem.sem("const_landed")
    with nc.Block() as block:
        @block.sync
        def _(sp):
            for target, source in targets:
                sp.dma_start(target, source).then_inc(landed, 16)
            sp.wait_ge(landed, 16 * len(targets))

        @block.vector
        def _(dve):
            dve.wait_ge(landed, 16 * len(targets))
            for source, target in narrow:
                dve.tensor_copy(target, source)


def stage_copy(nc, mem, pairs):
    copied = mem.sem("copied")
    with nc.Block() as block:
        @block.sync
        def _(sp):
            for target, source in pairs:
                sp.dma_start(target, source).then_inc(copied, 16)
            sp.wait_ge(copied, 16 * len(pairs))


def trunk_step(nc, x_prompt, x_sample, cache_cmp, cache_slc, page_table, state_win, state_pool,
               n_ffn1, w1_gate, w1_up, w1_down, n_mix, w_in, w_cmp_k1, w_cmp_k2, pe_k, w_cmp_v1, w_cmp_v2, pe_v,
               w_pool, pool_scale, w_out, n_ffn2, w2_gate, w2_up, w2_down, n_final,
               c_ident, c_ones, c_cos, c_sin, c_inv_count, c_diagonal, c_edge, c_blocks, c_has_block, c_head_sum,
               c_new_mask, c_win_mask,
               y_prompt, y_sample, new_cmp_prompt, new_slc_prompt, new_win_prompt, new_pool_prompt,
               new_cmp_sample, new_slc_sample, new_win_sample, new_pool_sample):
    x_saved = nc.dram_tensor("x_saved", [P, KT, T], F32).ap()
    kc_saved = nc.dram_tensor("kc_saved", [P, DEC_BATCH, PAST_LEN // CMP_STRIDE], F32).ap()
    vc_saved = nc.dram_tensor("vc_saved", [P, DEC_BATCH, 2, P], F32).ap()
    gates_saved = nc.dram_tensor("gates_saved", [N_SAMPLE, 3 * N_HEADS], F32).ap()
    n_pages = PAST_LEN // PAGE
    BF16 = mybir.dt.bfloat16

    def flat(a):
        return a.rearrange("o b t c g d -> (o b t) (c g d)")

    cmp_weights = ((w_cmp_k1[0], w_cmp_v1[0]), (w_cmp_k2[0], w_cmp_v2[0]), (pe_k, pe_v))
    with ExitStack() as whole:
        mem = Mem(nc)
        K = {"ident": mem.sb(whole, "ident", [P, P]), "ones": mem.sb(whole, "ones", [P, P])}
        pages = mem.sb(whole, "pages", [1, DEC_BATCH * n_pages], I32)
        stage_constants(nc, mem, [(K["ident"][:], c_ident), (K["ones"][:], c_ones), (pages[:], page_table)])

        with ExitStack() as scope:
            kc = mem.sb(scope, "kc", [P, DEC_BATCH, PAST_LEN // CMP_STRIDE])
            vc = mem.sb(scope, "vc", [P, DEC_BATCH, 2, P])
            stage_compress(nc, mem, K, pages, cache_cmp[0].rearrange("a (c s) k g d -> a c (s k g d)", s=CMP_STRIDE),
                           n_pages, DEC_BATCH, PAST_LEN // CMP_STRIDE, *cmp_weights, kc, vc, "cs")
            mem.end_stage()
            stage_copy(nc, mem, [(kc_saved, kc[:]), (vc_saved, vc[:])])

        trunk = mem.sb(whole, "trunk", [P, KT, T])
        win_rows = WINDOW - DEC_SEQ
        state_copies = [(new_win_sample[0, b].rearrange("t c g d -> t (c g d)")[0:win_rows, :],
                         state_win[0, b].rearrange("t c g d -> t (c g d)")[DEC_SEQ:WINDOW, :]) for b in range(DEC_BATCH)]
        state_copies.append((new_pool_sample[0, :, 0:POOL_STATE - DEC_SEQ, :], state_pool[0, :, DEC_SEQ:POOL_STATE, :]))
        states_copied = mem.lasting_sem("states_copied")
        stage_load_x(nc, mem, K, trunk, x_prompt[0], x_sample.rearrange("b t n -> (b t) n"), state_copies, states_copied)
        mem.end_stage()
        stage_ffn(nc, mem, K, trunk, n_ffn1, w1_gate[0], w1_up[0], w1_down[0], "f1")
        mem.end_stage()

        with ExitStack() as mixer:
            z_sample = mem.sb(mixer, "z_sample", [N_SAMPLE, OFF_POOL])
            with ExitStack() as scope_z:
                z = mem.sb(scope_z, "z", [P, TT, OFF_POOL])
                with ExitStack() as scope:
                    for name, shape, source in (("cos", [P, TT, 8], c_cos), ("sin", [P, TT, 8], c_sin),
                                                ("inv_count", [P, 4, 16], c_inv_count)):
                        K[name] = mem.sb(scope, name, shape)
                    stage_constants(nc, mem, [(K["cos"][:], c_cos), (K["sin"][:], c_sin),
                                              (K["inv_count"][:], c_inv_count)])
                    uT = mem.sb(scope, "uT", [P, 4, T])
                    outs = dict(cmp_prompt=flat(new_cmp_prompt), cmp_sample=flat(new_cmp_sample),
                                slc_prompt=flat(new_slc_prompt), slc_sample=flat(new_slc_sample),
                                win_prompt=flat(new_win_prompt), x=x_saved)
                    stage_in_project(nc, mem, K, trunk, n_mix, w_in[0], z, z_sample, uT, outs)
                    mem.end_stage()
                    stage_pool(nc, mem, K, uT, trunk, state_pool[0], w_pool[0], pool_scale, new_pool_prompt[0, 0],
                               new_pool_sample[0])
                    mem.end_stage()
                kcp = mem.sb(scope_z, "kcp", [P, 1, SEQ // CMP_STRIDE])
                vcp = mem.sb(scope_z, "vcp", [P, 1, 1, P])
                spare = trunk[:, 0:4, :].rearrange("p k t -> p (k t)")[:, 0:CMP_STRIDE * KV_WIDTH]
                stage_compress(nc, mem, K, None, flat(new_cmp_prompt).rearrange("(c s) n -> c (s n)", s=CMP_STRIDE),
                               0, 1, SEQ // CMP_STRIDE, *cmp_weights, kcp, vcp, "cp", spare)
                mem.end_stage()
                with ExitStack() as scope:
                    narrow = []
                    for name, width in (("ident16", P), ("diagonal", P), ("edge", P), ("blocks", 120)):
                        K[name] = mem.sb(scope, name, [P, width], BF16)
                    K["has_block"] = mem.sb(scope, "has_block", [P, 1])
                    with ExitStack() as wide_scope:
                        wide = {name: mem.sb(wide_scope, name + "_wide", [P, width])
                                for name, width in (("diagonal", P), ("edge", P), ("blocks", 120))}
                        stage_constants(nc, mem, [(wide["diagonal"][:], c_diagonal), (wide["edge"][:], c_edge),
                                                  (wide["blocks"][:], c_blocks), (K["has_block"][:], c_has_block)],
                                        [(K["ident"][:], K["ident16"][:])]
                                        + [(wide[name][:], K[name][:]) for name in wide])
                    stage_attend_prompt(nc, mem, K, z, kcp[:, 0], vcp[:, 0, 0], trunk)
                    mem.end_stage()
            for name, shape in (("head_sum", [P, P]), ("new_mask", [P, 2, N_SAMPLE]), ("win_mask", [P, WINDOW])):
                K[name] = mem.sb(mixer, name, shape)
            new_rows = [(new_win_sample[0, b].rearrange("t c g d -> t (c g d)")[win_rows:WINDOW, :],
                         z_sample[DEC_SEQ * b:DEC_SEQ * b + DEC_SEQ, OFF_WIN:OFF_GATE]) for b in range(DEC_BATCH)]
            stage_constants(nc, mem, [(K["head_sum"][:], c_head_sum), (K["new_mask"][:], c_new_mask),
                                      (K["win_mask"][:], c_win_mask)] + new_rows)
            stage_attend_sample(nc, mem, K, z_sample, pages, cache_slc[0].rearrange("a t c g d -> a t (c g d)"),
                                state_win[0].rearrange("b t c g d -> b t (c g d)"), kc_saved, vc_saved,
                                gates_saved, trunk)
            mem.end_stage()
        stage_out_project(nc, mem, K, trunk, x_saved, w_out[0])
        mem.end_stage()
        stage_ffn(nc, mem, K, trunk, n_ffn2, w2_gate[0], w2_up[0], w2_down[0], "f2")
        mem.end_stage()
        stage_finish(nc, mem, K, trunk, n_final, y_prompt[0], y_sample.rearrange("b t n -> (b t) n"),
                     states_copied, 16 * len(state_copies))
        mem.end_stage()


_INS = ["x_prompt", "x_sample", "cache_kv_cmp", "cache_kv_slc", "page_table", "state_kv_win", "state_pool",
        "n_ffn1", "w_ffn1_gate", "w_ffn1_up", "w_ffn1_down", "n_mix", "w_in", "w_cmp_k1", "w_cmp_k2", "pe_cmp_k",
        "w_cmp_v1", "w_cmp_v2", "pe_cmp_v", "w_pool", "pool_scale", "w_out", "n_ffn2", "w_ffn2_gate", "w_ffn2_up",
        "w_ffn2_down", "n_final"]
_KV = (2, N_KV, HD)
_OUTS = [(1, SEQ, D_MODEL), (DEC_BATCH, DEC_SEQ, D_MODEL), (1, 1, SEQ, *_KV), (1, 1, SEQ, *_KV), (1, 1, WINDOW, *_KV),
         (1, 1, POOL_STATE, POOL_WIDTH), (1, DEC_BATCH, DEC_SEQ, *_KV), (1, DEC_BATCH, DEC_SEQ, *_KV),
         (1, DEC_BATCH, WINDOW, *_KV), (1, DEC_BATCH, POOL_STATE, POOL_WIDTH)]


def shape_constants():
    f32 = np.float32
    inv = np.power(f32(500000.0), -np.arange(8, dtype=f32) / f32(8)).astype(f32)
    pos = np.concatenate([np.arange(SEQ), np.tile(PAST_LEN + np.arange(DEC_SEQ), DEC_BATCH),
                          np.zeros(TT * P - T)]).astype(f32)
    ang = pos[:, None] * inv
    tiles = lambda a: np.ascontiguousarray(a.reshape(TT, P, 8).transpose(1, 0, 2))
    inv_count = np.zeros((P, 4, 16), f32)
    for g, w in enumerate(POOL_WINDOWS):
        inv_count[:, g] = 1 / np.minimum(w, np.arange(16) + 1)
    row, col = np.arange(P)[:, None], np.arange(P)[None]
    starts = np.arange(120)[None] - 56
    req, kvh, tok = row // 32, (row // 16) % 2, row % 4
    new_mask = np.zeros((P, 2, N_SAMPLE), f32)
    key = np.arange(N_SAMPLE)[None]
    for half in range(2):
        new_mask[:, half] = np.where((key // DEC_SEQ == 4 * half + req) & (key % DEC_SEQ <= tok), 0, NEG)
    return dict(
        ident=np.eye(P, dtype=f32), ones=np.ones((P, P), f32), cos=tiles(np.cos(ang)), sin=tiles(np.sin(ang)),
        inv_count=inv_count, diagonal=np.where(col <= row, 0, NEG).astype(f32),
        edge=np.where(col >= row, 0, NEG).astype(f32),
        blocks=np.where(CMP_STRIDE * starts + CMP_BLOCK - 1 <= row, 0, NEG).astype(f32),
        has_block=(row >= CMP_BLOCK - 1).astype(f32),
        head_sum=((req == req.T) & (kvh == kvh.T) & (tok == tok.T)).astype(f32),
        new_mask=new_mask, win_mask=np.where(np.arange(WINDOW)[None] >= tok, 0, NEG).astype(f32))


def kernel(**inputs):
    import concourse.bacc as bacc
    from concourse.bass_utils import run_bass_kernel_spmd

    nc = bacc.Bacc("TRN2", target_bir_lowering=False, num_devices=1)

    def columns(a):
        return np.ascontiguousarray(a.reshape(-1, P).T)

    arrays, args = {}, []
    for name in _INS:
        a = np.ascontiguousarray(inputs[name])
        if name in ("n_ffn1", "n_mix", "n_ffn2", "n_final", "pool_scale", "pe_cmp_k", "pe_cmp_v"):
            a = columns(a)
        if name == "page_table":
            a = a.reshape(1, -1)
        arrays[f"in_{name}_dram"] = a
    for name, a in shape_constants().items():
        arrays[f"const_{name}_dram"] = a
    for name, a in arrays.items():
        args.append(nc.dram_tensor(name, a.shape, mybir.dt.from_np(a.dtype), kind="ExternalInput").ap())
    for i, shape in enumerate(_OUTS):
        args.append(nc.dram_tensor(f"out_{i}_dram", shape, F32, kind="ExternalOutput").ap())
    trunk_step(nc, *args)
    r = run_bass_kernel_spmd(nc, [arrays], core_ids=[0])
    return tuple(r.results[0][f"out_{i}_dram"] for i in range(len(_OUTS)))
```

```python
from contextlib import ExitStack

import numpy as np

import concourse.bass as bass
from concourse import mybir

F32 = mybir.dt.float32
F32R = mybir.dt.float32r
I32 = mybir.dt.int32
ACT = mybir.ActivationFunctionType
ALU = mybir.AluOpType
AX = mybir.AxisListType

P = 128
BANK = 512
D_MODEL, SEQ, DEC_BATCH, DEC_SEQ = 1024, 1024, 8, 4
PAST_LEN, PAGE, WINDOW = 4096, 128, 512
N_SAMPLE = DEC_BATCH * DEC_SEQ
T = SEQ + N_SAMPLE
CHUNKS = 3
CH = T // CHUNKS
KT = D_MODEL // P
TT = SEQ // P + 1
D_FF = 2816
FT = D_FF // P
HD, N_HEADS, N_KV, GROUP = 64, 8, 2, 4
NSA_WIDTH, POOL_WIDTH, KV_WIDTH = 512, 512, 256
OFF_CMP, OFF_SLC, OFF_WIN, OFF_GATE = 512, 768, 1024, 1280
OFF_POOL = OFF_GATE + 3 * N_HEADS
IN_WIDTH = OFF_POOL + POOL_WIDTH
CMP_STRIDE, CMP_HIDDEN, CMP_BLOCK = 16, 256, 32
SLC_BLOCK = 64
POOL_WINDOWS = (2, 4, 8, 16)
POOL_STATE = 15
SCALE = HD ** -0.5
EPS = 1e-6
NEG = -1e30


class Order:

    def __init__(self, sem):
        self.sem, self.n = sem, 0

    def did(self, instruction):
        instruction.then_inc(self.sem, 1)
        self.n += 1
        return instruction

    def wait(self, engine):
        engine.wait_ge(self.sem, self.n)


class Mem:

    def __init__(self, nc):
        self.nc, self.serial, self.stage_sems = nc, 0, []

    def sem(self, name):
        self.stage_sems.append(self.lasting_sem(name))
        return self.stage_sems[-1]

    def lasting_sem(self, name):
        self.serial += 1
        return self.nc.alloc_semaphore(name=f"{name}_{self.serial}")

    def end_stage(self):
        self.nc.clear_and_free_semaphores(self.stage_sems)
        self.nc.all_engine_barrier()
        self.stage_sems = []

    def sb(self, stack, name, shape, dt=F32):
        self.serial += 1
        return stack.enter_context(self.nc.sbuf_tensor(f"{name}_{self.serial}", shape, dt))

    def ps(self, stack, name, shape=(P, BANK)):
        self.serial += 1
        return stack.enter_context(self.nc.psum_tensor(f"{name}_{self.serial}", list(shape), F32))


def product3(pe, out, w_hi, w_lo, x_hi, x_lo, first, last):
    pe.matmul(out, w_hi, x_hi, start=first, stop=False)
    pe.matmul(out, w_hi, x_lo, start=False, stop=False)
    return pe.matmul(out, w_lo, x_hi, start=False, stop=last)


def chunk(c):
    return slice(c * CH, (c + 1) * CH)


class Norm:

    def __init__(self, mem, scope, K, name, split=True):
        self.K = K
        self.sq = mem.sb(scope, name + "_sq", [P, KT, CH])
        if split:
            self.h = mem.sb(scope, name + "_h", [P, KT, CH])
        self.var = mem.sb(scope, name + "_var", [P, CH])
        self.inv = mem.sb(scope, name + "_inv", [P, CH])
        self.tmp = self.h[:, 0, :] if split else mem.sb(scope, name + "_tmp", [P, CH])[:]
        self.gain = mem.sb(scope, name + "_gain", [P, KT])
        self.split = split
        self.gain_in = mem.sem(name + "_gain_in")
        self.sq_done = mem.sem(name + "_sq_done")
        self.sum_done = mem.sem(name + "_sum_done")
        self.var_done = mem.sem(name + "_var_done")
        self.h_done = mem.sem(name + "_h_done")
        self.hi_done = mem.sem(name + "_hi_done")
        self.rms_done = mem.sem(name + "_rms_done")
        self.dve_step = mem.sem(name + "_dve_step")
        self.ready = mem.sem(name + "_ready")

    def load(self, sp, gain):
        sp.dma_start(self.gain[:], gain).then_inc(self.gain_in, 16)

    def scalar(self, act, xT, h_hi):
        def root(c):
            act.wait_ge(self.var_done, c + 1)
            if c:
                act.wait_ge(self.h_done, 2 * c)
            act.activation(self.inv[:], self.var[:], ACT.Sqrt).then_inc(self.rms_done, 1)

        act.activation(self.sq[:], xT[:, :, chunk(0)], ACT.Square).then_inc(self.sq_done, 1)
        root(0)
        for c in range(CHUNKS):
            if c + 1 < CHUNKS:
                act.wait_ge(self.sum_done, c + 1)
                act.activation(self.sq[:], xT[:, :, chunk(c + 1)], ACT.Square).then_inc(self.sq_done, 1)
            for k in range(0, KT if self.split else 0, KT // 2):
                n = 2 * c + (k > 0) + 1
                act.wait_ge(self.h_done, n)
                act.activation(h_hi[:, k:k + KT // 2, chunk(c)], self.h[:, k:k + KT // 2, :],
                               ACT.Copy).then_inc(self.hi_done, 1)
            if c + 1 < CHUNKS:
                root(c + 1)

    def tensor(self, pe, bank):
        for c in range(CHUNKS):
            pe.wait_ge(self.sq_done, c + 1)
            if c:
                pe.wait_ge(self.var_done, c)
            for k in range(KT):
                mm = pe.matmul(bank[:, 0:CH], self.K["ones"][:], self.sq[:, k, :],
                               start=(k == 0), stop=(k == KT - 1))
            mm.then_inc(self.sum_done, 1)

    def vector(self, dve, xT, bank, h_hi, h_lo):
        step = Order(self.dve_step)

        def mean_square(c):
            dve.wait_ge(self.sum_done, c + 1)
            dve.tensor_scalar(self.var[:], bank[:, 0:CH], 1.0 / D_MODEL, EPS, ALU.mult,
                              ALU.add).then_inc(self.var_done, 1)

        def reciprocal_root(c):
            dve.wait_ge(self.var_done, c + 1)
            dve.wait_ge(self.rms_done, c + 1)
            step.did(dve.reciprocal(self.inv[:], self.inv[:]))
            step.wait(dve)
            step.did(dve.tensor_tensor(self.tmp, self.inv[:], self.inv[:], ALU.mult))
            step.wait(dve)
            step.did(dve.tensor_tensor(self.tmp, self.tmp, self.var[:], ALU.mult))
            step.wait(dve)
            step.did(dve.tensor_scalar(self.tmp, self.tmp, -0.5, 1.5, ALU.mult, ALU.add))
            step.wait(dve)
            step.did(dve.tensor_tensor(self.inv[:], self.inv[:], self.tmp, ALU.mult))
            step.wait(dve)

        mean_square(0)
        dve.wait_ge(self.gain_in, 16)
        for c in range(CHUNKS):
            reciprocal_root(c)
            for k in range(KT):
                out = self.h[:, k, :] if self.split else h_hi[:, k, chunk(c)]
                last = dve.scalar_tensor_tensor(out, xT[:, k, chunk(c)], self.gain[:, k:k + 1],
                                                self.inv[:], ALU.mult, ALU.mult)
                if k % (KT // 2) == KT // 2 - 1:
                    last.then_inc(self.h_done, 1)
            if c + 1 < CHUNKS:
                mean_square(c + 1)
            for k in range(0, KT if self.split else 0, KT // 2):
                part = slice(k, k + KT // 2)
                dve.wait_ge(self.hi_done, 2 * c + (k > 0) + 1)
                low = dve.tensor_tensor(h_lo[:, part, chunk(c)], self.h[:, part, :],
                                        h_hi[:, part, chunk(c)].bitcast(F32), ALU.subtract)
                if k:
                    low.then_inc(self.ready, 1)


def stage_load_x(nc, mem, K, xT, x_prompt, x_sample, copies, copied):
    with ExitStack() as scope:
        x_in = mem.sb(scope, "x_in", [P, TT, D_MODEL])
        banks = [mem.ps(scope, f"xbank{i}") for i in range(4)]
        landed = [mem.sem(f"x_landed{t}") for t in range(TT)]
        turned, taken = mem.sem("x_turned"), mem.sem("x_taken")

        with nc.Block() as block:
            @block.gpsimd
            def _(pool):
                for target, source in copies:
                    pool.dma_start(target, source).then_inc(copied, 16)

            @block.sync
            def _(sp):
                for t in range(TT):
                    if t < TT - 1:
                        sp.dma_start(x_in[:, t, :], x_prompt[t * P:(t + 1) * P, :]).then_inc(landed[t], 16)
                    else:
                        sp.dma_start(x_in[0:N_SAMPLE, t, :], x_sample).then_inc(landed[t], 16)

            @block.tensor
            def _(pe):
                for t in range(TT):
                    n = P if t < TT - 1 else N_SAMPLE
                    pe.wait_ge(landed[t], 16)
                    for half in range(2):
                        u = 2 * t + half
                        if u >= 4:
                            pe.wait_ge(taken, u - 3)
                        for k in range(4):
                            tr = pe.transpose(banks[u % 4][:, k * P:k * P + n],
                                              x_in[0:n, t, (4 * half + k) * P:(4 * half + k + 1) * P],
                                              K["ident"][0:n, 0:n])
                        tr.then_inc(turned, 1)

            @block.vector
            def _(dve):
                for t in range(TT):
                    n = P if t < TT - 1 else N_SAMPLE
                    for half in range(2):
                        u = 2 * t + half
                        dve.wait_ge(turned, u + 1)
                        dve.tensor_copy(
                            xT[:, 4 * half:4 * half + 4, t * P:t * P + n],
                            banks[u % 4][:, :].rearrange("p (k n) -> p k n", k=4)[:, :, 0:n],
                        ).then_inc(taken, 1)


def stage_ffn(nc, mem, K, xT, gain, w_gate, w_up, w_down, name):
    PAIRS = FT // 2
    wg_v = w_gate.rearrange("(k p) (f n) -> p k f n", p=P, n=P)
    wu_v = w_up.rearrange("(k p) (f n) -> p k f n", p=P, n=P)
    wd_v = w_down.rearrange("(f p) n -> p f n", p=P)
    with ExitStack() as scope:
        h_hi = mem.sb(scope, name + "_h_hi", [P, KT, T], F32R)
        h_lo = mem.sb(scope, name + "_h_lo", [P, KT, T], F32R)
        with ExitStack() as norm_scope:
            norm = Norm(mem, norm_scope, K, name)
        wd_hi = mem.sb(scope, name + "_wd_hi", [P, 2, D_MODEL], F32R)
        wd_lo = mem.sb(scope, name + "_wd_lo", [P, 2, D_MODEL], F32R)
        act_up = mem.sb(scope, name + "_act_up", [P, CH])
        gu_raw, gu_hi, gu_lo = [None] * 2, [None] * 2, [None] * 2
        for s in (1, 0):
            gu_raw[s] = mem.sb(scope, f"{name}_gu_raw{s}", [P, 2, KT, P])
            gu_hi[s] = mem.sb(scope, f"{name}_gu_hi{s}", [P, 2, KT, P], F32R)
            gu_lo[s] = mem.sb(scope, f"{name}_gu_lo{s}", [P, 2, KT, P], F32R)
        wd_raw = mem.sb(scope, name + "_wd_raw", [P, 2, D_MODEL])
        a_hi = mem.sb(scope, name + "_a_hi", [P, 2, T], F32R)
        a_lo = mem.sb(scope, name + "_a_lo", [P, 2, T], F32R)
        act_gate = mem.sb(scope, name + "_act_gate", [P, 2, CH])
        gate_bank = [mem.ps(scope, f"{name}_gate{i}") for i in range(2)]
        up_bank = [mem.ps(scope, f"{name}_up{i}") for i in range(2)]
        down_bank = [mem.ps(scope, f"{name}_down{i}") for i in range(4)]
        sum_bank = down_bank[0]

        gu_landed = [mem.sem(f"{name}_gu_landed{s}") for s in range(2)]
        gu_hi_done = [mem.sem(f"{name}_gu_hi_done{s}") for s in range(2)]
        gu_split = [mem.sem(f"{name}_gu_split{s}") for s in range(2)]
        wd_landed, wd_hi_done = mem.sem(name + "_wd_landed"), mem.sem(name + "_wd_hi_done")
        wd_split = mem.sem(name + "_wd_split")
        gate_done, up_done = mem.sem(name + "_gate_done"), mem.sem(name + "_up_done")
        silu_done, pair_free = mem.sem(name + "_silu_done"), mem.sem(name + "_pair_free")
        a_ready, dve_step = mem.sem(name + "_a_ready"), mem.sem(name + "_dve_step2")
        down_done, down_free = mem.sem(name + "_down_done"), mem.sem(name + "_down_free")
        UNITS = 2 * CHUNKS
        DOWNS = KT * CHUNKS

        with nc.Block() as block:
            @block.sync
            def _(sp):
                norm.load(sp, gain)

                def load_gu(s, i, tile):
                    sp.wait_ge(gu_split[s], i)
                    sp.dma_start(gu_raw[s][:, 0], wg_v[:, :, tile, :]).then_inc(gu_landed[s], 16)
                    sp.dma_start(gu_raw[s][:, 1], wu_v[:, :, tile, :]).then_inc(gu_landed[s], 16)

                def pair(i, last):
                    load_gu(1, i, 2 * i + 1)
                    sp.wait_ge(wd_split, i)
                    sp.dma_start(wd_raw[:], wd_v[:, bass.ds(2 * i, 2), :]).then_inc(wd_landed, 16)
                    if not last:
                        load_gu(0, i + 1, 2 * i + 2)

                load_gu(0, 0, 0)
                sp.wait_ge(norm.ready, CHUNKS)
                with sp.Fori(0, PAIRS - 1) as i:
                    pair(i, False)
                pair(PAIRS - 1, True)

            @block.scalar
            def _(act):
                def high_gu(s, i, first=False):
                    act.wait_ge(gu_landed[s], 32 * i + 32)
                    if not first:
                        act.wait_ge(up_done, UNITS * i if s else UNITS * i - CHUNKS)
                    act.activation(gu_hi[s][:], gu_raw[s][:], ACT.Copy).then_inc(gu_hi_done[s], 1)

                def silu(i, s, c):
                    u = UNITS * i + CHUNKS * s + c
                    b = (CHUNKS * s + c) % 2
                    act.wait_ge(gate_done, u + 1)
                    act.wait_ge(pair_free, u + 1)
                    act.activation(act_gate[:, b, :], gate_bank[b][:, 0:CH], ACT.Silu).then_inc(silu_done, 1)

                def pair(i, last):
                    high_gu(1, i)
                    for c in range(CHUNKS):
                        silu(i, 0, c)
                    act.wait_ge(wd_landed, 16 * i + 16)
                    act.wait_ge(down_done, DOWNS * i)
                    act.activation(wd_hi[:], wd_raw[:], ACT.Copy).then_inc(wd_hi_done, 1)
                    if not last:
                        high_gu(0, i + 1)
                    for c in range(CHUNKS):
                        silu(i, 1, c)

                high_gu(0, 0, True)
                norm.scalar(act, xT, h_hi)
                with act.Fori(0, PAIRS - 1) as i:
                    pair(i, False)
                pair(PAIRS - 1, True)

            @block.vector
            def _(dve):
                dve.sem_inc(pair_free, 2)
                dve.sem_inc(down_free, 4)

                def low_gu(s, i):
                    dve.wait_ge(gu_hi_done[s], i + 1)
                    dve.tensor_tensor(gu_lo[s][:], gu_raw[s][:], gu_hi[s][:].bitcast(F32),
                                      ALU.subtract).then_inc(gu_split[s], 1)

                low_gu(0, 0)
                norm.vector(dve, xT, sum_bank, h_hi, h_lo)

                def multiply(i, s, c):
                    u = UNITS * i + CHUNKS * s + c
                    b = (CHUNKS * s + c) % 2
                    dve.wait_ge(silu_done, u + 1)
                    dve.wait_ge(up_done, u + 1)
                    dve.wait_ge(a_ready, u)
                    dve.tensor_tensor(act_up[:], act_gate[:, b, :], up_bank[b][:, 0:CH],
                                      ALU.mult).then_inc(pair_free, 1)
                    dve.wait_ge(pair_free, u + 3)
                    dve.tensor_copy(a_hi[:, s, chunk(c)], act_up[:]).then_inc(dve_step, 1)
                    dve.wait_ge(dve_step, u + 1)
                    dve.tensor_tensor(a_lo[:, s, chunk(c)], act_up[:], a_hi[:, s, chunk(c)].bitcast(F32),
                                      ALU.subtract).then_inc(a_ready, 1)

                def pair(i, last):
                    low_gu(1, i)
                    for c in range(CHUNKS):
                        multiply(i, 0, c)
                    dve.wait_ge(wd_hi_done, i + 1)
                    dve.tensor_tensor(wd_lo[:], wd_raw[:], wd_hi[:].bitcast(F32),
                                      ALU.subtract).then_inc(wd_split, 1)
                    if not last:
                        low_gu(0, i + 1)
                    for c in range(CHUNKS):
                        multiply(i, 1, c)
                    dve.wait_ge(down_free, DOWNS * i + 4)
                    for c in range(CHUNKS):
                        for m in range(KT):
                            n = KT * c + m
                            dve.wait_ge(down_done, DOWNS * i + n + 1)
                            dve.scalar_tensor_tensor(xT[:, m, chunk(c)], down_bank[n % 4][:, 0:CH], 0.5,
                                                     xT[:, m, chunk(c)], ALU.mult,
                                                     ALU.add).then_inc(down_free, 1)

                with dve.Fori(0, PAIRS - 1) as i:
                    pair(i, False)
                pair(PAIRS - 1, True)

            @block.tensor
            def _(pe):
                norm.tensor(pe, sum_bank)

                def gate_up(i, s, c):
                    u = UNITS * i + CHUNKS * s + c
                    b = (CHUNKS * s + c) % 2
                    pe.wait_ge(pair_free, u + 1)
                    for j, (bank, done) in enumerate(((gate_bank[b], gate_done), (up_bank[b], up_done))):
                        for k in range(KT):
                            mm = product3(pe, bank[:, 0:CH], gu_hi[s][:, j, k, :], gu_lo[s][:, j, k, :],
                                          h_hi[:, k, chunk(c)], h_lo[:, k, chunk(c)], k == 0, k == KT - 1)
                        mm.then_inc(done, 1)

                def pair(i, first):
                    for s in range(2):
                        pe.wait_ge(gu_split[s], i + 1)
                        for c in range(CHUNKS):
                            if first and s == 0:
                                pe.wait_ge(norm.ready, c + 1)
                            gate_up(i, s, c)
                    pe.wait_ge(wd_split, i + 1)
                    for c in range(CHUNKS):
                        pe.wait_ge(a_ready, UNITS * i + CHUNKS + c + 1)
                        for m in range(KT):
                            n = KT * c + m
                            pe.wait_ge(down_free, DOWNS * i + n + 1)
                            for s in range(2):
                                mm = product3(pe, down_bank[n % 4][:, 0:CH],
                                              wd_hi[:, s, m * P:(m + 1) * P], wd_lo[:, s, m * P:(m + 1) * P],
                                              a_hi[:, s, chunk(c)], a_lo[:, s, chunk(c)], s == 0, s == 1)
                            mm.then_inc(down_done, 1)

                pair(0, True)
                with pe.Fori(1, PAIRS) as i:
                    pair(i, False)


def stage_compress(nc, mem, K, pages, source, n_pages_seq, n_seq, chunks, w1, w2, pe_cols,
                   kc_out, vc_out, name, bias, bias_known=False, spare=None):
    HALVES = max(1, chunks // P)
    R = min(chunks, P)
    W = chunks + 2
    SLOTS = CMP_BLOCK // CMP_STRIDE
    NF = CMP_HIDDEN // P
    UNITS = HALVES * KT // 2
    ALL = n_seq * 2
    VT = max(1, chunks // P)
    with ExitStack() as scope:
        raw = [mem.sb(scope, f"{name}_raw{h}", [P, CMP_STRIDE * KV_WIDTH]) if h == 0 or spare is None else spare
               for h in range(2)]
        w1_hi = [mem.sb(scope, f"{name}_w1_hi{j}", [P, SLOTS * KT, CMP_HIDDEN], F32R) for j in range(2)]
        with ExitStack() as landing:
            w1_whole = [mem.sb(landing, f"{name}_w1_whole{j}", [P, SLOTS * KT, CMP_HIDDEN]) for j in range(2)]
        w1_lo = [mem.sb(scope, f"{name}_w1_lo{j}", [P, SLOTS * KT, CMP_HIDDEN], F32R) for j in range(2)]
        w2_sb = mem.sb(scope, name + "_w2", [P, 2, NF, HD])
        pe_sb = mem.sb(scope, name + "_pe", [P, 2, SLOTS * KT])
        x_hi = [mem.sb(scope, f"{name}_x_hi{j}", [P, KT, N_KV, W], F32R) for j in range(2)]
        x_lo = [mem.sb(scope, f"{name}_x_lo{j}", [P, KT, N_KV, W], F32R) for j in range(2)]
        packed = [mem.sb(scope, f"{name}_packed{i}", [P, N_KV, CMP_STRIDE, HD]) for i in range(2)]
        hidden = [mem.sb(scope, f"{name}_hidden{j}", [P, NF, N_KV, chunks]) for j in range(2)]
        turn_bank = [mem.ps(scope, f"{name}_turn{i}") for i in range(2)]
        hid_bank = [mem.ps(scope, f"{name}_hid{i}") for i in range(NF)]
        out_bank = [mem.ps(scope, f"{name}_out{i}") for i in range(2)]

        w_landed = [mem.sem(f"{name}_w_landed{j}") for j in range(2)]
        small_landed, w_hi_done = mem.sem(name + "_small_landed"), mem.sem(name + "_w_hi_done")
        w_split, bias_sum = mem.sem(name + "_w_split"), mem.sem(name + "_bias_sum")
        bias_done, zeroed = mem.sem(name + "_bias_done"), mem.sem(name + "_zeroed")
        raw_landed = [mem.sem(f"{name}_raw_landed{h}") for h in range(HALVES)]
        packed_done = [mem.sem(f"{name}_packed_done{i}") for i in range(2)]
        turned = [mem.sem(f"{name}_turned{j}") for j in range(2)]
        x_hi_done = [mem.sem(f"{name}_x_hi_done{j}") for j in range(2)]
        x_ready = [mem.sem(f"{name}_x_ready{j}") for j in range(2)]
        hid_done, gelu_done = mem.sem(name + "_hid_done"), mem.sem(name + "_gelu_done")
        out_done, out_taken = mem.sem(name + "_out_done"), mem.sem(name + "_out_taken")
        LOADS = R // 8 if pages is not None else 1


        def pack_slot(j, h):
            return (j * HALVES + h) % 2

        def packs(b, j, h):
            return 2 * b + j + 1 if HALVES == 2 else b + 1

        with nc.Block() as block:
            @block.sync
            def _(sp):
                def load_w1(j):
                    sp.dma_start(w1_whole[j][:],
                                 w1[j].rearrange("(k p) f -> p k f", p=P)).then_inc(w_landed[j], 16)

                for j in range(2):
                    sp.dma_start(pe_sb[:, j], pe_cols[j]).then_inc(small_landed, 16)
                load_w1(0)

                def load(b, again):
                    for h in range(HALVES):
                        if again:
                            sp.wait_ge(packed_done[pack_slot(1, h)], packs(b - 1, 1, h))
                        if pages is None:
                            sp.dma_start(raw[h][0:R, :], source).then_inc(raw_landed[h], 16)
                            continue
                        for q in range(LOADS):
                            if q % 8 == 0:
                                _, numbers = nc.values_load_multi_w_load_instructions(
                                    pages[0:1, bass.ds(b * n_pages_seq + LOADS * h + q, 8)],
                                    [mybir.EngineType.SP], min_val=0, max_val=source.shape[0] - 1)
                            page = numbers[q % 8]
                            sp.dma_start(raw[h][8 * q:8 * q + 8, :],
                                         source[bass.ds(page, 1)].rearrange("a c n -> (a c) n")
                                         ).then_inc(raw_landed[h], 16)

                load(0, False)
                load_w1(1)
                sp.wait_ge(small_landed, 32)
                for j in range(2):
                    sp.dma_start(w2_sb[:, j], w2[j].rearrange("(k p) n -> p k n", p=P)).then_inc(small_landed, 16)
                if n_seq > 1:
                    with sp.Fori(1, n_seq) as b:
                        load(b, True)

            @block.scalar
            def _(act):
                def high_w1(j):
                    act.wait_ge(w_landed[j], 16)
                    act.activation(w1_hi[j][:], w1_whole[j][:], ACT.Copy).then_inc(w_hi_done, 1)

                def pack(b, j, h, first=False):
                    act.wait_ge(raw_landed[h], 16 * LOADS * (b + 1))
                    if j == 1 and HALVES == 2:
                        act.wait_ge(turned[0], UNITS * b + 4 * (h + 1))
                    elif not first:
                        act.wait_ge(turned[1], UNITS * (b - 1) + 4 * (h + 1))
                    i = pack_slot(j, h)
                    rows = raw[h][0:R, :].rearrange("p (s j g d) -> p j g s d", s=CMP_STRIDE, j=2, g=N_KV)
                    act.activation(packed[i][0:R], rows[:, j], ACT.Copy).then_inc(packed_done[i], 1)

                def high_x(b, j, t):
                    h, q = divmod(t, KT // 2)
                    act.wait_ge(turned[j], UNITS * b + t + 1)
                    bank = turn_bank[(UNITS * j + t) % 2]
                    act.activation(x_hi[j][:, 2 * q:2 * q + 2, :, h * R:h * R + R],
                                   bank[:, 0:4 * R].rearrange("p (k g n) -> p k g n", k=2, g=2),
                                   ACT.Copy).then_inc(x_hi_done[j], 1)

                def gelu(b, j, f):
                    u = 2 * NF * b + NF * j + f
                    act.wait_ge(hid_done, u + 1)
                    act.activation(hidden[j][:, f], hid_bank[f][:, 0:2 * chunks].rearrange("p (g n) -> p g n", g=2),
                                   ACT.Gelu_apprx_tanh,
                                   bias=bias[:, NF * j + f:NF * j + f + 1]).then_inc(gelu_done, 1)

                def slot(highs, pack_next, gelu_now):
                    for u in highs[:len(highs) // 2]:
                        high_x(*u)
                    if pack_next is not None:
                        pack(*pack_next)
                    for u in highs[len(highs) // 2:]:
                        high_x(*u)
                    gelu(*gelu_now)

                def sequence(b, last):
                    span = [range(f * UNITS // 2, (f + 1) * UNITS // 2) for f in range(NF)]
                    slot([(b, 1, t) for t in span[0]], (b, 1, 1) if HALVES == 2 else None, (b, 0, 0))
                    slot([(b, 1, t) for t in span[1]], None if last else (b + 1, 0, 0), (b, 0, 1))
                    slot([] if last else [(b + 1, 0, t) for t in span[0]],
                         None if last else (b + 1, 0, 1), (b, 1, 0))
                    slot([] if last else [(b + 1, 0, t) for t in span[1]],
                         None if last else (b + 1, 1, 0), (b, 1, 1))

                high_w1(0)
                for h in range(HALVES):
                    pack(0, 0, h, True)
                for t in range(UNITS):
                    high_x(0, 0, t)
                pack(0, 1, 0, HALVES == 1)
                high_w1(1)
                act.wait_ge(bias_done, 1)
                if n_seq > 1:
                    with act.Fori(0, n_seq - 1) as b:
                        sequence(b, False)
                sequence(n_seq - 1, True)

            @block.vector
            def _(dve):
                for j in range(2):
                    for x in (x_hi[j], x_lo[j]):
                        z = dve.memset(x[:, :, :, chunks:W].bitcast(F32), 0.0)
                z.then_inc(zeroed, 1)

                def low_w1(j):
                    dve.wait_ge(w_hi_done, j + 1)
                    if not bias_known:
                        dve.wait_ge(bias_sum, j + 1)
                    dve.tensor_tensor(w1_lo[j][:], w1_whole[j][:], w1_hi[j][:].bitcast(F32),
                                      ALU.subtract).then_inc(w_split, 1)

                def low_x(b, j, t):
                    h, q = divmod(t, KT // 2)
                    dve.wait_ge(x_hi_done[j], UNITS * b + t + 1)
                    bank = turn_bank[(UNITS * j + t) % 2]
                    out = x_lo[j][:, 2 * q:2 * q + 2, :, h * R:h * R + R]
                    dve.tensor_tensor(out, bank[:, 0:4 * R].rearrange("p (k g n) -> p k g n", k=2, g=2),
                                      x_hi[j][:, 2 * q:2 * q + 2, :, h * R:h * R + R].bitcast(F32),
                                      ALU.subtract).then_inc(x_ready[j], 1)

                def take(b, j):
                    dve.wait_ge(out_done, 2 * b + j + 1)
                    if j == 0:
                        dve.tensor_copy(kc_out[:, bass.ds(b, 1), :].rearrange("p a n -> p (a n)"),
                                        out_bank[0][:, 0:chunks]).then_inc(out_taken, 1)
                    else:
                        dve.tensor_copy(vc_out[0:R, bass.ds(b, 1), :, :].rearrange("p a t n -> p (a t n)"),
                                        out_bank[1][0:R, 0:VT * P]).then_inc(out_taken, 1)

                def sequence(b, last):
                    for t in range(UNITS):
                        low_x(b, 1, t)
                    take(b, 0)
                    if not last:
                        for t in range(UNITS):
                            low_x(b + 1, 0, t)
                    take(b, 1)

                low_w1(0)
                for t in range(UNITS):
                    low_x(0, 0, t)
                low_w1(1)
                if bias_known:
                    dve.engine_nop().then_inc(bias_done, 1)
                else:
                    dve.tensor_copy(bias[:], out_bank[0][:, 0:2 * NF]).then_inc(bias_done, 1)
                if n_seq > 1:
                    with dve.Fori(0, n_seq - 1) as b:
                        sequence(b, False)
                sequence(n_seq - 1, True)

            @block.tensor
            def _(pe):
                def bias_of(j):
                    if bias_known:
                        return
                    pe.wait_ge(w_landed[j], 16)
                    for f in range(NF):
                        for k in range(SLOTS * KT):
                            mm = pe.matmul(out_bank[0][:, NF * j + f:NF * j + f + 1],
                                           w1_whole[j][:, k, f * P:(f + 1) * P],
                                           pe_sb[:, j, k:k + 1], start=(k == 0), stop=(k == SLOTS * KT - 1))
                    mm.then_inc(bias_sum, 1)

                def turn(b, j, t):
                    h, q = divmod(t, KT // 2)
                    if q == 0:
                        pe.wait_ge(packed_done[pack_slot(j, h)], packs(b, j, h))
                    if t >= 2:
                        pe.wait_ge(x_ready[j], UNITS * b + t - 1)
                    elif j == 1:
                        pe.wait_ge(x_ready[0], UNITS * (b + 1))
                    elif type(b) is not int or b:
                        pe.wait_ge(x_ready[1], UNITS * b)
                    rows = packed[pack_slot(j, h)][0:R].rearrange("p g (k s) d -> p g k (s d)", s=2)
                    bank = turn_bank[(UNITS * j + t) % 2]
                    for k in range(2):
                        for g in range(N_KV):
                            tr = pe.transpose(bank[:, (2 * k + g) * R:(2 * k + g + 1) * R],
                                              rows[:, g, 2 * q + k, :], K["ident"][0:R, 0:R])
                    tr.then_inc(turned[j], 1)

                def hidden_of(b, j, f, turns):
                    pe.wait_ge(x_ready[j], UNITS * (b + 1))
                    if j == 1:
                        pe.wait_ge(gelu_done, 2 * NF * b + f + 1)
                    elif type(b) is not int or b:
                        pe.wait_ge(gelu_done, 2 * NF * b - NF + f + 1)
                    n = 0
                    for slot in range(SLOTS):
                        for k in range(KT):
                            w = slot * KT + k
                            mm = product3(pe, hid_bank[f][:, 0:2 * chunks],
                                          w1_hi[j][:, w, f * P:(f + 1) * P], w1_lo[j][:, w, f * P:(f + 1) * P],
                                          x_hi[j][:, k, :, slot:slot + chunks],
                                          x_lo[j][:, k, :, slot:slot + chunks],
                                          w == 0, w == SLOTS * KT - 1)
                            if w % (SLOTS * KT // max(1, UNITS // 2)) == 0 and n < len(turns):
                                turn(*turns[n])
                                n += 1
                    mm.then_inc(hid_done, 1)

                def second(b, j):
                    pe.wait_ge(gelu_done, 2 * NF * b + NF * (j + 1))
                    bank = out_bank[j]
                    if type(b) is int and b == 0:
                        if j == 0:
                            pe.wait_ge(bias_done, 1)
                    else:
                        pe.wait_ge(out_taken, 2 * b - 1 + j)
                    for g in range(N_KV):
                        if j == 0:
                            for f in range(NF):
                                mm = pe.matmul(bank[g * HD:(g + 1) * HD, 0:chunks], w2_sb[:, 0, f, :],
                                               hidden[0][:, f, g, :], start=(f == 0), stop=(f == NF - 1))
                        else:
                            for v in range(VT):
                                for f in range(NF):
                                    mm = pe.matmul(bank[0:R, v * P + g * HD:v * P + (g + 1) * HD],
                                                   hidden[1][:, f, g, v * R:(v + 1) * R], w2_sb[:, 1, f, :],
                                                   start=(f == 0), stop=(f == NF - 1))
                    mm.then_inc(out_done, 1)

                def sequence(b, last):
                    for j in range(2):
                        for f in range(NF):
                            span = range(f * UNITS // 2, (f + 1) * UNITS // 2)
                            turns = [(b, 1, t) for t in span] if j == 0 else \
                                [] if last else [(b + 1, 0, t) for t in span]
                            hidden_of(b, j, f, turns)
                        second(b, j)

                pe.wait_ge(small_landed, 32)
                bias_of(0)
                for t in range(UNITS):
                    turn(0, 0, t)
                bias_of(1)
                pe.wait_ge(small_landed, 64)
                pe.wait_ge(zeroed, 1)
                if n_seq > 1:
                    sequence(0, False)
                    if n_seq > 2:
                        with pe.Fori(1, n_seq - 1) as b:
                            sequence(b, False)
                sequence(n_seq - 1, True)


def stage_in_project(nc, mem, K, xT, gain, w_in, z, z_sample, uT, outs):
    ZG = 4
    ZN = OFF_POOL // ZG
    UG, UN = 2, POOL_WIDTH // 2
    with ExitStack() as scope:
        h_hi = mem.sb(scope, "in_h_hi", [P, KT, T], F32R)
        h_lo = mem.sb(scope, "in_h_lo", [P, KT, T], F32R)
        with ExitStack() as norm_scope:
            norm = Norm(mem, norm_scope, K, "in")
        w_hi = mem.sb(scope, "in_w_hi", [P, KT, ZN], F32R)
        w_lo = mem.sb(scope, "in_w_lo", [P, KT, ZN], F32R)
        rot = [mem.sb(scope, f"in_rot{i}", [P, TT, 4, 8]) for i in range(4)]
        w_raw = mem.sb(scope, "in_w_raw", [P, KT, ZN])
        banks = [mem.ps(scope, f"in_bank{i}") for i in range(4)]
        w_landed, w_hi_done, w_split = mem.sem("in_w_landed"), mem.sem("in_w_hi_done"), mem.sem("in_w_split")
        z_done, z_taken, u_done, u_taken = (mem.sem("in_z_done"), mem.sem("in_z_taken"),
                                            mem.sem("in_u_done"), mem.sem("in_u_taken"))
        padded, rotated, gated, out_sem = (mem.sem("in_padded"), mem.sem("in_rotated"),
                                           mem.sem("in_gated"), mem.sem("in_out"))
        rope_step = mem.sem("in_rope_step")
        w_view = w_in.rearrange("(k p) n -> p k n", p=P)

        with nc.Block() as block:
            @block.sync
            def _(sp):
                norm.load(sp, gain)
                sp.dma_start(outs["x"], xT[:]).then_inc(out_sem, 16)

                def load(i, start, n):
                    sp.wait_ge(w_split, i)
                    sp.dma_start(w_raw[:, :, 0:n], w_view[:, :, bass.ds(start, n)]).then_inc(w_landed, 16)

                with sp.Fori(0, ZG) as i:
                    load(i, ZN * i, ZN)
                for i in range(UG):
                    load(ZG + i, OFF_POOL + UN * i, UN)
                sp.wait_ge(rotated, 1)
                sp.wait_ge(z_taken, ZG * TT)
                for key, off in (("cmp", OFF_CMP), ("slc", OFF_SLC), ("win", OFF_WIN)):
                    first = 0 if key != "win" else (SEQ - WINDOW) // P
                    sp.dma_start(outs[key + "_prompt"].rearrange("(t p) n -> p t n", p=P),
                                 z[:, first:TT - 1, off:off + KV_WIDTH]).then_inc(out_sem, 16)
                    if key != "win":
                        sp.dma_start(outs[key + "_sample"], z[0:N_SAMPLE, TT - 1, off:off + KV_WIDTH]
                                     ).then_inc(out_sem, 16)
                sp.dma_start(z_sample[:], z[0:N_SAMPLE, TT - 1, :]).then_inc(out_sem, 16)
                sp.wait_ge(out_sem, 16 * 7)

            @block.scalar
            def _(act):
                norm.scalar(act, xT, h_hi)

                def high(i, n, used):
                    act.wait_ge(w_landed, 16 * i + 16)
                    used()
                    act.activation(w_hi[:, :, 0:n], w_raw[:, :, 0:n], ACT.Copy).then_inc(w_hi_done, 1)

                act.wait_ge(padded, 1)

                def z_group(i):
                    high(i, ZN, lambda: act.wait_ge(z_done, TT * i))
                    for t in range(TT):
                        act.wait_ge(z_done, TT * i + t + 1)
                        rows = slice(0, P) if t < TT - 1 else slice(P - N_SAMPLE, P)
                        n = P if t < TT - 1 else N_SAMPLE
                        act.activation(z[0:n, t, bass.ds(ZN * i, ZN)], banks[t % 4][rows, 0:ZN],
                                       ACT.Copy).then_inc(z_taken, 1)

                with act.Fori(0, ZG) as i:
                    z_group(i)
                high(ZG, UN, lambda: act.wait_ge(z_done, TT * ZG))
                act.wait_ge(z_taken, ZG * TT)
                act.activation(z[:, :, OFF_GATE:OFF_POOL], z[:, :, OFF_GATE:OFF_POOL],
                               ACT.Sigmoid).then_inc(gated, 1)
                for m in range(2 * UG):
                    if m == 2:
                        high(ZG + 1, UN, lambda: act.wait_ge(u_done, 2 * CHUNKS))
                    for c in range(CHUNKS):
                        n = CHUNKS * m + c
                        act.wait_ge(u_done, n + 1)
                        act.activation(uT[:, m, chunk(c)], banks[n % 4][:, 0:CH], ACT.Copy).then_inc(u_taken, 1)

            @block.vector
            def _(dve):
                norm.vector(dve, xT, banks[0], h_hi, h_lo)
                dve.memset(z[:, TT - 1, :], 0.0).then_inc(padded, 1)

                def low(i, n):
                    dve.wait_ge(w_hi_done, i + 1)
                    dve.tensor_tensor(w_lo[:, :, 0:n], w_raw[:, :, 0:n], w_hi[:, :, 0:n].bitcast(F32),
                                      ALU.subtract).then_inc(w_split, 1)

                with dve.Fori(0, ZG) as i:
                    low(i, ZN)
                low(ZG, UN)
                dve.wait_ge(z_taken, ZG * TT)
                step = Order(rope_step)
                for n, (off, heads) in enumerate(((0, 4), (4 * HD, 4), (OFF_CMP, 2), (OFF_SLC, 2), (OFF_WIN, 2))):
                    if n == 2:
                        low(ZG + 1, UN)
                    view = z[:, :, off:off + heads * HD].rearrange("p t (h d) -> p t h d", d=HD)
                    x1, x2 = view[:, :, :, 0:8], view[:, :, :, 8:16]
                    cos = K["cos"][:].unsqueeze(2).to_broadcast([P, TT, heads, 8])
                    sin = K["sin"][:].unsqueeze(2).to_broadcast([P, TT, heads, 8])
                    r = [x[:, :, 0:heads, :] for x in rot]
                    step.wait(dve)
                    for out, a, b in ((r[0], x1, cos), (r[1], x2, sin), (r[2], x1, sin), (r[3], x2, cos)):
                        step.did(dve.tensor_tensor(out, a, b, ALU.mult))
                    step.wait(dve)
                    step.did(dve.tensor_tensor(x1, r[0], r[1], ALU.subtract))
                    step.did(dve.tensor_tensor(x2, r[2], r[3], ALU.add))
                step.wait(dve)
                dve.engine_nop().then_inc(rotated, 1)

            @block.tensor
            def _(pe):
                norm.tensor(pe, banks[0])

                with pe.Fori(0, ZG) as i:
                    pe.wait_ge(w_split, i + 1)
                    pe.wait_ge(norm.ready, CHUNKS)
                    for t in range(TT):
                        pe.wait_ge(z_taken, TT * i + t - 3 if t > 3 else TT * i)
                        last = t == TT - 1
                        tokens = slice(T - P, T) if last else slice(t * P, (t + 1) * P)
                        for k in range(KT):
                            mm = product3(pe, banks[t % 4][:, 0:ZN], h_hi[:, k, tokens], h_lo[:, k, tokens],
                                          w_hi[:, k, :], w_lo[:, k, :], k == 0, k == KT - 1)
                        mm.then_inc(z_done, 1)
                for m in range(2 * UG):
                    if m % 2 == 0:
                        pe.wait_ge(w_split, ZG + m // 2 + 1)
                    w = slice((m % 2) * P, (m % 2) * P + P)
                    for c in range(CHUNKS):
                        n = CHUNKS * m + c
                        if n < 4:
                            pe.wait_ge(z_taken, ZG * TT)
                        else:
                            pe.wait_ge(u_taken, n - 3)
                        for k in range(KT):
                            mm = product3(pe, banks[n % 4][:, 0:CH], w_hi[:, k, w], w_lo[:, k, w],
                                          h_hi[:, k, chunk(c)], h_lo[:, k, chunk(c)], k == 0, k == KT - 1)
                        mm.then_inc(u_done, 1)


def stage_pool(nc, mem, K, uT, mix, state_pool, w_pool, pool_scale, out_prompt, out_sample):
    ROWS = POOL_STATE + N_SAMPLE
    EXT = POOL_STATE + DEC_SEQ
    with ExitStack() as scope:
        state = mem.sb(scope, "pl_state", [P, POOL_WIDTH])
        w_sb = mem.sb(scope, "pl_w", [P, 4, P])
        scale = mem.sb(scope, "pl_scale", [P, 4])
        rows = mem.sb(scope, "pl_rows", [P, POOL_WIDTH])
        prompt = [mem.sb(scope, f"pl_prompt{i}", [P, POOL_STATE + SEQ]) for i in range(3)]
        sample = [mem.sb(scope, f"pl_sample{i}", [P, DEC_BATCH, EXT]) for i in range(3)]
        diff = mem.sb(scope, "pl_diff", [P, T])
        state_bank, row_bank = mem.ps(scope, "pl_state_bank"), mem.ps(scope, "pl_row_bank")
        banks = [mem.ps(scope, f"pl_bank{i}") for i in range(CHUNKS)]
        landed, turned, rows_taken, out_sem = (mem.sem("pl_landed"), mem.sem("pl_turned"),
                                               mem.sem("pl_rows_taken"), mem.sem("pl_out"))
        dve_step, diff_ready, map_done, map_taken = (mem.sem("pl_dve_step"), mem.sem("pl_diff_ready"),
                                                     mem.sem("pl_map_done"), mem.sem("pl_map_taken"))

        with nc.Block() as block:
            @block.sync
            def _(sp):
                sp.dma_start(state[0:DEC_BATCH * POOL_STATE, :],
                             state_pool.rearrange("b s n -> (b s) n")).then_inc(landed, 16)
                sp.dma_start(w_sb[:], w_pool.rearrange("g p n -> p g n")).then_inc(landed, 16)
                sp.dma_start(scale[:], pool_scale).then_inc(landed, 16)
                sp.wait_ge(rows_taken, 1)
                sp.dma_start(out_prompt, rows[0:POOL_STATE, :]).then_inc(out_sem, 16)
                for b in range(DEC_BATCH):
                    r = POOL_STATE + b * DEC_SEQ
                    sp.dma_start(out_sample[b, POOL_STATE - DEC_SEQ:POOL_STATE, :],
                                 rows[r:r + DEC_SEQ, :]).then_inc(out_sem, 16)
                sp.wait_ge(out_sem, 16 * (1 + DEC_BATCH))

            @block.tensor
            def _(pe):
                pe.wait_ge(landed, 48)
                n = DEC_BATCH * POOL_STATE
                for g in range(4):
                    pe.transpose(state_bank[:, g * P:g * P + n], state[0:n, g * P:(g + 1) * P], K["ident"][0:n, 0:n])
                    tr = pe.transpose(row_bank[0:ROWS, g * P:(g + 1) * P], uT[:, g, T - ROWS:T], K["ident"][:])
                tr.then_inc(turned, 1)
                for g in range(4):
                    pe.wait_ge(diff_ready, g + 1)
                    if g:
                        pe.wait_ge(map_taken, CHUNKS * g)
                    for c in range(CHUNKS):
                        pe.matmul(banks[c][:, 0:CH], w_sb[:, g, :], diff[:, chunk(c)], start=True,
                                  stop=True).then_inc(map_done, 1)

            @block.scalar
            def _(act):
                act.wait_ge(turned, 1)
                act.activation(rows[0:ROWS, :], row_bank[0:ROWS, :], ACT.Copy).then_inc(rows_taken, 1)
                act.wait_ge(landed, 48)
                for g in range(4):
                    for c in range(CHUNKS):
                        act.wait_ge(map_done, CHUNKS * g + c + 1)
                        act.activation(mix[:, KT // 2 + g, chunk(c)], banks[c][:, 0:CH], ACT.Copy,
                                       scale=scale[:, g:g + 1]).then_inc(map_taken, 1)

            @block.vector
            def _(dve):
                step = Order(dve_step)
                dve.wait_ge(turned, 1)
                for g, w in enumerate(POOL_WINDOWS):
                    step.wait(dve)
                    if g == 0:
                        step.did(dve.memset(prompt[0][:, 0:POOL_STATE], 0.0))
                    step.did(dve.tensor_copy(prompt[0][:, POOL_STATE:], uT[:, g, 0:SEQ]))
                    n = DEC_BATCH * POOL_STATE
                    step.did(dve.tensor_copy(sample[0][:, :, 0:POOL_STATE],
                                             state_bank[:, g * P:g * P + n].rearrange("p (b s) -> p b s", b=DEC_BATCH)))
                    step.did(dve.tensor_copy(sample[0][:, :, POOL_STATE:],
                                             uT[:, g, SEQ:T].rearrange("p (b s) -> p b s", b=DEC_BATCH)))
                    step.wait(dve)
                    reach, at = 1, 0
                    while reach < w:
                        to = 2 if at == 1 else 1
                        lo = 2 * reach - 1
                        step.did(dve.tensor_tensor(prompt[to][:, lo:], prompt[at][:, lo:],
                                                   prompt[at][:, lo - reach:POOL_STATE + SEQ - reach], ALU.add))
                        step.did(dve.tensor_tensor(sample[to][:, :, lo:], sample[at][:, :, lo:],
                                                   sample[at][:, :, lo - reach:EXT - reach], ALU.add))
                        step.wait(dve)
                        reach, at = 2 * reach, to
                    if g:
                        dve.wait_ge(map_done, CHUNKS * g)
                    step.did(dve.scalar_tensor_tensor(diff[:, 0:SEQ], prompt[at][:, POOL_STATE:], 1.0 / w,
                                                      prompt[0][:, POOL_STATE:], ALU.mult, ALU.subtract))
                    step.did(dve.scalar_tensor_tensor(
                        diff[:, SEQ:T].rearrange("p (b s) -> p b s", b=DEC_BATCH), sample[at][:, :, POOL_STATE:],
                        1.0 / w, sample[0][:, :, POOL_STATE:], ALU.mult, ALU.subtract))
                    step.wait(dve)
                    step.did(dve.tensor_tensor(prompt[at][:, POOL_STATE:POOL_STATE + 16],
                                               prompt[at][:, POOL_STATE:POOL_STATE + 16], K["inv_count"][:, g, :], ALU.mult))
                    step.wait(dve)
                    step.did(dve.tensor_tensor(diff[:, 0:16], prompt[at][:, POOL_STATE:POOL_STATE + 16],
                                               prompt[0][:, POOL_STATE:POOL_STATE + 16], ALU.subtract))
                    step.wait(dve)
                    dve.engine_nop().then_inc(diff_ready, 1)


def stage_attend_prompt(nc, mem, K, z, kcp, vcp, mixT):
    QT = SEQ // P
    WT = WINDOW // P
    NB = SEQ // CMP_STRIDE - 1
    WIN0, CMP0 = SEQ, SEQ + (WT + 1) * P
    PW = CMP0 + 64
    LEAD = 12

    def win_tiles(qt):
        return list(range(max(0, qt - WT + 1), qt + 1)) + ([qt - WT] if qt >= WT else [])

    def value_units(qt):
        return ([(t * P, P, (0, t)) for t in range(qt + 1)]
                + [(WIN0 + i * P, P, (1, t)) for i, t in enumerate(win_tiles(qt))]
                + [(CMP0, NB, None)])

    UNITS = [len(value_units(q)) for q in range(QT)]
    PER_GROUP = LEAD + sum(UNITS)
    assert PER_GROUP % 2 == 0

    with ExitStack() as scope:
        q_rows = mem.sb(scope, "at_q_rows", [P, QT, GROUP, HD])
        k_rows = mem.sb(scope, "at_k_rows", [P, 2, QT, HD])
        values = mem.sb(scope, "at_values", [P, 2, QT, HD])
        vc_rows = mem.sb(scope, "at_vc_rows", [P, HD])
        kc = mem.sb(scope, "at_kc", [HD, N_KV, SEQ // CMP_STRIDE])
        qT = mem.sb(scope, "at_qT", [HD, GROUP, SEQ])
        kT = mem.sb(scope, "at_kT", [HD, 2, SEQ])
        probs = [mem.sb(scope, f"at_probs{i}", [P, GROUP, PW]) for i in range(2)]
        neg_max = mem.sb(scope, "at_neg_max", [P, 2, GROUP, 3])
        sums = mem.sb(scope, "at_sums", [P, 2, GROUP, 3])
        factor = mem.sb(scope, "at_factor", [P, GROUP, 3])
        turned_sb = [mem.sb(scope, f"at_turned{i}", [P, BANK]) for i in range(2)]
        slc_bank = mem.ps(scope, "at_slc_bank", (P, 2 * BANK))
        win_bank = mem.ps(scope, "at_win_bank", (P, 2 * BANK))
        turn_bank = [mem.ps(scope, f"at_turn_bank{i}") for i in range(2)]
        out_bank = [mem.ps(scope, f"at_out_bank{i}") for i in range(2)]

        kc_ready, q_copied, kv_copied = mem.sem("at_kc_ready"), mem.sem("at_q_copied"), mem.sem("at_kv_copied")
        turned, taken, pv_done = mem.sem("at_turned"), mem.sem("at_taken"), mem.sem("at_pv_done")
        scored = [mem.sem(f"at_scored{i}") for i in range(2)]
        maxed = [mem.sem(f"at_maxed{i}") for i in range(2)]
        exped = [mem.sem(f"at_exped{i}") for i in range(2)]
        p_ready, out_done, out_taken = mem.sem("at_p_ready"), mem.sem("at_out_done"), mem.sem("at_out_taken")
        dve_step = mem.sem("at_dve_step")
        STEPS = QT * 3 + 1

        def unit_base(qt):
            return LEAD + sum(UNITS[:qt])

        def quarter(qt, r):
            n = UNITS[qt]
            return range(n * r // GROUP, n * (r + 1) // GROUP)

        with nc.Block() as block:
            @block.scalar
            def _(act):
                with act.Fori(0, N_KV) as g:
                    act.wait_ge(taken, PER_GROUP * g)
                    act.wait_ge(turned, PER_GROUP * g)
                    act.activation(q_rows[:], z[:, 0:QT, bass.ds(g * GROUP * HD, GROUP * HD)].rearrange(
                        "p t (r d) -> p t r d", r=GROUP), ACT.Copy, scale=SCALE).then_inc(q_copied, 1)
                    for n in range(QT):
                        act.wait_ge(turned, PER_GROUP * g + n + 1)
                        act.activation(qT[:, :, n * P:(n + 1) * P],
                                       turn_bank[n % 2][0:HD, :].rearrange("p (r n) -> p r n", r=GROUP),
                                       ACT.Copy).then_inc(taken, 1)
                    for n in range(QT, LEAD):
                        b, half = divmod(n - QT, 2)
                        act.wait_ge(turned, PER_GROUP * g + n + 1)
                        act.activation(kT[:, b, half * BANK:(half + 1) * BANK], turn_bank[n % 2][0:HD, :],
                                       ACT.Copy).then_inc(taken, 1)
                    for qt in range(QT + 1):
                        for r in range(GROUP):
                            if qt < QT:
                                n = GROUP * qt + r
                                nm, sm, p = neg_max[:, qt % 2, r], sums[:, qt % 2, r], probs[qt % 2][:, r]
                                act.wait_ge(maxed[0], GROUP * QT * g + n + 1)
                                act.activation(p[:, 0:(qt + 1) * P], slc_bank[:, 0:(qt + 1) * P], ACT.Exp,
                                               bias=nm[:, 1:2], accum_out=sm[:, 1:2]).then_inc(exped[0], 1)
                                act.wait_ge(maxed[1], GROUP * QT * g + n + 1)
                                w = len(win_tiles(qt)) * P
                                act.activation(p[:, WIN0:WIN0 + w], win_bank[:, 0:w], ACT.Exp,
                                               bias=nm[:, 2:3], accum_out=sm[:, 2:3])
                                act.activation(p[:, CMP0:CMP0 + NB], win_bank[:, (WT + 1) * P:(WT + 1) * P + NB],
                                               ACT.Exp, bias=nm[:, 0:1],
                                               accum_out=sm[:, 0:1]).then_inc(exped[1], 1)
                            if qt > 0:
                                for u in quarter(qt - 1, r):
                                    n = unit_base(qt - 1) + u
                                    rows = value_units(qt - 1)[u][1]
                                    act.wait_ge(turned, PER_GROUP * g + n + 1)
                                    if n - LEAD >= 2:
                                        act.wait_ge(pv_done, (PER_GROUP - LEAD) * g + n - LEAD - 1)
                                    act.activation(turned_sb[n % 2][0:rows, :], turn_bank[n % 2][0:rows, :],
                                                   ACT.Copy).then_inc(taken, 1)

            @block.vector
            def _(dve):
                for g in range(N_KV):
                    k = dve.tensor_copy(kc[:, g, :], kcp[g * HD:(g + 1) * HD, :])
                k.then_inc(kc_ready, 1)
                with dve.Fori(0, N_KV) as g:
                    dve.wait_ge(turned, PER_GROUP * g)
                    dve.wait_ge(pv_done, (PER_GROUP - LEAD) * g)
                    for b, off in enumerate((OFF_SLC, OFF_WIN)):
                        dve.tensor_copy(k_rows[:, b], z[:, 0:QT, bass.ds(off + g * HD, HD)])
                        dve.tensor_copy(values[:, b], z[:, 0:QT, bass.ds(off + N_KV * HD + g * HD, HD)])
                    dve.tensor_copy(vc_rows[0:NB], vcp[0:NB, bass.ds(g * HD, HD)]).then_inc(kv_copied, 1)
                    for qt in range(QT + 1):
                        if qt < QT:
                            for r in range(GROUP):
                                n = GROUP * qt + r
                                nm = neg_max[:, qt % 2, r]
                                dve.wait_ge(scored[0], GROUP * QT * g + n + 1)
                                dve.tensor_reduce(nm[:, 1:2], slc_bank[:, 0:(qt + 1) * P], AX.X, ALU.max,
                                                  negate=True).then_inc(maxed[0], 1)
                                dve.wait_ge(scored[1], GROUP * QT * g + n + 1)
                                dve.tensor_reduce(nm[:, 2:3], win_bank[:, 0:len(win_tiles(qt)) * P], AX.X,
                                                  ALU.max, negate=True)
                                dve.tensor_reduce(nm[:, 0:1], win_bank[:, (WT + 1) * P:(WT + 1) * P + NB], AX.X,
                                                  ALU.max, negate=True).then_inc(maxed[1], 1)
                            for i in range(2):
                                dve.wait_ge(exped[i], GROUP * QT * g + GROUP * (qt + 1))
                            dve.tensor_scalar(factor[:], sums[:, qt % 2], 1e-30, None, ALU.max).then_inc(dve_step, 1)
                            dve.wait_ge(dve_step, STEPS * g + 3 * qt + (1 if qt else 0) + 1)
                            dve.reciprocal(factor[:], factor[:]).then_inc(dve_step, 1)
                            dve.wait_ge(dve_step, STEPS * g + 3 * qt + (1 if qt else 0) + 2)
                            dve.tensor_tensor(factor[:], factor[:], z[:, qt, bass.ds(OFF_GATE + g * 3 * GROUP, 3 * GROUP)]
                                              .rearrange("p (r b) -> p r b", b=3), ALU.mult).then_inc(dve_step, 1)
                            dve.wait_ge(dve_step, STEPS * g + 3 * qt + (1 if qt else 0) + 3)
                            if qt == 0:
                                dve.tensor_scalar(factor[:, :, 0:1], factor[:, :, 0:1], K["has_block"][:], None,
                                                  ALU.mult).then_inc(dve_step, 1)
                                dve.wait_ge(dve_step, STEPS * g + 4)
                            for r in range(GROUP):
                                p = probs[qt % 2][:, r]
                                w = len(win_tiles(qt)) * P
                                for b, lo, n in ((1, 0, (qt + 1) * P), (2, WIN0, w), (0, CMP0, NB)):
                                    last = dve.tensor_scalar(p[:, lo:lo + n], p[:, lo:lo + n],
                                                             factor[:, r, b:b + 1], None, ALU.mult)
                            last.then_inc(p_ready, 1)
                        if qt > 0:
                            dve.wait_ge(out_done, QT * g + qt)
                            for r in range(GROUP):
                                half = slice((r % 2) * HD, (r % 2 + 1) * HD)
                                last = dve.tensor_copy(
                                    mixT[half, bass.ds(2 * g + r // 2, 1), (qt - 1) * P:qt * P],
                                    out_bank[(qt - 1) % 2][0:HD, r * P:(r + 1) * P].unsqueeze(1))
                            last.then_inc(out_taken, 1)

            @block.tensor
            def _(pe):
                pe.wait_ge(kc_ready, 1)

                def free_turn_bank(g, n):
                    if n >= 2:
                        pe.wait_ge(taken, PER_GROUP * g + n - 1)
                    else:
                        pe.wait_ge(taken, PER_GROUP * g)
                    pe.nop(nofuse=True)

                def scores(g, qt, r):
                    n = GROUP * qt + r
                    q = qT[:, r, qt * P:(qt + 1) * P]
                    pe.wait_ge(exped[0], GROUP * QT * g + n)
                    for lo in range(0, (qt + 1) * P, BANK):
                        hi = min(lo + BANK, (qt + 1) * P)
                        diagonal = hi == (qt + 1) * P
                        mm = pe.matmul(slc_bank[:, lo:hi], q, kT[:, 0, lo:hi], start=True, stop=not diagonal)
                        if diagonal:
                            mm = pe.matmul(slc_bank[:, hi - P:hi], K["ident16"][:], K["diagonal"][:],
                                           start=False, stop=True)
                    mm.then_inc(scored[0], 1)
                    pe.wait_ge(exped[1], GROUP * QT * g + n)
                    first = max(0, qt - WT + 1)
                    w = (qt + 1 - first) * P
                    pe.matmul(win_bank[:, 0:w], q, kT[:, 1, first * P:(qt + 1) * P], start=True, stop=False)
                    pe.matmul(win_bank[:, w - P:w], K["ident16"][:], K["diagonal"][:], start=False, stop=True)
                    if qt >= WT:
                        pe.matmul(win_bank[:, BANK:BANK + P], q, kT[:, 1, (qt - WT) * P:(qt - WT + 1) * P],
                                  start=True, stop=False)
                        pe.matmul(win_bank[:, BANK:BANK + P], K["ident16"][:], K["edge"][:], start=False, stop=True)
                    c = (WT + 1) * P
                    pe.matmul(win_bank[:, c:c + NB], q, kc[:, bass.ds(g, 1), 0:NB].rearrange("p a n -> p (a n)"),
                              start=True, stop=False)
                    at = (SEQ - P) // CMP_STRIDE - qt * (P // CMP_STRIDE)
                    pe.matmul(win_bank[:, c:c + NB], K["ident16"][:], K["blocks"][:, at:at + NB], start=False,
                              stop=True).then_inc(scored[1], 1)

                def value_product(g, qt, u):
                    n = unit_base(qt) + u
                    _, rows, source = value_units(qt)[u]
                    pe.wait_ge(taken, PER_GROUP * g + n + 1)
                    if u == 0 and qt >= 2:
                        pe.wait_ge(out_taken, QT * g + qt - 1)
                    elif u == 0:
                        pe.wait_ge(out_taken, QT * g)
                    pe.nop(nofuse=True)
                    v = vc_rows[0:rows, :] if source is None else values[:, source[0], source[1], :]
                    mm = pe.matmul(out_bank[qt % 2][0:HD, :], v, turned_sb[n % 2][0:rows, :],
                                   start=(u == 0), stop=(u == UNITS[qt] - 1))
                    mm.then_inc(pv_done, 1)
                    if u == UNITS[qt] - 1:
                        pe.wait_ge(pv_done, (PER_GROUP - LEAD) * g + n - LEAD + 1)
                        pe.nop().then_inc(out_done, 1)

                with pe.Fori(0, N_KV) as g:
                    pe.wait_ge(q_copied, g + 1)
                    for n in range(QT):
                        free_turn_bank(g, n)
                        for r in range(GROUP):
                            tr = pe.transpose(turn_bank[n % 2][0:HD, r * P:(r + 1) * P], q_rows[:, n, r, :],
                                              K["ident"][:])
                        tr.then_inc(turned, 1)
                    pe.wait_ge(kv_copied, g + 1)
                    for n in range(QT, LEAD):
                        b, half = divmod(n - QT, 2)
                        free_turn_bank(g, n)
                        for i in range(4):
                            tr = pe.transpose(turn_bank[n % 2][0:HD, i * P:(i + 1) * P],
                                              k_rows[:, b, 4 * half + i, :], K["ident"][:])
                        tr.then_inc(turned, 1)
                    pe.wait_ge(taken, PER_GROUP * g + LEAD)
                    pending = None
                    for qt in range(QT + 1):
                        for r in range(GROUP):
                            if qt < QT:
                                scores(g, qt, r)
                            if qt > 0:
                                for u in quarter(qt - 1, r):
                                    lo, rows, _ = value_units(qt - 1)[u]
                                    n = unit_base(qt - 1) + u
                                    if u == 0:
                                        pe.wait_ge(p_ready, QT * g + qt)
                                    free_turn_bank(g, n)
                                    for h in range(GROUP):
                                        tr = pe.transpose(turn_bank[n % 2][0:rows, h * P:(h + 1) * P],
                                                          probs[(qt - 1) % 2][:, h, lo:lo + rows], K["ident"][:])
                                    tr.then_inc(turned, 1)
                                    if pending:
                                        value_product(g, *pending)
                                    pending = (qt - 1, u)
                    value_product(g, *pending)


def stage_attend_sample(nc, mem, K, z_s, pages, cache_slc, state_win, kc_dram, vc_dram, gates_dram, mixT):
    NP = PAST_LEN // PAGE
    HB = 2
    RQ = DEC_BATCH // HB
    ROWS = P // RQ
    NBLK = (PAST_LEN - CMP_BLOCK) // CMP_STRIDE + 1
    CB = PAST_LEN // CMP_STRIDE
    NSLC = PAST_LEN // SLC_BLOCK
    GP = BANK // P
    KG = NP // GP
    RING = 4
    WT = WINDOW // P
    NEW = N_SAMPLE
    SIDE = CB // P + WT + 1
    UNITS = SIDE + 1 + NP
    TURNS = RQ * (KG + 1)
    BPG = BANK // SLC_BLOCK
    with ExitStack() as scope:
        q_rows = mem.sb(scope, "as_q_rows", [N_SAMPLE, GROUP, N_KV, HD])
        q_diag = mem.sb(scope, "as_q_diag", [P, DEC_BATCH, N_KV, GROUP, DEC_SEQ])
        k_new = mem.sb(scope, "as_k_new", [P, 2, N_SAMPLE])
        kc = mem.sb(scope, "as_kc", [P, DEC_BATCH, CB])
        vc = mem.sb(scope, "as_vc", [P, DEC_BATCH, CB // P, P])
        state = [mem.sb(scope, f"as_state{i}", [P, RQ, WT, KV_WIDTH]) for i in range(HB)]
        gate = mem.sb(scope, "as_gate", [P, HB, 3])
        page_ring = [mem.sb(scope, f"as_pages{i}", [P, RQ, GP, KV_WIDTH]) for i in range(RING)]
        kT = [mem.sb(scope, f"as_kT{i}", [P, BANK]) for i in range(2)]
        pT = [mem.sb(scope, f"as_pT{i}", [P, P]) for i in range(2)]
        p_cmp = mem.sb(scope, "as_p_cmp", [P, CB])
        p_cmp_gated = mem.sb(scope, "as_p_cmp_gated", [P, CB])
        p_win = mem.sb(scope, "as_p_win", [P, WINDOW + NEW])
        p_new = mem.sb(scope, "as_p_new", [P, NEW])
        p_page = [mem.sb(scope, f"as_p_page{i}", [P, BANK]) for i in range(2)]
        grouped = mem.sb(scope, "as_grouped", [P, NSLC + 1, 4])
        score = [mem.sb(scope, f"as_score{i}", [P, NSLC + 1]) for i in range(2)]
        best = mem.sb(scope, "as_best", [P, 8])
        left_out = mem.sb(scope, "as_left_out", [P, NSLC])
        small = mem.sb(scope, "as_small", [P, 3, 3])
        neg_max = mem.sb(scope, "as_neg_max", [P, 4])
        group_max = mem.sb(scope, "as_group_max", [P, 1])
        shrink = mem.sb(scope, "as_shrink", [P, 4])
        group_sum = mem.sb(scope, "as_group_sum", [P, 4])
        total = mem.sb(scope, "as_total", [P, 1])
        acc = mem.sb(scope, "as_acc", [P, P])
        out_rows = mem.sb(scope, "as_out_rows", [P, P])
        kt_bank = [mem.ps(scope, f"as_kt_bank{i}") for i in range(2)]
        s_bank = [mem.ps(scope, f"as_s_bank{i}") for i in range(2)]
        c_bank = mem.ps(scope, "as_c_bank")
        pt_bank = [mem.ps(scope, f"as_pt_bank{i}") for i in range(2)]
        out_bank = mem.ps(scope, "as_out_bank")

        gates_out, landed, gate_in = mem.sem("as_gates_out"), mem.sem("as_landed"), mem.sem("as_gate_in")
        state_landed = [mem.sem(f"as_state_landed{i}") for i in range(HB)]
        pages_landed = [mem.sem(f"as_pages_landed{i}") for i in range(RING)]
        q_packed, q_turned, q_ready, kn_ready = (mem.sem("as_q_packed"), mem.sem("as_q_turned"),
                                                 mem.sem("as_q_ready"), mem.sem("as_kn_ready"))
        c_done, kt_turned, kt_taken, s_done = (mem.sem("as_c_done"), mem.sem("as_kt_turned"),
                                               mem.sem("as_kt_taken"), mem.sem("as_s_done"))
        s_group, s_added = mem.sem("as_s_group"), mem.sem("as_s_added")
        maxed, exped = mem.sem("as_maxed"), mem.sem("as_exped")
        c_normed, g_done, win_ready = mem.sem("as_c_normed"), mem.sem("as_g_done"), mem.sem("as_win_ready")
        pt_turned, pt_taken, pv_done = mem.sem("as_pt_turned"), mem.sem("as_pt_taken"), mem.sem("as_pv_done")
        pv_group, acc_done = mem.sem("as_pv_group"), mem.sem("as_acc_done")
        out_ready, out_turned, out_taken = mem.sem("as_out_ready"), mem.sem("as_out_turned"), mem.sem("as_out_taken")
        dve_step, group_maxed = mem.sem("as_dve_step"), mem.sem("as_group_maxed")
        SOFT, BANKS, SUMS = 3 + KG, 1 + KG, 1 + KG
        S_TOKEN, ACC_TOKENS, RING_TOKENS = 1, RING, 2

        with nc.Block() as block:
            @block.sync
            def _(sp):
                sp.dma_start(kc[:], kc_dram).then_inc(landed, 16)
                sp.dma_start(vc[:], vc_dram).then_inc(landed, 16)
                pages_by_request = pages[:].rearrange("o (b n) -> o b n", n=NP)
                for hb in range(HB):
                    with sp.Fori(0, KG // RING) as i:
                        for s in range(RING):
                            sp.wait_ge(acc_done, SUMS * hb + (RING + 1) * i + s + 1)
                            for pair in range(RQ // 2):
                                _, numbers = nc.values_load_multi_w_load_instructions(
                                    pages_by_request[0:1, RQ * hb + 2 * pair:RQ * hb + 2 * pair + 2,
                                                     bass.ds(GP * RING * i + GP * s, GP)],
                                    [mybir.EngineType.SP], min_val=0, max_val=cache_slc.shape[0] - 1)
                                for n, page in enumerate(numbers):
                                    sp.dma_start(page_ring[s][:, 2 * pair + n // GP, n % GP, :],
                                                 cache_slc[bass.ds(page, 1)].rearrange("a t n -> (a t) n")
                                                 ).then_inc(pages_landed[s], 16)

            @block.gpsimd
            def _(pool):
                pool.dma_start(gates_dram, z_s[:, OFF_GATE:OFF_POOL]).then_inc(gates_out, 16)
                for b in range(RQ):
                    pool.dma_start(state[0][:, b], state_win[b].rearrange("(w p) n -> p w n", p=P)
                                   ).then_inc(state_landed[0], 16)
                pool.wait_ge(gates_out, 16)
                for b in range(DEC_BATCH):
                    pool.dma_start(gate[ROWS * (b % RQ):ROWS * (b % RQ + 1), b // RQ, :],
                                   gates_dram[DEC_SEQ * b:DEC_SEQ * b + DEC_SEQ, :].rearrange("t (h c) -> h t c", c=3)
                                   ).then_inc(gate_in, 16)
                for b in range(RQ):
                    pool.dma_start(state[1][:, b], state_win[RQ + b].rearrange("(w p) n -> p w n", p=P)
                                   ).then_inc(state_landed[1], 16)

            @block.scalar
            def _(act):
                act.sem_inc(kt_taken, RING_TOKENS)
                act.sem_inc(pt_taken, RING_TOKENS)
                act.activation(q_rows[:], z_s[:, 0:NSA_WIDTH].rearrange("p (g r d) -> p r g d", g=N_KV, r=GROUP),
                               ACT.Copy, scale=SCALE).then_inc(q_packed, 1)
                act.wait_ge(q_turned, 2)
                act.activation(k_new[:], pt_bank[1][:, 0:2 * N_SAMPLE].rearrange("p (b n) -> p b n", b=2),
                               ACT.Copy).then_inc(kn_ready, 1)

                def take_kt(hb, group, b):
                    n = TURNS * hb + RQ * group + b
                    act.wait_ge(kt_turned, n + 1)
                    act.wait_ge(s_done, n + 1)
                    act.activation(kT[b % 2][:], kt_bank[b % 2][:], ACT.Copy).then_inc(kt_taken, 1)

                def take_pt(hb, n, i, rows):
                    act.wait_ge(pt_turned, UNITS * hb + n + 1)
                    act.wait_ge(pv_done, UNITS * hb + n + 1)
                    act.activation(pT[i][0:rows, :], pt_bank[i][0:rows, 0:P], ACT.Copy).then_inc(pt_taken, 1)

                for hb in range(HB):
                    act.wait_ge(maxed, SOFT * hb + 1)
                    act.activation(p_cmp[:, 0:NBLK], c_bank[:, 0:NBLK], ACT.Exp, bias=small[:, 0, 0:1],
                                   accum_out=small[:, 1, 0:1]).then_inc(exped, 1)
                    for b in range(RQ):
                        take_kt(hb, 0, b)
                    act.wait_ge(maxed, SOFT * hb + 2)
                    act.activation(p_win[:], p_win[:], ACT.Exp, bias=small[:, 0, 2:3],
                                   accum_out=small[:, 1, 2:3]).then_inc(exped, 1)
                    act.wait_ge(maxed, SOFT * hb + 3)
                    act.activation(p_new[:], p_new[:], ACT.Exp, bias=neg_max[:, 3:4],
                                   accum_out=group_sum[:, 3:4]).then_inc(exped, 1)
                    for n in range(SIDE + 1):
                        take_pt(hb, n, n % 2, P if n < SIDE - 1 else NEW)
                    with act.Fori(0, KG // RING) as i:
                        for k in range(RING + 1):
                            if k < RING:
                                g = RING * i + k
                                for b in range(RQ):
                                    take_kt(hb, g + 1, b)
                                act.wait_ge(maxed, SOFT * hb + 4 + g)
                                act.activation(p_page[k % 2][:], p_page[k % 2][:], ACT.Exp, bias=neg_max[:, k:k + 1],
                                               accum_out=group_sum[:, k:k + 1])
                                before = (k + 3) % 4
                                act.activation(shrink[:, k:k + 1], neg_max[:, before:before + 1], ACT.Exp,
                                               bias=neg_max[:, k:k + 1], scale=-1.0).then_inc(exped, 1)
                            if k > 0:
                                for j in range(GP):
                                    take_pt(hb, SIDE + 1 + GP * (RING * i + k - 1) + j, j % 2, P)

            @block.vector
            def _(dve):
                dve.sem_inc(s_added, S_TOKEN)
                dve.sem_inc(acc_done, ACC_TOKENS)
                step = Order(dve_step)
                step.did(dve.memset(q_diag[:], 0.0))
                step.did(dve.memset(grouped[:, 0, :], 0.0))
                step.did(dve.memset(p_cmp[:, NBLK:CB], 0.0))
                step.wait(dve)
                dve.wait_ge(q_turned, 1)
                for g in range(N_KV):
                    half = slice(g * HD, (g + 1) * HD)
                    qd = dve.tensor_copy(q_diag[half, :, g].rearrange("p b r t -> p r b t"),
                                         pt_bank[0][half, 0:GROUP * N_SAMPLE].rearrange(
                                             "p (r b t) -> p r b t", r=GROUP, t=DEC_SEQ))
                qd.then_inc(q_ready, 1)
                dve.wait_ge(gate_in, 16 * DEC_BATCH)

                def factor(hb, branch, exponentials, gated=True):
                    f = small[:, 2, branch:branch + 1]
                    step.did(dve.tensor_scalar(f, exponentials, 1e-30, None, ALU.max))
                    step.wait(dve)
                    step.did(dve.reciprocal(f, f))
                    step.wait(dve)
                    if gated:
                        step.did(dve.tensor_tensor(f, f, gate[:, hb, branch:branch + 1], ALU.mult))
                        step.wait(dve)
                    return f

                def accumulate(hb, g, k):
                    dve.wait_ge(pv_group, SUMS * hb + g + 2)
                    dve.wait_ge(acc_done, ACC_TOKENS + SUMS * hb + g + 1)
                    dve.scalar_tensor_tensor(total[:], total[:], shrink[:, k:k + 1], group_sum[:, k:k + 1],
                                             ALU.mult, ALU.add)
                    dve.scalar_tensor_tensor(acc[:], acc[:], shrink[:, k:k + 1], out_bank[:, 0:P],
                                             ALU.mult, ALU.add).then_inc(acc_done, 1)

                for hb in range(HB):
                    dve.wait_ge(c_done, hb + 1)
                    step.did(dve.tensor_tensor(p_win[:, WINDOW:], c_bank[:, CB + NEW:CB + 2 * NEW],
                                               K["new_mask"][:, hb, :], ALU.add))
                    step.did(dve.tensor_tensor(p_new[:], c_bank[:, CB:CB + NEW], K["new_mask"][:, hb, :], ALU.add))
                    step.wait(dve)
                    dve.tensor_reduce(small[:, 0, 0:1], c_bank[:, 0:NBLK], AX.X, ALU.max,
                                      negate=True).then_inc(maxed, 1)
                    dve.wait_ge(s_group, BANKS * hb + 1)
                    dve.tensor_tensor(p_win[:, 0:WINDOW], s_bank[1][:], K["win_mask"][:], ALU.add).then_inc(s_added, 1)
                    dve.wait_ge(s_added, S_TOKEN + BANKS * hb + 1)
                    dve.tensor_reduce(small[:, 0, 2:3], p_win[:], AX.X, ALU.max, negate=True).then_inc(maxed, 1)
                    dve.tensor_reduce(neg_max[:, 3:4], p_new[:], AX.X, ALU.max, negate=True).then_inc(maxed, 1)
                    dve.wait_ge(exped, SOFT * hb + 1)
                    f = factor(hb, 0, small[:, 1, 0:1], False)
                    dve.tensor_scalar(p_cmp[:, 0:NBLK], p_cmp[:, 0:NBLK], f, None, ALU.mult).then_inc(c_normed, 1)
                    dve.wait_ge(c_normed, hb + 1)
                    step.did(dve.tensor_scalar(p_cmp_gated[:], p_cmp[:], gate[:, hb, 0:1], None, ALU.mult))
                    dve.wait_ge(exped, SOFT * hb + 2)
                    f = factor(hb, 2, small[:, 1, 2:3])
                    dve.tensor_scalar(p_win[:], p_win[:], f, None, ALU.mult).then_inc(win_ready, 1)
                    dve.wait_ge(g_done, hb + 1)
                    step.did(dve.tensor_copy(grouped[:, 1:, :], s_bank[0][:, 0:CB].rearrange("p (j c) -> p j c", c=4)))
                    step.wait(dve)
                    now, before = grouped[:, 1:, :], grouped[:, 0:NSLC, 3]
                    sc = score[0][:, 0:NSLC]
                    step.did(dve.tensor_tensor(sc, now[:, :, 0], now[:, :, 1], ALU.add))
                    step.wait(dve)
                    step.did(dve.tensor_tensor(sc, sc, now[:, :, 2], ALU.add))
                    step.wait(dve)
                    step.did(dve.scalar_tensor_tensor(sc, now[:, :, 3], 0.5, sc, ALU.mult, ALU.add))
                    step.wait(dve)
                    step.did(dve.scalar_tensor_tensor(sc, before, 0.5, sc, ALU.mult, ALU.add))
                    step.wait(dve)
                    step.did(dve.memset(score[0][:, 0:1], 1e4))
                    step.did(dve.memset(score[0][:, NSLC - 1:NSLC + 1], 1e4))
                    step.wait(dve)
                    for i in range(2):
                        step.did(dve.max(best[:], score[i][:]))
                        step.wait(dve)
                        step.did(dve.match_replace(score[1 - i][:], best[:], score[i][:], -1.0))
                        step.wait(dve)
                    step.did(dve.tensor_scalar(left_out[:], score[0][:, 0:NSLC], 0.0, NEG, ALU.is_ge, ALU.mult))
                    dve.wait_ge(pv_group, SUMS * hb + 1)
                    dve.wait_ge(exped, SOFT * hb + 3)
                    step.did(dve.tensor_copy(total[:], group_sum[:, 3:4]))
                    step.wait(dve)
                    dve.tensor_copy(acc[:], out_bank[:, 0:P]).then_inc(acc_done, 1)
                    with dve.Fori(0, KG // RING) as i:
                        for k in range(RING + 1):
                            g = RING * i + k
                            if k < RING:
                                dve.wait_ge(s_group, BANKS * hb + g + 2)
                                mask = left_out[:, bass.ds(BPG * g, BPG)].unsqueeze(2).to_broadcast(
                                    [P, BPG, SLC_BLOCK])
                                dve.tensor_tensor(p_page[k % 2][:].rearrange("p (j n) -> p j n", j=BPG),
                                                  s_bank[k % 2][:].rearrange("p (j n) -> p j n", j=BPG),
                                                  mask, ALU.add).then_inc(s_added, 1)
                                dve.wait_ge(s_added, S_TOKEN + BANKS * hb + g + 2)
                                dve.tensor_reduce(group_max[:], p_page[k % 2][:], AX.X, ALU.max,
                                                  negate=True).then_inc(group_maxed, 1)
                                dve.wait_ge(group_maxed, KG * hb + g + 1)
                                before = (k + 3) % 4
                                dve.tensor_tensor(neg_max[:, k:k + 1], neg_max[:, before:before + 1], group_max[:],
                                                  ALU.min).then_inc(maxed, 1)
                                dve.wait_ge(maxed, SOFT * hb + 4 + g)
                            if k > 0:
                                accumulate(hb, g - 1, k - 1)
                    dve.wait_ge(acc_done, ACC_TOKENS + SUMS * (hb + 1))
                    f = factor(hb, 1, total[:])
                    dve.scalar_tensor_tensor(out_rows[:], acc[:], f, c_bank[:, 0:P], ALU.mult,
                                             ALU.add).then_inc(out_ready, 1)
                    dve.wait_ge(out_turned, hb + 1)
                    src = kt_bank[0][:, 0:P].rearrange("p (b g r t) -> p b g r t", b=RQ, g=N_KV, r=GROUP)
                    for g in range(N_KV):
                        for r in range(GROUP):
                            half = slice((r % 2) * HD, (r % 2 + 1) * HD)
                            at = SEQ + RQ * DEC_SEQ * hb
                            last = dve.tensor_copy(
                                mixT[half, 2 * g + r // 2, at:at + RQ * DEC_SEQ].rearrange("p (b t) -> p b t", t=DEC_SEQ),
                                src[g * HD:(g + 1) * HD, :, g, r, :])
                    last.then_inc(out_taken, 1)

            @block.tensor
            def _(pe):
                pe.sem_inc(s_done, RING_TOKENS)
                pe.sem_inc(pv_done, RING_TOKENS)
                pe.wait_ge(q_packed, 1)
                for r in range(GROUP):
                    tr = pe.transpose(pt_bank[0][:, r * N_SAMPLE:(r + 1) * N_SAMPLE],
                                      q_rows[:, r].rearrange("p g d -> p (g d)"), K["ident"][0:N_SAMPLE, 0:N_SAMPLE])
                tr.then_inc(q_turned, 1)
                for i, off in enumerate((OFF_SLC, OFF_WIN)):
                    tr = pe.transpose(pt_bank[1][:, i * N_SAMPLE:(i + 1) * N_SAMPLE], z_s[:, off:off + P],
                                      K["ident"][0:N_SAMPLE, 0:N_SAMPLE])
                tr.then_inc(q_turned, 1)
                pe.wait_ge(landed, 32)
                pe.wait_ge(q_ready, 1)
                pe.wait_ge(kn_ready, 1)

                def queries(b):
                    return q_diag[:, b].rearrange("p g r t -> p (g r t)")

                def turn_keys(hb, group, b, tiles):
                    n = TURNS * hb + RQ * group + b
                    pe.wait_ge(kt_taken, n + 1)
                    for j in range(GP):
                        tr = pe.transpose(kt_bank[b % 2][:, j * P:(j + 1) * P], tiles[j], K["ident"][:])
                    tr.then_inc(kt_turned, 1)

                def key_scores(hb, group, b, bank):
                    n = TURNS * hb + RQ * group + b
                    pe.wait_ge(kt_taken, n + RING_TOKENS + 1)
                    mm = pe.matmul(bank[ROWS * b:ROWS * (b + 1), :], queries(RQ * hb + b), kT[b % 2][:],
                                   start=True, stop=True)
                    mm.then_inc(s_done, 1)
                    if b == RQ - 1:
                        pe.wait_ge(s_done, n + RING_TOKENS + 1)
                        pe.nop().then_inc(s_group, 1)

                def key_group(hb, group, bank, tiles):
                    for b in range(RQ + 1):
                        if b < RQ:
                            turn_keys(hb, group, b, tiles(b))
                        if b > 0:
                            key_scores(hb, group, b - 1, bank)

                def turn_probs(hb, n, i, source, rows):
                    pe.wait_ge(pt_taken, UNITS * hb + n + 1)
                    pe.transpose(pt_bank[i][0:rows, 0:P], source, K["ident"][:]).then_inc(pt_turned, 1)

                def value_product(hb, n, i, rows, values, bank, first, last):
                    pe.wait_ge(pt_taken, UNITS * hb + n + RING_TOKENS + 1)
                    for b in range(RQ):
                        mm = pe.matmul(bank[ROWS * b:ROWS * (b + 1), 0:P], pT[i][0:rows, ROWS * b:ROWS * (b + 1)],
                                       values(b), start=first, stop=last)
                    mm.then_inc(pv_done, 1)

                for hb in range(HB):
                    if hb:
                        pe.wait_ge(out_ready, hb)
                    for b in range(RQ):
                        rows = slice(ROWS * b, ROWS * (b + 1))
                        pe.matmul(c_bank[rows, 0:NBLK], queries(RQ * hb + b), kc[:, RQ * hb + b, 0:NBLK],
                                  start=True, stop=True)
                        for i in range(2):
                            mm = pe.matmul(c_bank[rows, CB + i * NEW:CB + (i + 1) * NEW], queries(RQ * hb + b),
                                           k_new[:, i, :], start=True, stop=True)
                    mm.then_inc(c_done, 1)
                    pe.wait_ge(state_landed[hb], 16 * RQ)
                    if hb:
                        pe.wait_ge(s_added, S_TOKEN + BANKS * hb)
                        pe.wait_ge(out_taken, hb)
                    key_group(hb, 0, s_bank[1], lambda b: [state[hb][:, b, j, 0:P] for j in range(WT)])
                    pe.wait_ge(c_normed, hb + 1)
                    pe.matmul(s_bank[0][:, 0:CB], K["head_sum"][:], p_cmp[:], start=True, stop=True).then_inc(g_done, 1)
                    units = [(p_cmp_gated[:, i * P:(i + 1) * P], P, lambda b, i=i: vc[:, RQ * hb + b, i, :])
                             for i in range(CB // P)]
                    units += [(p_win[:, i * P:(i + 1) * P], P, lambda b, i=i: state[hb][:, b, i, P:2 * P])
                              for i in range(WT)]
                    units += [(p_win[:, WINDOW:], NEW, lambda b: z_s[:, OFF_WIN + P:OFF_WIN + 2 * P])]
                    units += [(p_new[:], NEW, lambda b: z_s[:, OFF_SLC + P:OFF_SLC + 2 * P])]
                    pe.wait_ge(win_ready, hb + 1)
                    for n in range(SIDE + 2):
                        if n < SIDE + 1:
                            if n == SIDE:
                                pe.wait_ge(exped, SOFT * hb + 3)
                            turn_probs(hb, n, n % 2, units[n][0], units[n][1])
                        if 0 < n <= SIDE:
                            value_product(hb, n - 1, (n - 1) % 2, units[n - 1][1], units[n - 1][2], c_bank,
                                          n == 1, n == SIDE)
                    value_product(hb, SIDE, SIDE % 2, NEW, units[SIDE][2], out_bank, True, True)
                    pe.wait_ge(pv_done, UNITS * hb + SIDE + 1 + RING_TOKENS)
                    pe.nop().then_inc(pv_group, 1)
                    with pe.Fori(0, KG // RING) as i:
                        for k in range(RING + 1):
                            g = RING * i + k
                            if k < RING:
                                pe.wait_ge(pages_landed[k], 16 * RQ * GP * (KG // RING * hb + i + 1))
                                pe.wait_ge(s_added, S_TOKEN + BANKS * hb + g)
                                if k == 0:
                                    pe.wait_ge(acc_done, ACC_TOKENS + SUMS * hb + g + 1)
                                key_group(hb, g + 1, s_bank[k % 2],
                                          lambda b, k=k: [page_ring[k][:, b, j, 0:P] for j in range(GP)])
                            if k > 0:
                                pe.wait_ge(exped, SOFT * hb + g + 3)
                                pe.wait_ge(acc_done, ACC_TOKENS + SUMS * hb + g)
                                first = SIDE + 1 + GP * (g - 1)
                                for j in range(GP + 1):
                                    if j < GP:
                                        turn_probs(hb, first + j, j % 2, p_page[(k - 1) % 2][:, j * P:(j + 1) * P], P)
                                    if j > 0:
                                        value_product(hb, first + j - 1, (j - 1) % 2, P,
                                                      lambda b, k=k, j=j: page_ring[k - 1][:, b, j - 1, P:2 * P],
                                                      out_bank, j == 1, j == GP)
                                pe.wait_ge(pv_done, UNITS * hb + first + GP + RING_TOKENS)
                                pe.nop().then_inc(pv_group, 1)
                    pe.wait_ge(out_ready, hb + 1)
                    pe.transpose(kt_bank[0][:, 0:P], out_rows[:], K["ident"][:]).then_inc(out_turned, 1)


def stage_out_project(nc, mem, K, trunk, x_saved, w_out):
    mixT = xT = trunk
    w_view = w_out.rearrange("(k p) (m n) -> p m k n", p=P, n=P)
    with ExitStack() as scope:
        mix_hi = mem.sb(scope, "op_mix_hi", [P, KT, T], F32R)
        mix_lo = mem.sb(scope, "op_mix_lo", [P, KT, T], F32R)
        w_raw = [mem.sb(scope, f"op_w_raw{i}", [P, KT, P]) for i in range(2)]
        w_hi = [mem.sb(scope, f"op_w_hi{i}", [P, KT, P], F32R) for i in range(2)]
        w_lo = [mem.sb(scope, f"op_w_lo{i}", [P, KT, P], F32R) for i in range(2)]
        banks = [mem.ps(scope, f"op_bank{i}") for i in range(4)]
        x_in, w_landed = mem.sem("op_x_in"), [mem.sem(f"op_w_landed{i}") for i in range(2)]
        mix_hi_done, mix_split = mem.sem("op_mix_hi_done"), mem.sem("op_mix_split")
        w_hi_done, w_split = mem.sem("op_w_hi_done"), mem.sem("op_w_split")
        done, added = mem.sem("op_done"), mem.sem("op_added")

        with nc.Block() as block:
            @block.sync
            def _(sp):
                for m in range(KT):
                    if m >= 2:
                        sp.wait_ge(w_split, m - 1)
                    sp.dma_start(w_raw[m % 2][:], w_view[:, m]).then_inc(w_landed[m % 2], 16)
                    if m == 2:
                        sp.wait_ge(mix_split, CHUNKS)
                        sp.dma_start(xT[:], x_saved).then_inc(x_in, 16)

            @block.scalar
            def _(act):
                def high(m):
                    act.wait_ge(w_landed[m % 2], 16 * (m // 2) + 16)
                    if m >= 2:
                        act.wait_ge(done, CHUNKS * (m - 1))
                    act.activation(w_hi[m % 2][:], w_raw[m % 2][:], ACT.Copy).then_inc(w_hi_done, 1)

                high(0)
                for c in range(CHUNKS):
                    act.activation(mix_hi[:, :, chunk(c)], mixT[:, :, chunk(c)], ACT.Copy).then_inc(mix_hi_done, 1)
                for m in range(1, KT):
                    high(m)

            @block.vector
            def _(dve):
                def low(m):
                    dve.wait_ge(w_hi_done, m + 1)
                    dve.tensor_tensor(w_lo[m % 2][:], w_raw[m % 2][:], w_hi[m % 2][:].bitcast(F32),
                                      ALU.subtract).then_inc(w_split, 1)

                low(0)
                for c in range(CHUNKS):
                    dve.wait_ge(mix_hi_done, c + 1)
                    dve.tensor_tensor(mix_lo[:, :, chunk(c)], mixT[:, :, chunk(c)],
                                      mix_hi[:, :, chunk(c)].bitcast(F32), ALU.subtract).then_inc(mix_split, 1)
                dve.wait_ge(x_in, 16)
                for m in range(KT):
                    if m + 1 < KT:
                        low(m + 1)
                    for c in range(CHUNKS):
                        n = CHUNKS * m + c
                        dve.wait_ge(done, n + 1)
                        dve.tensor_tensor(xT[:, m, chunk(c)], xT[:, m, chunk(c)], banks[n % 4][:, 0:CH],
                                          ALU.add).then_inc(added, 1)

            @block.tensor
            def _(pe):
                for m in range(KT):
                    pe.wait_ge(w_split, m + 1)
                    for c in range(CHUNKS):
                        n = CHUNKS * m + c
                        if m == 0:
                            pe.wait_ge(mix_split, c + 1)
                        if n >= 4:
                            pe.wait_ge(added, n - 3)
                        for k in range(KT):
                            mm = product3(pe, banks[n % 4][:, 0:CH], w_hi[m % 2][:, k, :], w_lo[m % 2][:, k, :],
                                          mix_hi[:, k, chunk(c)], mix_lo[:, k, chunk(c)], k == 0, k == KT - 1)
                        mm.then_inc(done, 1)


def stage_finish(nc, mem, K, xT, gain, y_prompt, y_sample, states_copied, n_states_copied):
    with ExitStack() as scope:
        h = mem.sb(scope, "fin_h", [P, KT, T])
        y = [mem.sb(scope, f"fin_y{i}", [P, D_MODEL]) for i in range(3)]
        norm = Norm(mem, scope, K, "fin", split=False)
        banks = [mem.ps(scope, f"fin_bank{i}") for i in range(4)]
        sum_bank = mem.ps(scope, "fin_sum")
        turned, taken = mem.sem("fin_turned"), mem.sem("fin_taken")
        out_sem = [mem.sem(f"fin_out{i}") for i in range(3)]

        with nc.Block() as block:
            @block.sync
            def _(sp):
                norm.load(sp, gain)
                for t in range(TT):
                    sp.wait_ge(taken, 2 * t + 2)
                    target = y_prompt[t * P:(t + 1) * P, :] if t < TT - 1 else y_sample
                    n = P if t < TT - 1 else N_SAMPLE
                    sp.dma_start(target, y[t % 3][0:n, :]).then_inc(out_sem[t % 3], 16)
                sp.wait_ge(states_copied, n_states_copied)
                for i in range(3):
                    sp.wait_ge(out_sem[i], 16 * (TT // 3))

            @block.scalar
            def _(act):
                norm.scalar(act, xT, h)
                for t in range(TT):
                    n = P if t < TT - 1 else N_SAMPLE
                    if t >= 3:
                        act.wait_ge(out_sem[t % 3], 16 * (t // 3))
                    for half in range(2):
                        u = 2 * t + half
                        act.wait_ge(turned, u + 1)
                        act.activation(y[t % 3][0:n, half * BANK:(half + 1) * BANK], banks[u % 4][0:n, :],
                                       ACT.Copy).then_inc(taken, 1)

            @block.vector
            def _(dve):
                norm.vector(dve, xT, sum_bank, h, None)

            @block.tensor
            def _(pe):
                norm.tensor(pe, sum_bank)
                for t in range(TT):
                    n = P if t < TT - 1 else N_SAMPLE
                    pe.wait_ge(norm.h_done, 2 * -(-(t * P + n) // CH))
                    for half in range(2):
                        u = 2 * t + half
                        if u >= 4:
                            pe.wait_ge(taken, u - 3)
                        for k in range(4):
                            tr = pe.transpose(banks[u % 4][0:n, k * P:(k + 1) * P],
                                              h[:, 4 * half + k, t * P:t * P + n], K["ident"][:])
                        tr.then_inc(turned, 1)


def stage_constants(nc, mem, targets, narrow=()):
    landed = mem.sem("const_landed")
    with nc.Block() as block:
        @block.sync
        def _(sp):
            for target, source in targets:
                sp.dma_start(target, source).then_inc(landed, 16)
            sp.wait_ge(landed, 16 * len(targets))

        @block.vector
        def _(dve):
            dve.wait_ge(landed, 16 * len(targets))
            for source, target in narrow:
                dve.tensor_copy(target, source)


def stage_copy(nc, mem, pairs):
    copied = mem.sem("copied")
    with nc.Block() as block:
        @block.sync
        def _(sp):
            for target, source in pairs:
                sp.dma_start(target, source).then_inc(copied, 16)
            sp.wait_ge(copied, 16 * len(pairs))


def trunk_step(nc, x_prompt, x_sample, cache_cmp, cache_slc, page_table, state_win, state_pool,
               n_ffn1, w1_gate, w1_up, w1_down, n_mix, w_in, w_cmp_k1, w_cmp_k2, pe_k, w_cmp_v1, w_cmp_v2, pe_v,
               w_pool, pool_scale, w_out, n_ffn2, w2_gate, w2_up, w2_down, n_final,
               c_ident, c_ones, c_cos, c_sin, c_inv_count, c_diagonal, c_edge, c_blocks, c_has_block, c_head_sum,
               c_new_mask, c_win_mask,
               y_prompt, y_sample, new_cmp_prompt, new_slc_prompt, new_win_prompt, new_pool_prompt,
               new_cmp_sample, new_slc_sample, new_win_sample, new_pool_sample):
    x_saved = nc.dram_tensor("x_saved", [P, KT, T], F32).ap()
    kc_saved = nc.dram_tensor("kc_saved", [P, DEC_BATCH, PAST_LEN // CMP_STRIDE], F32).ap()
    vc_saved = nc.dram_tensor("vc_saved", [P, DEC_BATCH, 2, P], F32).ap()
    gates_saved = nc.dram_tensor("gates_saved", [N_SAMPLE, 3 * N_HEADS], F32).ap()
    n_pages = PAST_LEN // PAGE
    BF16 = mybir.dt.bfloat16

    def flat(a):
        return a.rearrange("o b t c g d -> (o b t) (c g d)")

    cmp_weights = ((w_cmp_k1[0], w_cmp_v1[0]), (w_cmp_k2[0], w_cmp_v2[0]), (pe_k, pe_v))
    with ExitStack() as whole:
        mem = Mem(nc)
        K = {"ident": mem.sb(whole, "ident", [P, P]), "ones": mem.sb(whole, "ones", [P, P])}
        pages = mem.sb(whole, "pages", [1, DEC_BATCH * n_pages], I32)
        cmp_bias = mem.sb(whole, "cmp_bias", [P, 2 * CMP_HIDDEN // P])
        stage_constants(nc, mem, [(K["ident"][:], c_ident), (K["ones"][:], c_ones), (pages[:], page_table)])

        with ExitStack() as scope:
            kc = mem.sb(scope, "kc", [P, DEC_BATCH, PAST_LEN // CMP_STRIDE])
            vc = mem.sb(scope, "vc", [P, DEC_BATCH, 2, P])
            stage_compress(nc, mem, K, pages, cache_cmp[0].rearrange("a (c s) k g d -> a c (s k g d)", s=CMP_STRIDE),
                           n_pages, DEC_BATCH, PAST_LEN // CMP_STRIDE, *cmp_weights, kc, vc, "cs", cmp_bias)
            mem.end_stage()
            stage_copy(nc, mem, [(kc_saved, kc[:]), (vc_saved, vc[:])])

        trunk = mem.sb(whole, "trunk", [P, KT, T])
        win_rows = WINDOW - DEC_SEQ
        state_copies = [(new_win_sample[0, b].rearrange("t c g d -> t (c g d)")[0:win_rows, :],
                         state_win[0, b].rearrange("t c g d -> t (c g d)")[DEC_SEQ:WINDOW, :]) for b in range(DEC_BATCH)]
        state_copies.append((new_pool_sample[0, :, 0:POOL_STATE - DEC_SEQ, :], state_pool[0, :, DEC_SEQ:POOL_STATE, :]))
        states_copied = mem.lasting_sem("states_copied")
        stage_load_x(nc, mem, K, trunk, x_prompt[0], x_sample.rearrange("b t n -> (b t) n"), state_copies, states_copied)
        mem.end_stage()
        stage_ffn(nc, mem, K, trunk, n_ffn1, w1_gate[0], w1_up[0], w1_down[0], "f1")
        mem.end_stage()

        with ExitStack() as mixer:
            z_sample = mem.sb(mixer, "z_sample", [N_SAMPLE, OFF_POOL])
            with ExitStack() as scope_z:
                z = mem.sb(scope_z, "z", [P, TT, OFF_POOL])
                with ExitStack() as scope:
                    for name, shape, source in (("cos", [P, TT, 8], c_cos), ("sin", [P, TT, 8], c_sin),
                                                ("inv_count", [P, 4, 16], c_inv_count)):
                        K[name] = mem.sb(scope, name, shape)
                    stage_constants(nc, mem, [(K["cos"][:], c_cos), (K["sin"][:], c_sin),
                                              (K["inv_count"][:], c_inv_count)])
                    uT = mem.sb(scope, "uT", [P, 4, T])
                    outs = dict(cmp_prompt=flat(new_cmp_prompt), cmp_sample=flat(new_cmp_sample),
                                slc_prompt=flat(new_slc_prompt), slc_sample=flat(new_slc_sample),
                                win_prompt=flat(new_win_prompt), x=x_saved)
                    stage_in_project(nc, mem, K, trunk, n_mix, w_in[0], z, z_sample, uT, outs)
                    mem.end_stage()
                    stage_pool(nc, mem, K, uT, trunk, state_pool[0], w_pool[0], pool_scale, new_pool_prompt[0, 0],
                               new_pool_sample[0])
                    mem.end_stage()
                kcp = mem.sb(scope_z, "kcp", [P, 1, SEQ // CMP_STRIDE])
                vcp = mem.sb(scope_z, "vcp", [P, 1, 1, P])
                spare = trunk[:, 0:4, :].rearrange("p k t -> p (k t)")[:, 0:CMP_STRIDE * KV_WIDTH]
                stage_compress(nc, mem, K, None, flat(new_cmp_prompt).rearrange("(c s) n -> c (s n)", s=CMP_STRIDE),
                               0, 1, SEQ // CMP_STRIDE, *cmp_weights, kcp, vcp, "cp", cmp_bias, True, spare)
                mem.end_stage()
                with ExitStack() as scope:
                    narrow = []
                    for name, width in (("ident16", P), ("diagonal", P), ("edge", P), ("blocks", 120)):
                        K[name] = mem.sb(scope, name, [P, width], BF16)
                    K["has_block"] = mem.sb(scope, "has_block", [P, 1])
                    with ExitStack() as wide_scope:
                        wide = {name: mem.sb(wide_scope, name + "_wide", [P, width])
                                for name, width in (("diagonal", P), ("edge", P), ("blocks", 120))}
                        stage_constants(nc, mem, [(wide["diagonal"][:], c_diagonal), (wide["edge"][:], c_edge),
                                                  (wide["blocks"][:], c_blocks), (K["has_block"][:], c_has_block)],
                                        [(K["ident"][:], K["ident16"][:])]
                                        + [(wide[name][:], K[name][:]) for name in wide])
                    stage_attend_prompt(nc, mem, K, z, kcp[:, 0], vcp[:, 0, 0], trunk)
                    mem.end_stage()
            for name, shape in (("head_sum", [P, P]), ("new_mask", [P, 2, N_SAMPLE]), ("win_mask", [P, WINDOW])):
                K[name] = mem.sb(mixer, name, shape)
            new_rows = [(new_win_sample[0, b].rearrange("t c g d -> t (c g d)")[win_rows:WINDOW, :],
                         z_sample[DEC_SEQ * b:DEC_SEQ * b + DEC_SEQ, OFF_WIN:OFF_GATE]) for b in range(DEC_BATCH)]
            stage_constants(nc, mem, [(K["head_sum"][:], c_head_sum), (K["new_mask"][:], c_new_mask),
                                      (K["win_mask"][:], c_win_mask)] + new_rows)
            stage_attend_sample(nc, mem, K, z_sample, pages, cache_slc[0].rearrange("a t c g d -> a t (c g d)"),
                                state_win[0].rearrange("b t c g d -> b t (c g d)"), kc_saved, vc_saved,
                                gates_saved, trunk)
            mem.end_stage()
        stage_out_project(nc, mem, K, trunk, x_saved, w_out[0])
        mem.end_stage()
        stage_ffn(nc, mem, K, trunk, n_ffn2, w2_gate[0], w2_up[0], w2_down[0], "f2")
        mem.end_stage()
        stage_finish(nc, mem, K, trunk, n_final, y_prompt[0], y_sample.rearrange("b t n -> (b t) n"),
                     states_copied, 16 * len(state_copies))
        mem.end_stage()


_INS = ["x_prompt", "x_sample", "cache_kv_cmp", "cache_kv_slc", "page_table", "state_kv_win", "state_pool",
        "n_ffn1", "w_ffn1_gate", "w_ffn1_up", "w_ffn1_down", "n_mix", "w_in", "w_cmp_k1", "w_cmp_k2", "pe_cmp_k",
        "w_cmp_v1", "w_cmp_v2", "pe_cmp_v", "w_pool", "pool_scale", "w_out", "n_ffn2", "w_ffn2_gate", "w_ffn2_up",
        "w_ffn2_down", "n_final"]
_KV = (2, N_KV, HD)
_OUTS = [(1, SEQ, D_MODEL), (DEC_BATCH, DEC_SEQ, D_MODEL), (1, 1, SEQ, *_KV), (1, 1, SEQ, *_KV), (1, 1, WINDOW, *_KV),
         (1, 1, POOL_STATE, POOL_WIDTH), (1, DEC_BATCH, DEC_SEQ, *_KV), (1, DEC_BATCH, DEC_SEQ, *_KV),
         (1, DEC_BATCH, WINDOW, *_KV), (1, DEC_BATCH, POOL_STATE, POOL_WIDTH)]


def shape_constants():
    f32 = np.float32
    inv = np.power(f32(500000.0), -np.arange(8, dtype=f32) / f32(8)).astype(f32)
    pos = np.concatenate([np.arange(SEQ), np.tile(PAST_LEN + np.arange(DEC_SEQ), DEC_BATCH),
                          np.zeros(TT * P - T)]).astype(f32)
    ang = pos[:, None] * inv
    tiles = lambda a: np.ascontiguousarray(a.reshape(TT, P, 8).transpose(1, 0, 2))
    inv_count = np.zeros((P, 4, 16), f32)
    for g, w in enumerate(POOL_WINDOWS):
        inv_count[:, g] = 1 / np.minimum(w, np.arange(16) + 1)
    row, col = np.arange(P)[:, None], np.arange(P)[None]
    starts = np.arange(120)[None] - 56
    req, kvh, tok = row // 32, (row // 16) % 2, row % 4
    new_mask = np.zeros((P, 2, N_SAMPLE), f32)
    key = np.arange(N_SAMPLE)[None]
    for half in range(2):
        new_mask[:, half] = np.where((key // DEC_SEQ == 4 * half + req) & (key % DEC_SEQ <= tok), 0, NEG)
    return dict(
        ident=np.eye(P, dtype=f32), ones=np.ones((P, P), f32), cos=tiles(np.cos(ang)), sin=tiles(np.sin(ang)),
        inv_count=inv_count, diagonal=np.where(col <= row, 0, NEG).astype(f32),
        edge=np.where(col >= row, 0, NEG).astype(f32),
        blocks=np.where(CMP_STRIDE * starts + CMP_BLOCK - 1 <= row, 0, NEG).astype(f32),
        has_block=(row >= CMP_BLOCK - 1).astype(f32),
        head_sum=((req == req.T) & (kvh == kvh.T) & (tok == tok.T)).astype(f32),
        new_mask=new_mask, win_mask=np.where(np.arange(WINDOW)[None] >= tok, 0, NEG).astype(f32))


def kernel(**inputs):
    import concourse.bacc as bacc
    from concourse.bass_utils import run_bass_kernel_spmd

    nc = bacc.Bacc("TRN2", target_bir_lowering=False, num_devices=1)

    def columns(a):
        return np.ascontiguousarray(a.reshape(-1, P).T)

    arrays, args = {}, []
    for name in _INS:
        a = np.ascontiguousarray(inputs[name])
        if name in ("n_ffn1", "n_mix", "n_ffn2", "n_final", "pool_scale", "pe_cmp_k", "pe_cmp_v"):
            a = columns(a)
        if name == "page_table":
            a = a.reshape(1, -1)
        arrays[f"in_{name}_dram"] = a
    for name, a in shape_constants().items():
        arrays[f"const_{name}_dram"] = a
    for name, a in arrays.items():
        args.append(nc.dram_tensor(name, a.shape, mybir.dt.from_np(a.dtype), kind="ExternalInput").ap())
    for i, shape in enumerate(_OUTS):
        args.append(nc.dram_tensor(f"out_{i}_dram", shape, F32, kind="ExternalOutput").ap())
    trunk_step(nc, *args)
    r = run_bass_kernel_spmd(nc, [arrays], core_ids=[0])
    return tuple(r.results[0][f"out_{i}_dram"] for i in range(len(_OUTS)))
```

```python
from contextlib import ExitStack

import numpy as np

import concourse.bass as bass
from concourse import mybir

F32 = mybir.dt.float32
F32R = mybir.dt.float32r
I32 = mybir.dt.int32
ACT = mybir.ActivationFunctionType
ALU = mybir.AluOpType
AX = mybir.AxisListType

P = 128
BANK = 512
D_MODEL, SEQ, DEC_BATCH, DEC_SEQ = 1024, 1024, 8, 4
PAST_LEN, PAGE, WINDOW = 4096, 128, 512
N_SAMPLE = DEC_BATCH * DEC_SEQ
T = SEQ + N_SAMPLE
CHUNKS = 3
CH = T // CHUNKS
KT = D_MODEL // P
TT = SEQ // P + 1
D_FF = 2816
FT = D_FF // P
HD, N_HEADS, N_KV, GROUP = 64, 8, 2, 4
NSA_WIDTH, POOL_WIDTH, KV_WIDTH = 512, 512, 256
OFF_CMP, OFF_SLC, OFF_WIN, OFF_GATE = 512, 768, 1024, 1280
OFF_POOL = OFF_GATE + 3 * N_HEADS
IN_WIDTH = OFF_POOL + POOL_WIDTH
CMP_STRIDE, CMP_HIDDEN, CMP_BLOCK = 16, 256, 32
SLC_BLOCK = 64
POOL_WINDOWS = (2, 4, 8, 16)
POOL_STATE = 15
SCALE = HD ** -0.5
EPS = 1e-6
NEG = -1e30


class Order:

    def __init__(self, sem):
        self.sem, self.n = sem, 0

    def did(self, instruction):
        instruction.then_inc(self.sem, 1)
        self.n += 1
        return instruction

    def wait(self, engine):
        engine.wait_ge(self.sem, self.n)


class Mem:

    def __init__(self, nc):
        self.nc, self.serial, self.stage_sems = nc, 0, []

    def sem(self, name):
        self.stage_sems.append(self.lasting_sem(name))
        return self.stage_sems[-1]

    def lasting_sem(self, name):
        self.serial += 1
        return self.nc.alloc_semaphore(name=f"{name}_{self.serial}")

    def end_stage(self):
        self.nc.clear_and_free_semaphores(self.stage_sems)
        self.nc.all_engine_barrier()
        self.stage_sems = []

    def sb(self, stack, name, shape, dt=F32):
        self.serial += 1
        return stack.enter_context(self.nc.sbuf_tensor(f"{name}_{self.serial}", shape, dt))

    def ps(self, stack, name, shape=(P, BANK)):
        self.serial += 1
        return stack.enter_context(self.nc.psum_tensor(f"{name}_{self.serial}", list(shape), F32))


def product3(pe, out, w_hi, w_lo, x_hi, x_lo, first, last):
    pe.matmul(out, w_hi, x_hi, start=first, stop=False)
    pe.matmul(out, w_hi, x_lo, start=False, stop=False)
    return pe.matmul(out, w_lo, x_hi, start=False, stop=last)


def chunk(c):
    return slice(c * CH, (c + 1) * CH)


class Norm:

    def __init__(self, mem, scope, K, name, split=True, spare=None, spare_h=None):
        self.K = K
        if spare is None:
            spare = mem.sb(scope, name + "_spare", [P, (KT + 2) * CH])[:]
        if split and spare_h is None:
            spare_h = mem.sb(scope, name + "_spare_h", [P, KT * CH])[:]
        self.sq = spare[:, 0:KT * CH].rearrange("p (k n) -> p k n", k=KT)
        self.var, self.inv = spare[:, KT * CH:(KT + 1) * CH], spare[:, (KT + 1) * CH:(KT + 2) * CH]
        if split:
            self.h = spare_h[:, 0:KT * CH].rearrange("p (k n) -> p k n", k=KT)
        self.tmp = self.h[:, 0, :] if split else mem.sb(scope, name + "_tmp", [P, CH])[:]
        self.gain = mem.sb(scope, name + "_gain", [P, KT])
        self.split = split
        self.gain_in = mem.sem(name + "_gain_in")
        self.sq_done = mem.sem(name + "_sq_done")
        self.sum_done = mem.sem(name + "_sum_done")
        self.var_done = mem.sem(name + "_var_done")
        self.h_done = mem.sem(name + "_h_done")
        self.hi_done = mem.sem(name + "_hi_done")
        self.rms_done = mem.sem(name + "_rms_done")
        self.dve_step = mem.sem(name + "_dve_step")
        self.ready, self.ready_too = mem.sem(name + "_ready"), mem.sem(name + "_ready_too")

    def wait_ready(self, engine, chunks):
        engine.wait_ge(self.ready, chunks)
        engine.wait_ge(self.ready_too, chunks)

    def load(self, sp, gain):
        sp.dma_start(self.gain[:], gain).then_inc(self.gain_in, 16)

    def scalar(self, act, xT, h_hi, behind_first=None):
        def root(c):
            act.wait_ge(self.var_done, c + 1)
            if c:
                act.wait_ge(self.h_done, 2 * c)
            act.activation(self.inv, self.var, ACT.Sqrt).then_inc(self.rms_done, 1)

        def square(c):
            for k in range(0, KT, KT // 2):
                act.activation(self.sq[:, k:k + KT // 2], xT[:, k:k + KT // 2, chunk(c)],
                               ACT.Square).then_inc(self.sq_done, 1)

        square(0)
        root(0)
        for c in range(CHUNKS):
            if c + 1 < CHUNKS:
                act.wait_ge(self.sum_done, c + 1)
                square(c + 1)
            for k in range(0, KT if self.split else 0, KT // 2):
                n = 2 * c + (k > 0) + 1
                act.wait_ge(self.h_done, n)
                act.activation(h_hi[:, k:k + KT // 2, chunk(c)], self.h[:, k:k + KT // 2, :],
                               ACT.Copy).then_inc(self.hi_done, 1)
            if c == 0 and behind_first:
                behind_first()
            if c + 1 < CHUNKS:
                root(c + 1)

    def tensor(self, pe, bank, c):
        if c:
            pe.wait_ge(self.var_done, c)
        for k in range(KT):
            if k % (KT // 2) == 0:
                pe.wait_ge(self.sq_done, 2 * c + (k > 0) + 1)
            mm = pe.matmul(bank[:, 0:CH], self.K["ones"][:], self.sq[:, k, :],
                           start=(k == 0), stop=(k == KT - 1))
        mm.then_inc(self.sum_done, 1)

    def gpsimd(self, pool, h_hi, h_lo):
        part = slice(KT // 2, KT)
        for c in range(CHUNKS):
            pool.wait_ge(self.h_done, 2 * c + 2)
            pool.wait_ge(self.hi_done, 2 * c + 2)
            pool.tensor_tensor(h_lo[:, part, chunk(c)], self.h[:, part, :],
                               h_hi[:, part, chunk(c)].bitcast(F32), ALU.subtract).then_inc(self.ready_too, 1)

    def vector(self, dve, xT, bank, h_hi, h_lo, behind_first=None):
        step = Order(self.dve_step)

        def mean_square(c):
            dve.wait_ge(self.sum_done, c + 1)
            dve.tensor_scalar(self.var, bank[:, 0:CH], 1.0 / D_MODEL, EPS, ALU.mult,
                              ALU.add).then_inc(self.var_done, 1)

        def reciprocal_root(c):
            dve.wait_ge(self.var_done, c + 1)
            dve.wait_ge(self.rms_done, c + 1)
            step.did(dve.reciprocal(self.inv, self.inv))
            step.wait(dve)
            step.did(dve.tensor_tensor(self.tmp, self.inv, self.inv, ALU.mult))
            step.wait(dve)
            step.did(dve.tensor_tensor(self.tmp, self.tmp, self.var, ALU.mult))
            step.wait(dve)
            step.did(dve.tensor_scalar(self.tmp, self.tmp, -0.5, 1.5, ALU.mult, ALU.add))
            step.wait(dve)
            step.did(dve.tensor_tensor(self.inv, self.inv, self.tmp, ALU.mult))
            step.wait(dve)

        mean_square(0)
        dve.wait_ge(self.gain_in, 16)
        for c in range(CHUNKS):
            reciprocal_root(c)
            for k in range(KT):
                if self.split and c and k == KT // 2:
                    dve.wait_ge(self.ready_too, c)
                out = self.h[:, k, :] if self.split else h_hi[:, k, chunk(c)]
                last = dve.scalar_tensor_tensor(out, xT[:, k, chunk(c)], self.gain[:, k:k + 1],
                                                self.inv, ALU.mult, ALU.mult)
                if k % (KT // 2) == KT // 2 - 1:
                    last.then_inc(self.h_done, 1)
            if c + 1 < CHUNKS:
                mean_square(c + 1)
            if self.split:
                part = slice(0, KT // 2)
                dve.wait_ge(self.hi_done, 2 * c + 1)
                dve.tensor_tensor(h_lo[:, part, chunk(c)], self.h[:, part, :],
                                  h_hi[:, part, chunk(c)].bitcast(F32), ALU.subtract).then_inc(self.ready, 1)
            if c == 0 and behind_first:
                behind_first()


def stage_load_x(nc, mem, K, xT, x_prompt, x_sample):
    with ExitStack() as scope:
        x_in = mem.sb(scope, "x_in", [P, TT, D_MODEL])
        banks = [mem.ps(scope, f"xbank{i}") for i in range(4)]
        landed = [mem.sem(f"x_landed{t}") for t in range(TT)]
        turned, taken = mem.sem("x_turned"), mem.sem("x_taken")

        with nc.Block() as block:
            @block.sync
            def _(sp):
                for t in range(TT):
                    if t < TT - 1:
                        sp.dma_start(x_in[:, t, :], x_prompt[t * P:(t + 1) * P, :]).then_inc(landed[t], 16)
                    else:
                        sp.dma_start(x_in[0:N_SAMPLE, t, :], x_sample).then_inc(landed[t], 16)

            @block.tensor
            def _(pe):
                for t in range(TT):
                    n = P if t < TT - 1 else N_SAMPLE
                    pe.wait_ge(landed[t], 16)
                    for half in range(2):
                        u = 2 * t + half
                        if u >= 4:
                            pe.wait_ge(taken, u - 3)
                        for k in range(4):
                            tr = pe.transpose(banks[u % 4][:, k * P:k * P + n],
                                              x_in[0:n, t, (4 * half + k) * P:(4 * half + k + 1) * P],
                                              K["ident"][0:n, 0:n])
                        tr.then_inc(turned, 1)

            @block.vector
            def _(dve):
                for t in range(TT):
                    n = P if t < TT - 1 else N_SAMPLE
                    for half in range(2):
                        u = 2 * t + half
                        dve.wait_ge(turned, u + 1)
                        dve.tensor_copy(
                            xT[:, 4 * half:4 * half + 4, t * P:t * P + n],
                            banks[u % 4][:, :].rearrange("p (k n) -> p k n", k=4)[:, :, 0:n],
                        ).then_inc(taken, 1)


def stage_ffn(nc, mem, K, xT, gain, w_gate, w_up, w_down, name, copies=(), copied=None):
    PAIRS = FT // 2
    wg_v = w_gate.rearrange("(k p) (f n) -> p k f n", p=P, n=P)
    wu_v = w_up.rearrange("(k p) (f n) -> p k f n", p=P, n=P)
    wd_v = w_down.rearrange("(f p) n -> p f n", p=P)
    with ExitStack() as scope:
        h_hi = mem.sb(scope, name + "_h_hi", [P, KT, T], F32R)
        h_lo = mem.sb(scope, name + "_h_lo", [P, KT, T], F32R)
        with ExitStack() as norm_scope:
            norm = Norm(mem, norm_scope, K, name)
        wd_hi = mem.sb(scope, name + "_wd_hi", [P, 2, D_MODEL], F32R)
        wd_lo = mem.sb(scope, name + "_wd_lo", [P, 2, D_MODEL], F32R)
        act_up = mem.sb(scope, name + "_act_up", [P, CH])
        gu_hi, gu_lo = [None] * 2, [None] * 2
        for s in (1, 0):
            gu_hi[s] = mem.sb(scope, f"{name}_gu_hi{s}", [P, 2, KT, P], F32R)
            gu_lo[s] = mem.sb(scope, f"{name}_gu_lo{s}", [P, 2, KT, P], F32R)
        gu_raw = [mem.sb(scope, f"{name}_gu_raw{s}", [P, 2, KT, P]) for s in range(2)]
        wd_raw = mem.sb(scope, name + "_wd_raw", [P, 2, D_MODEL])
        a_hi = mem.sb(scope, name + "_a_hi", [P, 2, T], F32R)
        a_lo = mem.sb(scope, name + "_a_lo", [P, 2, T], F32R)
        act_gate = mem.sb(scope, name + "_act_gate", [P, 2, CH])
        gate_bank = [mem.ps(scope, f"{name}_gate{i}") for i in range(2)]
        up_bank = [mem.ps(scope, f"{name}_up{i}") for i in range(2)]
        down_bank = [mem.ps(scope, f"{name}_down{i}") for i in range(4)]
        sum_bank = down_bank[0]

        gu_landed = [mem.sem(f"{name}_gu_landed{s}") for s in range(2)]
        gu_hi_done = [mem.sem(f"{name}_gu_hi_done{s}") for s in range(2)]
        gu_split = [mem.sem(f"{name}_gu_split{s}") for s in range(2)]
        wd_landed, wd_hi_done = mem.sem(name + "_wd_landed"), mem.sem(name + "_wd_hi_done")
        wd_split = mem.sem(name + "_wd_split")
        gate_done, up_done = mem.sem(name + "_gate_done"), mem.sem(name + "_up_done")
        silu_done, pair_free = mem.sem(name + "_silu_done"), mem.sem(name + "_pair_free")
        a_ready, dve_step = mem.sem(name + "_a_ready"), mem.sem(name + "_dve_step2")
        down_done, down_free = mem.sem(name + "_down_done"), mem.sem(name + "_down_free")
        ONE = 1
        UNITS = 2 * CHUNKS
        DOWNS = KT * CHUNKS

        with nc.Block() as block:
            @block.gpsimd
            def _(pool):
                norm.gpsimd(pool, h_hi, h_lo)
                for target, source in copies:
                    pool.dma_start(target, source).then_inc(copied, 16)

            @block.sync
            def _(sp):
                norm.load(sp, gain)

                def load_gu(s, i, tile):
                    sp.wait_ge(gu_split[s], i + ONE)
                    sp.dma_start(gu_raw[s][:, 0], wg_v[:, :, tile, :]).then_inc(gu_landed[s], 16)
                    sp.dma_start(gu_raw[s][:, 1], wu_v[:, :, tile, :]).then_inc(gu_landed[s], 16)

                def pair(i, last):
                    load_gu(1, i, 2 * i + 1)
                    sp.wait_ge(wd_split, i + ONE)
                    sp.dma_start(wd_raw[:], wd_v[:, bass.ds(2 * i, 2), :]).then_inc(wd_landed, 16)
                    if not last:
                        load_gu(0, i + 1, 2 * i + 2)

                load_gu(0, 0, 0)
                with sp.Fori(0, PAIRS - 1) as i:
                    pair(i, False)
                pair(PAIRS - 1, True)

            @block.scalar
            def _(act):
                def high_gu(s, i, first=False):
                    act.wait_ge(gu_landed[s], 32 * i + 32)
                    if not first:
                        act.wait_ge(up_done, UNITS * i + ONE if s else UNITS * i - CHUNKS + ONE)
                    act.activation(gu_hi[s][:], gu_raw[s][:], ACT.Copy).then_inc(gu_hi_done[s], 1)

                def silu(i, s, c):
                    u = UNITS * i + CHUNKS * s + c
                    b = (CHUNKS * s + c) % 2
                    act.wait_ge(gate_done, u + 1)
                    act.wait_ge(pair_free, u + 1)
                    act.activation(act_gate[:, b, :], gate_bank[b][:, 0:CH], ACT.Silu).then_inc(silu_done, 1)

                def pair(i, last):
                    high_gu(1, i)
                    for c in range(CHUNKS):
                        silu(i, 0, c)
                    act.wait_ge(wd_landed, 16 * i + 16)
                    act.wait_ge(down_done, DOWNS * i + ONE)
                    act.activation(wd_hi[:], wd_raw[:], ACT.Copy).then_inc(wd_hi_done, 1)
                    if not last:
                        high_gu(0, i + 1)
                    for c in range(CHUNKS):
                        silu(i, 1, c)

                high_gu(0, 0, True)
                norm.scalar(act, xT, h_hi)
                norm.wait_ready(act, CHUNKS)
                with act.Fori(0, PAIRS - 1) as i:
                    pair(i, False)
                pair(PAIRS - 1, True)

            @block.vector
            def _(dve):
                dve.sem_inc(pair_free, 2)
                for done in (gu_split[0], gu_split[1], wd_split, a_ready):
                    dve.sem_inc(done, ONE)
                dve.sem_inc(down_free, 4)

                def low_gu(s, i):
                    dve.wait_ge(gu_hi_done[s], i + 1)
                    dve.tensor_tensor(gu_lo[s][:], gu_raw[s][:], gu_hi[s][:].bitcast(F32),
                                      ALU.subtract).then_inc(gu_split[s], 1)

                low_gu(0, 0)
                norm.vector(dve, xT, sum_bank, h_hi, h_lo)

                def multiply(i, s, c):
                    u = UNITS * i + CHUNKS * s + c
                    b = (CHUNKS * s + c) % 2
                    dve.wait_ge(silu_done, u + 1)
                    dve.wait_ge(up_done, u + 1 + ONE)
                    dve.wait_ge(a_ready, u + ONE)
                    dve.tensor_tensor(act_up[:], act_gate[:, b, :], up_bank[b][:, 0:CH],
                                      ALU.mult).then_inc(pair_free, 1)
                    dve.wait_ge(pair_free, u + 3)
                    dve.tensor_copy(a_hi[:, s, chunk(c)], act_up[:]).then_inc(dve_step, 1)
                    dve.wait_ge(dve_step, u + 1)
                    dve.tensor_tensor(a_lo[:, s, chunk(c)], act_up[:], a_hi[:, s, chunk(c)].bitcast(F32),
                                      ALU.subtract).then_inc(a_ready, 1)

                def pair(i, last):
                    low_gu(1, i)
                    for c in range(CHUNKS):
                        multiply(i, 0, c)
                    dve.wait_ge(wd_hi_done, i + 1)
                    dve.tensor_tensor(wd_lo[:], wd_raw[:], wd_hi[:].bitcast(F32),
                                      ALU.subtract).then_inc(wd_split, 1)
                    if not last:
                        low_gu(0, i + 1)
                    for c in range(CHUNKS):
                        multiply(i, 1, c)
                    dve.wait_ge(down_free, DOWNS * i + 4)
                    for c in range(CHUNKS):
                        for m in range(KT):
                            n = KT * c + m
                            dve.wait_ge(down_done, DOWNS * i + n + 1 + ONE)
                            dve.scalar_tensor_tensor(xT[:, m, chunk(c)], down_bank[n % 4][:, 0:CH], 0.5,
                                                     xT[:, m, chunk(c)], ALU.mult,
                                                     ALU.add).then_inc(down_free, 1)

                with dve.Fori(0, PAIRS - 1) as i:
                    pair(i, False)
                pair(PAIRS - 1, True)

            @block.tensor
            def _(pe):
                pe.sem_inc(up_done, ONE)
                pe.sem_inc(down_done, ONE)
                for c in range(CHUNKS):
                    norm.tensor(pe, sum_bank, c)

                def gate_up(i, s, c):
                    u = UNITS * i + CHUNKS * s + c
                    b = (CHUNKS * s + c) % 2
                    pe.wait_ge(pair_free, u + 1)
                    for j, (bank, done) in enumerate(((gate_bank[b], gate_done), (up_bank[b], up_done))):
                        for k in range(KT):
                            mm = product3(pe, bank[:, 0:CH], gu_hi[s][:, j, k, :], gu_lo[s][:, j, k, :],
                                          h_hi[:, k, chunk(c)], h_lo[:, k, chunk(c)], k == 0, k == KT - 1)
                        mm.then_inc(done, 1)

                def pair(i, first):
                    for s in range(2):
                        pe.wait_ge(gu_split[s], i + 1 + ONE)
                        for c in range(CHUNKS):
                            if first and s == 0:
                                norm.wait_ready(pe, c + 1)
                            gate_up(i, s, c)
                    pe.wait_ge(wd_split, i + 1 + ONE)
                    for c in range(CHUNKS):
                        pe.wait_ge(a_ready, UNITS * i + CHUNKS + c + 1 + ONE)
                        for m in range(KT):
                            n = KT * c + m
                            pe.wait_ge(down_free, DOWNS * i + n + 1)
                            for s in range(2):
                                mm = product3(pe, down_bank[n % 4][:, 0:CH],
                                              wd_hi[:, s, m * P:(m + 1) * P], wd_lo[:, s, m * P:(m + 1) * P],
                                              a_hi[:, s, chunk(c)], a_lo[:, s, chunk(c)], s == 0, s == 1)
                            mm.then_inc(down_done, 1)

                pair(0, True)
                with pe.Fori(1, PAIRS) as i:
                    pair(i, False)


def stage_compress(nc, mem, K, pages, source, n_pages_seq, n_seq, chunks, w1, w2, pe_cols,
                   kc_out, vc_out, name, bias, bias_known=False, spare=None):
    HALVES = max(1, chunks // P)
    R = min(chunks, P)
    W = chunks + 2
    SLOTS = CMP_BLOCK // CMP_STRIDE
    NF = CMP_HIDDEN // P
    UNITS = HALVES * KT // 2
    ALL = n_seq * 2
    VT = max(1, chunks // P)
    FIRST = 0
    with ExitStack() as scope:
        raw = [mem.sb(scope, f"{name}_raw{h}", [P, CMP_STRIDE * KV_WIDTH]) if h == 0 or spare is None else spare
               for h in range(2)]
        w1_hi = [mem.sb(scope, f"{name}_w1_hi{j}", [P, SLOTS * KT, CMP_HIDDEN], F32R) for j in range(2)]
        with ExitStack() as landing:
            w1_whole = [mem.sb(landing, f"{name}_w1_whole{j}", [P, SLOTS * KT, CMP_HIDDEN]) for j in range(2)]
        w1_lo = [mem.sb(scope, f"{name}_w1_lo{j}", [P, SLOTS * KT, CMP_HIDDEN], F32R) for j in range(2)]
        w2_sb = mem.sb(scope, name + "_w2", [P, 2, NF, HD])
        pe_sb = mem.sb(scope, name + "_pe", [P, 2, SLOTS * KT])
        x_hi = [mem.sb(scope, f"{name}_x_hi{j}", [P, KT, N_KV, W], F32R) for j in range(2)]
        x_lo = [mem.sb(scope, f"{name}_x_lo{j}", [P, KT, N_KV, W], F32R) for j in range(2)]
        packed = [mem.sb(scope, f"{name}_packed{i}", [P, N_KV, CMP_STRIDE, HD]) for i in range(2)]
        hidden = [mem.sb(scope, f"{name}_hidden{j}", [P, NF, N_KV, chunks]) for j in range(2)]
        turn_bank = [mem.ps(scope, f"{name}_turn{i}") for i in range(2)]
        hid_bank = [mem.ps(scope, f"{name}_hid{i}") for i in range(NF)]
        out_bank = [mem.ps(scope, f"{name}_out{i}") for i in range(2)]

        w_landed = [mem.sem(f"{name}_w_landed{j}") for j in range(2)]
        small_landed, w_hi_done = mem.sem(name + "_small_landed"), mem.sem(name + "_w_hi_done")
        w_split, bias_sum = mem.sem(name + "_w_split"), mem.sem(name + "_bias_sum")
        bias_done, zeroed = mem.sem(name + "_bias_done"), mem.sem(name + "_zeroed")
        raw_landed = [mem.sem(f"{name}_raw_landed{h}") for h in range(HALVES)]
        packed_done = [mem.sem(f"{name}_packed_done{i}") for i in range(2)]
        turned = [mem.sem(f"{name}_turned{j}") for j in range(2)]
        x_hi_done = [mem.sem(f"{name}_x_hi_done{j}") for j in range(2)]
        x_ready = [mem.sem(f"{name}_x_ready{j}") for j in range(2)]
        hid_done, gelu_done = mem.sem(name + "_hid_done"), mem.sem(name + "_gelu_done")
        out_done, out_taken = mem.sem(name + "_out_done"), mem.sem(name + "_out_taken")
        LOADS = R // 8 if pages is not None else 1


        def pack_slot(j, h):
            return (j * HALVES + h) % 2

        def packs(b, j, h):
            return 2 * b + j + 1 if HALVES == 2 else b + 1

        with nc.Block() as block:
            @block.sync
            def _(sp):
                def load_w1(j):
                    sp.dma_start(w1_whole[j][:],
                                 w1[j].rearrange("(k p) f -> p k f", p=P)).then_inc(w_landed[j], 16)

                for j in range(2):
                    sp.dma_start(pe_sb[:, j], pe_cols[j]).then_inc(small_landed, 16)
                load_w1(0)

                def load(b, again):
                    for h in range(HALVES):
                        if again:
                            sp.wait_ge(packed_done[pack_slot(1, h)], packs(b - 1, 1, h))
                        if pages is None:
                            sp.dma_start(raw[h][0:R, :], source).then_inc(raw_landed[h], 16)
                            continue
                        for q in range(LOADS):
                            if q % 8 == 0:
                                _, numbers = nc.values_load_multi_w_load_instructions(
                                    pages[0:1, bass.ds(b * n_pages_seq + LOADS * h + q, 8)],
                                    [mybir.EngineType.SP], min_val=0, max_val=source.shape[0] - 1)
                            page = numbers[q % 8]
                            sp.dma_start(raw[h][8 * q:8 * q + 8, :],
                                         source[bass.ds(page, 1)].rearrange("a c n -> (a c) n")
                                         ).then_inc(raw_landed[h], 16)

                load(0, False)
                load_w1(1)
                sp.wait_ge(small_landed, 32)
                for j in range(2):
                    sp.dma_start(w2_sb[:, j], w2[j].rearrange("(k p) n -> p k n", p=P)).then_inc(small_landed, 16)
                if n_seq > 1:
                    with sp.Fori(1, n_seq) as b:
                        load(b, True)

            @block.scalar
            def _(act):
                def high_w1(j):
                    act.wait_ge(w_landed[j], 16)
                    act.activation(w1_hi[j][:], w1_whole[j][:], ACT.Copy).then_inc(w_hi_done, 1)

                def pack(b, j, h, first=False):
                    act.wait_ge(raw_landed[h], 16 * LOADS * (b + 1))
                    if j == 1 and HALVES == 2:
                        act.wait_ge(turned[0], UNITS * b + 4 * (h + 1))
                    elif not first:
                        act.wait_ge(turned[1], UNITS * (b - 1) + 4 * (h + 1))
                    i = pack_slot(j, h)
                    rows = raw[h][0:R, :].rearrange("p (s j g d) -> p j g s d", s=CMP_STRIDE, j=2, g=N_KV)
                    act.activation(packed[i][0:R], rows[:, j], ACT.Copy).then_inc(packed_done[i], 1)

                def high_x(b, j, t):
                    h, q = divmod(t, KT // 2)
                    act.wait_ge(turned[j], UNITS * b + t + 1)
                    bank = turn_bank[(UNITS * j + t) % 2]
                    act.activation(x_hi[j][:, 2 * q:2 * q + 2, :, h * R:h * R + R],
                                   bank[:, 0:4 * R].rearrange("p (k g n) -> p k g n", k=2, g=2),
                                   ACT.Copy).then_inc(x_hi_done[j], 1)

                def gelu(b, j, f):
                    u = 2 * NF * b + NF * j + f
                    act.wait_ge(hid_done, u + 1)
                    act.activation(hidden[j][:, f], hid_bank[f][:, 0:2 * chunks].rearrange("p (g n) -> p g n", g=2),
                                   ACT.Gelu_apprx_tanh,
                                   bias=bias[:, NF * j + f:NF * j + f + 1]).then_inc(gelu_done, 1)

                def slot(highs, pack_next, gelu_now):
                    for u in highs[:len(highs) // 2]:
                        high_x(*u)
                    if pack_next is not None:
                        pack(*pack_next)
                    for u in highs[len(highs) // 2:]:
                        high_x(*u)
                    gelu(*gelu_now)

                def sequence(b, last):
                    span = [range(f * UNITS // 2, (f + 1) * UNITS // 2) for f in range(NF)]
                    slot([(b, 1, t) for t in span[0]], (b, 1, 1) if HALVES == 2 else None, (b, 0, 0))
                    slot([(b, 1, t) for t in span[1]], None if last else (b + 1, 0, 0), (b, 0, 1))
                    slot([] if last else [(b + 1, 0, t) for t in span[0]],
                         None if last else (b + 1, 0, 1), (b, 1, 0))
                    slot([] if last else [(b + 1, 0, t) for t in span[1]],
                         None if last else (b + 1, 1, 0), (b, 1, 1))

                high_w1(0)
                for h in range(HALVES):
                    pack(0, 0, h, True)
                for t in range(UNITS):
                    high_x(0, 0, t)
                pack(0, 1, 0, HALVES == 1)
                high_w1(1)
                act.wait_ge(bias_done, 1)
                if n_seq > 1:
                    with act.Fori(0, n_seq - 1) as b:
                        sequence(b, False)
                sequence(n_seq - 1, True)

            @block.vector
            def _(dve):
                for j in range(2):
                    for x in (x_hi[j], x_lo[j]):
                        z = dve.memset(x[:, :, :, chunks:W].bitcast(F32), 0.0)
                z.then_inc(zeroed, 1)

                def low_w1(j):
                    dve.wait_ge(w_hi_done, j + 1)
                    if not bias_known:
                        dve.wait_ge(bias_sum, j + 1)
                    dve.tensor_tensor(w1_lo[j][:], w1_whole[j][:], w1_hi[j][:].bitcast(F32),
                                      ALU.subtract).then_inc(w_split, 1)

                def low_x(b, j, t):
                    h, q = divmod(t, KT // 2)
                    dve.wait_ge(x_hi_done[j], UNITS * b + t + 1)
                    bank = turn_bank[(UNITS * j + t) % 2]
                    out = x_lo[j][:, 2 * q:2 * q + 2, :, h * R:h * R + R]
                    dve.tensor_tensor(out, bank[:, 0:4 * R].rearrange("p (k g n) -> p k g n", k=2, g=2),
                                      x_hi[j][:, 2 * q:2 * q + 2, :, h * R:h * R + R].bitcast(F32),
                                      ALU.subtract).then_inc(x_ready[j], 1)

                def take(b, j):
                    dve.wait_ge(out_done, 2 * b + j + 1)
                    if j == 0:
                        dve.tensor_copy(kc_out[:, bass.ds(b, 1), :].rearrange("p a n -> p (a n)"),
                                        out_bank[0][:, 0:chunks]).then_inc(out_taken, 1)
                    else:
                        dve.tensor_copy(vc_out[0:R, bass.ds(b, 1), :, :].rearrange("p a t n -> p (a t n)"),
                                        out_bank[1][0:R, 0:VT * P]).then_inc(out_taken, 1)

                def sequence(b, last):
                    for t in range(UNITS):
                        low_x(b, 1, t)
                    take(b, 0)
                    if not last:
                        for t in range(UNITS):
                            low_x(b + 1, 0, t)
                    take(b, 1)

                low_w1(0)
                for t in range(UNITS):
                    low_x(0, 0, t)
                low_w1(1)
                if bias_known:
                    dve.engine_nop().then_inc(bias_done, 1)
                else:
                    dve.tensor_copy(bias[:], out_bank[0][:, 0:2 * NF]).then_inc(bias_done, 1)
                if n_seq > 1:
                    with dve.Fori(0, n_seq - 1) as b:
                        sequence(b, False)
                sequence(n_seq - 1, True)

            @block.tensor
            def _(pe):
                def bias_of(j):
                    if bias_known:
                        return
                    pe.wait_ge(w_landed[j], 16)
                    for f in range(NF):
                        for k in range(SLOTS * KT):
                            mm = pe.matmul(out_bank[0][:, NF * j + f:NF * j + f + 1],
                                           w1_whole[j][:, k, f * P:(f + 1) * P],
                                           pe_sb[:, j, k:k + 1], start=(k == 0), stop=(k == SLOTS * KT - 1))
                    mm.then_inc(bias_sum, 1)

                def turn(b, j, t):
                    h, q = divmod(t, KT // 2)
                    if q == 0:
                        pe.wait_ge(packed_done[pack_slot(j, h)], packs(b, j, h))
                    if t >= 2:
                        pe.wait_ge(x_ready[j], UNITS * b + t - 1)
                    elif j == 1:
                        pe.wait_ge(x_ready[0], UNITS * (b + 1))
                    elif b is not FIRST:
                        pe.wait_ge(x_ready[1], UNITS * b)
                    rows = packed[pack_slot(j, h)][0:R].rearrange("p g (k s) d -> p g k (s d)", s=2)
                    bank = turn_bank[(UNITS * j + t) % 2]
                    for k in range(2):
                        for g in range(N_KV):
                            tr = pe.transpose(bank[:, (2 * k + g) * R:(2 * k + g + 1) * R],
                                              rows[:, g, 2 * q + k, :], K["ident"][0:R, 0:R])
                    tr.then_inc(turned[j], 1)

                def hidden_of(b, j, f, turns):
                    pe.wait_ge(x_ready[j], UNITS * (b + 1))
                    if j == 1:
                        pe.wait_ge(gelu_done, 2 * NF * b + f + 1)
                    elif b is not FIRST:
                        pe.wait_ge(gelu_done, 2 * NF * b - NF + f + 1)
                    n = 0
                    for slot in range(SLOTS):
                        for k in range(KT):
                            w = slot * KT + k
                            mm = product3(pe, hid_bank[f][:, 0:2 * chunks],
                                          w1_hi[j][:, w, f * P:(f + 1) * P], w1_lo[j][:, w, f * P:(f + 1) * P],
                                          x_hi[j][:, k, :, slot:slot + chunks],
                                          x_lo[j][:, k, :, slot:slot + chunks],
                                          w == 0, w == SLOTS * KT - 1)
                            if w % (SLOTS * KT // max(1, UNITS // 2)) == 0 and n < len(turns):
                                turn(*turns[n])
                                n += 1
                    mm.then_inc(hid_done, 1)

                def second(b, j):
                    pe.wait_ge(gelu_done, 2 * NF * b + NF * (j + 1))
                    bank = out_bank[j]
                    if b is FIRST:
                        if j == 0:
                            pe.wait_ge(bias_done, 1)
                    else:
                        pe.wait_ge(out_taken, 2 * b - 1 + j)
                    for g in range(N_KV):
                        if j == 0:
                            for f in range(NF):
                                mm = pe.matmul(bank[g * HD:(g + 1) * HD, 0:chunks], w2_sb[:, 0, f, :],
                                               hidden[0][:, f, g, :], start=(f == 0), stop=(f == NF - 1))
                        else:
                            for v in range(VT):
                                for f in range(NF):
                                    mm = pe.matmul(bank[0:R, v * P + g * HD:v * P + (g + 1) * HD],
                                                   hidden[1][:, f, g, v * R:(v + 1) * R], w2_sb[:, 1, f, :],
                                                   start=(f == 0), stop=(f == NF - 1))
                    mm.then_inc(out_done, 1)

                def sequence(b, last):
                    for j in range(2):
                        for f in range(NF):
                            span = range(f * UNITS // 2, (f + 1) * UNITS // 2)
                            turns = [(b, 1, t) for t in span] if j == 0 else \
                                [] if last else [(b + 1, 0, t) for t in span]
                            hidden_of(b, j, f, turns)
                        second(b, j)

                pe.wait_ge(small_landed, 32)
                bias_of(0)
                for t in range(UNITS):
                    turn(0, 0, t)
                bias_of(1)
                pe.wait_ge(small_landed, 64)
                pe.wait_ge(zeroed, 1)
                if n_seq > 1:
                    sequence(0, False)
                    if n_seq > 2:
                        with pe.Fori(1, n_seq - 1) as b:
                            sequence(b, False)
                sequence(n_seq - 1, True)


def stage_in_project(nc, mem, K, xT, gain, w_in, z, z_sample, uT, outs):
    ZG = 4
    ZN = OFF_POOL // ZG
    UG, UN = 2, POOL_WIDTH // 2
    ONE = 1
    with ExitStack() as scope:
        h_hi = mem.sb(scope, "in_h_hi", [P, KT, T], F32R)
        h_lo = mem.sb(scope, "in_h_lo", [P, KT, T], F32R)
        last_tiles = -(-KT * CH // OFF_POOL)
        norm = Norm(mem, scope, K, "in", True, uT[:].rearrange("p g t -> p (g t)"),
                    z[:, TT - last_tiles:TT, :].rearrange("p t n -> p (t n)"))
        w_hi = mem.sb(scope, "in_w_hi", [P, KT, ZN], F32R)
        w_lo = mem.sb(scope, "in_w_lo", [P, KT, ZN], F32R)
        rot = [mem.sb(scope, f"in_rot{i}", [P, TT, 4, 8]) for i in range(4)]
        w_raw = mem.sb(scope, "in_w_raw", [P, KT, ZN])
        banks = [mem.ps(scope, f"in_bank{i}") for i in range(4)]
        sum_bank = mem.ps(scope, "in_sum_bank")
        w_landed, w_hi_done, w_split = mem.sem("in_w_landed"), mem.sem("in_w_hi_done"), mem.sem("in_w_split")
        z_done, z_taken, u_done, u_taken = (mem.sem("in_z_done"), mem.sem("in_z_taken"),
                                            mem.sem("in_u_done"), mem.sem("in_u_taken"))
        padded, rotated, gated, out_sem = (mem.sem("in_padded"), mem.sem("in_rotated"),
                                           mem.sem("in_gated"), mem.sem("in_out"))
        rope_step = mem.sem("in_rope_step")
        w_view = w_in.rearrange("(k p) n -> p k n", p=P)

        with nc.Block() as block:
            @block.gpsimd
            def _(pool):
                norm.gpsimd(pool, h_hi, h_lo)

            @block.sync
            def _(sp):
                norm.load(sp, gain)

                def load(i, start, n):
                    sp.wait_ge(w_split, i + ONE)
                    sp.dma_start(w_raw[:, :, 0:n], w_view[:, :, bass.ds(start, n)]).then_inc(w_landed, 16)

                load(0, 0, ZN)
                sp.dma_start(outs["x"], xT[:]).then_inc(out_sem, 16)
                with sp.Fori(1, ZG) as i:
                    load(i, ZN * i, ZN)
                for i in range(UG):
                    load(ZG + i, OFF_POOL + UN * i, UN)
                sp.wait_ge(rotated, 1)
                sp.wait_ge(z_taken, ZG * TT + ONE)
                for key, off in (("cmp", OFF_CMP), ("slc", OFF_SLC), ("win", OFF_WIN)):
                    first = 0 if key != "win" else (SEQ - WINDOW) // P
                    sp.dma_start(outs[key + "_prompt"].rearrange("(t p) n -> p t n", p=P),
                                 z[:, first:TT - 1, off:off + KV_WIDTH]).then_inc(out_sem, 16)
                    if key != "win":
                        sp.dma_start(outs[key + "_sample"], z[0:N_SAMPLE, TT - 1, off:off + KV_WIDTH]
                                     ).then_inc(out_sem, 16)
                sp.dma_start(z_sample[:], z[0:N_SAMPLE, TT - 1, :]).then_inc(out_sem, 16)
                sp.dma_start(outs["gates"], z[0:N_SAMPLE, TT - 1, OFF_GATE:OFF_POOL]).then_inc(out_sem, 16)
                sp.wait_ge(out_sem, 16 * 8)

            @block.scalar
            def _(act):
                act.sem_inc(z_taken, ONE)

                def high(i, n, used=None):
                    act.wait_ge(w_landed, 16 * i + 16)
                    if used:
                        used()
                    act.activation(w_hi[:, :, 0:n], w_raw[:, :, 0:n], ACT.Copy).then_inc(w_hi_done, 1)

                norm.scalar(act, xT, h_hi, lambda: high(0, ZN))
                act.wait_ge(padded, 1)

                def z_group(i):
                    for t in range(TT):
                        act.wait_ge(z_done, TT * i + t + 1 + ONE)
                        rows = slice(0, P) if t < TT - 1 else slice(P - N_SAMPLE, P)
                        n = P if t < TT - 1 else N_SAMPLE
                        act.activation(z[0:n, t, bass.ds(ZN * i, ZN)], banks[t % 4][rows, 0:ZN],
                                       ACT.Copy).then_inc(z_taken, 1)

                z_group(0)
                with act.Fori(1, ZG) as i:
                    high(i, ZN, lambda: act.wait_ge(z_done, TT * i + ONE))
                    z_group(i)
                high(ZG, UN, lambda: act.wait_ge(z_done, TT * ZG + ONE))
                act.wait_ge(z_taken, ZG * TT + ONE)
                act.activation(z[:, :, OFF_GATE:OFF_POOL], z[:, :, OFF_GATE:OFF_POOL],
                               ACT.Sigmoid).then_inc(gated, 1)
                for m in range(2 * UG):
                    if m == 2:
                        high(ZG + 1, UN, lambda: act.wait_ge(u_done, 2 * CHUNKS))
                    for c in range(CHUNKS):
                        n = CHUNKS * m + c
                        act.wait_ge(u_done, n + 1)
                        act.activation(uT[:, m, chunk(c)], banks[n % 4][:, 0:CH], ACT.Copy).then_inc(u_taken, 1)

            @block.vector
            def _(dve):
                dve.sem_inc(w_split, ONE)

                def low(i, n):
                    dve.wait_ge(w_hi_done, i + 1)
                    dve.tensor_tensor(w_lo[:, :, 0:n], w_raw[:, :, 0:n], w_hi[:, :, 0:n].bitcast(F32),
                                      ALU.subtract).then_inc(w_split, 1)

                norm.vector(dve, xT, sum_bank, h_hi, h_lo, lambda: low(0, ZN))
                dve.wait_ge(norm.ready_too, CHUNKS)
                dve.memset(z[:, TT - 1, :], 0.0).then_inc(padded, 1)
                with dve.Fori(1, ZG) as i:
                    low(i, ZN)
                low(ZG, UN)
                dve.wait_ge(z_taken, ZG * TT + ONE)
                step = Order(rope_step)
                for n, (off, heads) in enumerate(((0, 4), (4 * HD, 4), (OFF_CMP, 2), (OFF_SLC, 2), (OFF_WIN, 2))):
                    if n == 2:
                        low(ZG + 1, UN)
                    view = z[:, :, off:off + heads * HD].rearrange("p t (h d) -> p t h d", d=HD)
                    x1, x2 = view[:, :, :, 0:8], view[:, :, :, 8:16]
                    cos = K["cos"][:].unsqueeze(2).to_broadcast([P, TT, heads, 8])
                    sin = K["sin"][:].unsqueeze(2).to_broadcast([P, TT, heads, 8])
                    r = [x[:, :, 0:heads, :] for x in rot]
                    step.wait(dve)
                    for out, a, b in ((r[0], x1, cos), (r[1], x2, sin), (r[2], x1, sin), (r[3], x2, cos)):
                        step.did(dve.tensor_tensor(out, a, b, ALU.mult))
                    step.wait(dve)
                    step.did(dve.tensor_tensor(x1, r[0], r[1], ALU.subtract))
                    step.did(dve.tensor_tensor(x2, r[2], r[3], ALU.add))
                step.wait(dve)
                dve.engine_nop().then_inc(rotated, 1)

            @block.tensor
            def _(pe):
                pe.sem_inc(z_done, ONE)
                for c in range(CHUNKS):
                    norm.tensor(pe, sum_bank, c)

                with pe.Fori(0, ZG) as i:
                    pe.wait_ge(w_split, i + 1 + ONE)
                    for t in range(TT):
                        norm.wait_ready(pe, -(-min((t + 1) * P, T) // CH))
                        pe.wait_ge(z_taken, TT * i + max(0, t - 3) + ONE)
                        last = t == TT - 1
                        tokens = slice(T - P, T) if last else slice(t * P, (t + 1) * P)
                        for k in range(KT):
                            mm = product3(pe, banks[t % 4][:, 0:ZN], h_hi[:, k, tokens], h_lo[:, k, tokens],
                                          w_hi[:, k, :], w_lo[:, k, :], k == 0, k == KT - 1)
                        mm.then_inc(z_done, 1)
                for m in range(2 * UG):
                    if m % 2 == 0:
                        pe.wait_ge(w_split, ZG + m // 2 + 1 + ONE)
                    w = slice((m % 2) * P, (m % 2) * P + P)
                    for c in range(CHUNKS):
                        n = CHUNKS * m + c
                        if n < 4:
                            pe.wait_ge(z_taken, ZG * TT + ONE)
                        else:
                            pe.wait_ge(u_taken, n - 3)
                        for k in range(KT):
                            mm = product3(pe, banks[n % 4][:, 0:CH], w_hi[:, k, w], w_lo[:, k, w],
                                          h_hi[:, k, chunk(c)], h_lo[:, k, chunk(c)], k == 0, k == KT - 1)
                        mm.then_inc(u_done, 1)


def stage_pool(nc, mem, K, uT, mix, state_pool, w_pool, pool_scale, out_prompt, out_sample):
    ROWS = POOL_STATE + N_SAMPLE
    EXT = POOL_STATE + DEC_SEQ
    with ExitStack() as scope:
        state = mem.sb(scope, "pl_state", [P, POOL_WIDTH])
        w_sb = mem.sb(scope, "pl_w", [P, 4, P])
        scale = mem.sb(scope, "pl_scale", [P, 4])
        rows = mem.sb(scope, "pl_rows", [P, POOL_WIDTH])
        prompt = [mem.sb(scope, f"pl_prompt{i}", [P, POOL_STATE + SEQ]) for i in range(3)]
        sample = [mem.sb(scope, f"pl_sample{i}", [P, DEC_BATCH, EXT]) for i in range(3)]
        diff = mem.sb(scope, "pl_diff", [P, T])
        state_bank, row_bank = mem.ps(scope, "pl_state_bank"), mem.ps(scope, "pl_row_bank")
        banks = [mem.ps(scope, f"pl_bank{i}") for i in range(CHUNKS)]
        landed, turned, rows_taken, out_sem = (mem.sem("pl_landed"), mem.sem("pl_turned"),
                                               mem.sem("pl_rows_taken"), mem.sem("pl_out"))
        dve_step, diff_ready, map_done, map_taken = (mem.sem("pl_dve_step"), mem.sem("pl_diff_ready"),
                                                     mem.sem("pl_map_done"), mem.sem("pl_map_taken"))

        with nc.Block() as block:
            @block.sync
            def _(sp):
                sp.dma_start(state[0:DEC_BATCH * POOL_STATE, :],
                             state_pool.rearrange("b s n -> (b s) n")).then_inc(landed, 16)
                sp.dma_start(w_sb[:], w_pool.rearrange("g p n -> p g n")).then_inc(landed, 16)
                sp.dma_start(scale[:], pool_scale).then_inc(landed, 16)
                sp.wait_ge(rows_taken, 1)
                sp.dma_start(out_prompt, rows[0:POOL_STATE, :]).then_inc(out_sem, 16)
                for b in range(DEC_BATCH):
                    r = POOL_STATE + b * DEC_SEQ
                    sp.dma_start(out_sample[b, POOL_STATE - DEC_SEQ:POOL_STATE, :],
                                 rows[r:r + DEC_SEQ, :]).then_inc(out_sem, 16)
                sp.wait_ge(out_sem, 16 * (1 + DEC_BATCH))

            @block.tensor
            def _(pe):
                pe.wait_ge(landed, 48)
                n = DEC_BATCH * POOL_STATE
                for g in range(4):
                    pe.transpose(state_bank[:, g * P:g * P + n], state[0:n, g * P:(g + 1) * P], K["ident"][0:n, 0:n])
                    tr = pe.transpose(row_bank[0:ROWS, g * P:(g + 1) * P], uT[:, g, T - ROWS:T], K["ident"][:])
                tr.then_inc(turned, 1)
                for g in range(4):
                    pe.wait_ge(diff_ready, g + 1)
                    if g:
                        pe.wait_ge(map_taken, CHUNKS * g)
                    for c in range(CHUNKS):
                        pe.matmul(banks[c][:, 0:CH], w_sb[:, g, :], diff[:, chunk(c)], start=True,
                                  stop=True).then_inc(map_done, 1)

            @block.scalar
            def _(act):
                act.wait_ge(turned, 1)
                act.activation(rows[0:ROWS, :], row_bank[0:ROWS, :], ACT.Copy).then_inc(rows_taken, 1)
                act.wait_ge(landed, 48)
                for g in range(4):
                    for c in range(CHUNKS):
                        act.wait_ge(map_done, CHUNKS * g + c + 1)
                        act.activation(mix[:, KT // 2 + g, chunk(c)], banks[c][:, 0:CH], ACT.Copy,
                                       scale=scale[:, g:g + 1]).then_inc(map_taken, 1)

            @block.vector
            def _(dve):
                step = Order(dve_step)
                dve.wait_ge(turned, 1)
                for g, w in enumerate(POOL_WINDOWS):
                    step.wait(dve)
                    if g == 0:
                        step.did(dve.memset(prompt[0][:, 0:POOL_STATE], 0.0))
                    step.did(dve.tensor_copy(prompt[0][:, POOL_STATE:], uT[:, g, 0:SEQ]))
                    n = DEC_BATCH * POOL_STATE
                    step.did(dve.tensor_copy(sample[0][:, :, 0:POOL_STATE],
                                             state_bank[:, g * P:g * P + n].rearrange("p (b s) -> p b s", b=DEC_BATCH)))
                    step.did(dve.tensor_copy(sample[0][:, :, POOL_STATE:],
                                             uT[:, g, SEQ:T].rearrange("p (b s) -> p b s", b=DEC_BATCH)))
                    step.wait(dve)
                    reach, at = 1, 0
                    while reach < w:
                        to = 2 if at == 1 else 1
                        lo = 2 * reach - 1
                        step.did(dve.tensor_tensor(prompt[to][:, lo:], prompt[at][:, lo:],
                                                   prompt[at][:, lo - reach:POOL_STATE + SEQ - reach], ALU.add))
                        step.did(dve.tensor_tensor(sample[to][:, :, lo:], sample[at][:, :, lo:],
                                                   sample[at][:, :, lo - reach:EXT - reach], ALU.add))
                        step.wait(dve)
                        reach, at = 2 * reach, to
                    if g:
                        dve.wait_ge(map_done, CHUNKS * g)
                    step.did(dve.scalar_tensor_tensor(diff[:, 0:SEQ], prompt[at][:, POOL_STATE:], 1.0 / w,
                                                      prompt[0][:, POOL_STATE:], ALU.mult, ALU.subtract))
                    step.did(dve.scalar_tensor_tensor(
                        diff[:, SEQ:T].rearrange("p (b s) -> p b s", b=DEC_BATCH), sample[at][:, :, POOL_STATE:],
                        1.0 / w, sample[0][:, :, POOL_STATE:], ALU.mult, ALU.subtract))
                    step.wait(dve)
                    step.did(dve.tensor_tensor(prompt[at][:, POOL_STATE:POOL_STATE + 16],
                                               prompt[at][:, POOL_STATE:POOL_STATE + 16], K["inv_count"][:, g, :], ALU.mult))
                    step.wait(dve)
                    step.did(dve.tensor_tensor(diff[:, 0:16], prompt[at][:, POOL_STATE:POOL_STATE + 16],
                                               prompt[0][:, POOL_STATE:POOL_STATE + 16], ALU.subtract))
                    step.wait(dve)
                    dve.engine_nop().then_inc(diff_ready, 1)


def stage_attend_prompt(nc, mem, K, z, kcp, vcp, mixT):
    QT = SEQ // P
    WT = WINDOW // P
    NB = SEQ // CMP_STRIDE
    WIN0, CMP0 = SEQ, SEQ + (WT + 1) * P
    PW = CMP0 + NB
    CMP, SLC, WIN = 0, 1, 2
    HEADS = QT * GROUP
    PAIR = 2

    def win_tiles(qt):
        return list(range(max(0, qt - WT + 1), qt + 1)) + ([qt - WT] if qt >= WT else [])

    def value_units(qt):
        return ([(SLC, t * P, P, (0, t)) for t in range(qt + 1)]
                + [(WIN, WIN0 + i * P, P, (1, t)) for i, t in enumerate(win_tiles(qt))]
                + [(CMP, CMP0, NB, None)])

    def quarter(qt, r):
        n = len(value_units(qt))
        return range(n * r // GROUP, n * (r + 1) // GROUP)

    LEAD = [("k", b, half) for b in range(2) for half in range(2)] + [("q", 0)]

    def turns(qt, r):
        return ([("q", qt + 1)] if r == 2 and qt + 1 < QT else []) + \
            ([("v", qt - 1, u) for u in quarter(qt - 1, r)] if qt > 0 else [])

    def steps(qt, r, before_selected, before_window):
        x = turns(qt, r)
        selected, window = (["selected"], ["window"]) if qt < QT else ([], [])
        return x[:before_selected] + selected + x[before_selected:before_window] + window + x[before_window:]

    order = LEAD + [x for qt in range(QT + 1) for r in range(GROUP) for x in turns(qt, r)]
    at = {x: n for n, x in enumerate(order)}
    dups = {x: n for n, x in enumerate([x for x in order if x[0] != "v"])}
    products = {x: n for n, x in enumerate([x for x in order if x[0] == "v"])}
    TURNS, DUPS, PRODUCTS = len(order), len(dups), len(products)
    assert TURNS % 2 == 0 and DUPS % 2 == 0 and PRODUCTS % 2 == 0
    ONE, RING = 1, 2
    PE_ORDER, ACT_ORDER, DVE_ORDER = (0, 0), (1, 2), (0, 0)

    with ExitStack() as scope:
        dup = [mem.sb(scope, f"at_dup{i}", [P, 4, 2, HD]) for i in range(2)]
        v_split = mem.sb(scope, "at_v_split", [P, 2, QT, 2, HD], F32R)
        vc_split = mem.sb(scope, "at_vc_split", [P, 2, HD], F32R)
        kc_dup = mem.sb(scope, "at_kc_dup", [P, N_KV, NB])
        kc_hi = mem.sb(scope, "at_kc_hi", [P, N_KV, NB], F32R)
        kc_lo = mem.sb(scope, "at_kc_lo", [P, N_KV, NB], F32R)
        q_split = mem.sb(scope, "at_q_split", [P, 2, GROUP, P], F32R)
        kT_hi = mem.sb(scope, "at_kT_hi", [P, 2, SEQ], F32R)
        kT_lo = mem.sb(scope, "at_kT_lo", [P, 2, SEQ], F32R)
        probs = [mem.sb(scope, f"at_probs{i}", [P, GROUP, PW]) for i in range(2)]
        diag = mem.sb(scope, "at_diag", [P, 2, GROUP, 3, P])
        neg_max = mem.sb(scope, "at_neg_max", [P, 2, GROUP, 3])
        sums = mem.sb(scope, "at_sums", [P, 2, GROUP, 3])
        factor = mem.sb(scope, "at_factor", [P, 2, GROUP, 3])
        turned_hi = [mem.sb(scope, f"at_turned_hi{i}", [P, BANK], F32R) for i in range(2)]
        turned_lo = [mem.sb(scope, f"at_turned_lo{i}", [P, BANK], F32R) for i in range(2)]
        upper = mem.sb(scope, "at_upper", [HD, BANK])
        slc_bank = mem.ps(scope, "at_slc_bank", (P, 2 * BANK))
        win_bank = mem.ps(scope, "at_win_bank", (P, 2 * BANK))
        turn_bank = [mem.ps(scope, f"at_turn_bank{i}") for i in range(2)]
        out_bank = [mem.ps(scope, f"at_out_bank{i}") for i in range(2)]

        kc_step, kc_ready = mem.sem("at_kc_step"), mem.sem("at_kc_ready")
        dup_ready, turned, hi_done, split = (mem.sem("at_dup_ready"), mem.sem("at_turned"),
                                             mem.sem("at_hi_done"), mem.sem("at_split"))
        v_hi_done, v_ready, pv_done = mem.sem("at_v_hi_done"), mem.sem("at_v_ready"), mem.sem("at_pv_done")
        scored = [mem.sem(f"at_scored{i}") for i in range(2)]
        maxed = [mem.sem(f"at_maxed{i}") for i in range(2)]
        exped = [mem.sem(f"at_exped{i}") for i in range(2)]
        factor_ready, diag_ready = mem.sem("at_factor_ready"), mem.sem("at_diag_ready")
        out_done, upper_done, out_taken = mem.sem("at_out_done"), mem.sem("at_upper_done"), mem.sem("at_out_taken")
        dve_step = mem.sem("at_dve_step")
        STEPS = 2 * 2 * QT + 2

        with nc.Block() as block:
            @block.gpsimd
            def _(pool):
                pool.sem_inc(diag_ready, ONE)

                def duplicate(g, x):
                    m = dups[x]
                    before = TURNS * g + ONE
                    if m >= 2:
                        before += at[[y for y in dups if dups[y] == m - 2][0]] + 1
                    pool.wait_ge(turned, before)
                    if x[0] == "k":
                        off = (OFF_SLC, OFF_WIN)[x[1]]
                        rows = z[:, 4 * x[2]:4 * x[2] + 4, bass.ds(off + g * HD, HD)]
                    else:
                        rows = z[:, x[1], bass.ds(g * GROUP * HD, GROUP * HD)].rearrange("p (r d) -> p r d", r=GROUP)
                    pool.tensor_copy(dup[m % 2][:], rows.unsqueeze(2).to_broadcast([P, 4, 2, HD])).then_inc(dup_ready, 1)

                def diagonals(g, qt, pair):
                    pool.wait_ge(factor_ready, 2 * QT * g + 2 * qt + pair + 1)
                    if qt >= 2:
                        last = ("v", qt - 2, len(value_units(qt - 2)) - 1)
                        pool.wait_ge(turned, TURNS * g + at[last] + 1 + ONE)
                    heads = slice(PAIR * pair, PAIR * pair + PAIR)
                    f = factor[:, qt % 2, heads, :]
                    pool.tensor_tensor(diag[:, qt % 2, heads].rearrange("p r b n -> p (r b) n"),
                                       K["ident"][:].unsqueeze(1).to_broadcast([P, 3 * PAIR, P]),
                                       f.rearrange("p r b -> p (r b)").unsqueeze(2).to_broadcast([P, 3 * PAIR, P]),
                                       ALU.mult).then_inc(diag_ready, 1)

                with pool.Fori(0, N_KV) as g:
                    for x in LEAD:
                        duplicate(g, x)
                    for qt in range(QT):
                        if qt + 1 < QT:
                            duplicate(g, ("q", qt + 1))
                        for pair in range(2):
                            diagonals(g, qt, pair)

            @block.scalar
            def _(act):
                for i in range(2):
                    act.sem_inc(exped[i], ONE)

                def high(g, x):
                    n = TURNS * g + at[x]
                    bank = turn_bank[at[x] % 2]
                    act.wait_ge(turned, n + 1 + ONE)
                    if x[0] == "k":
                        act.activation(kT_hi[:, x[1], x[2] * BANK:(x[2] + 1) * BANK], bank[:],
                                       ACT.Copy).then_inc(hi_done, 1)
                    elif x[0] == "q":
                        act.activation(q_split[:, x[1] % 2], bank[:].rearrange("p (r n) -> p r n", r=GROUP),
                                       ACT.Copy, scale=SCALE).then_inc(hi_done, 1)
                    else:
                        v, rows = products[x], value_units(x[1])[x[2]][2]
                        act.wait_ge(pv_done, PRODUCTS * g + v - 1 + RING)
                        act.activation(turned_hi[v % 2][0:rows, :], bank[0:rows, :], ACT.Copy).then_inc(hi_done, 1)

                def take_upper(g, t):
                    act.wait_ge(out_done, QT * g + t + 1)
                    act.wait_ge(out_taken, QT * g + t + ONE)
                    act.activation(upper[:], out_bank[t % 2][HD:2 * HD, :], ACT.Copy).then_inc(upper_done, 1)

                with act.Fori(0, N_KV) as g:
                    for x in LEAD:
                        high(g, x)
                    act.wait_ge(pv_done, PRODUCTS * g + RING)
                    for b, off in enumerate((OFF_SLC, OFF_WIN)):
                        act.activation(v_split[:, b, :, 0, :], z[:, 0:QT, bass.ds(off + N_KV * HD + g * HD, HD)], ACT.Copy)
                    act.activation(vc_split[0:NB, 0, :], vcp[0:NB, bass.ds(g * HD, HD)],
                                   ACT.Copy).then_inc(v_hi_done, 1)
                    for qt in range(QT + 1):
                        for r in range(GROUP):
                            if r == 1 and qt >= 2:
                                take_upper(g, qt - 2)
                            n = GROUP * qt + r
                            nm, sm, p = neg_max[:, qt % 2, r], sums[:, qt % 2, r], probs[qt % 2][:, r]
                            for x in steps(qt, r, *ACT_ORDER):
                                if x == "selected":
                                    act.wait_ge(maxed[0], HEADS * g + n + 1)
                                    act.activation(p[:, 0:(qt + 1) * P], slc_bank[:, 0:(qt + 1) * P], ACT.Exp,
                                                   bias=nm[:, SLC:SLC + 1], accum_out=sm[:, SLC:SLC + 1]
                                                   ).then_inc(exped[0], 1)
                                elif x == "window":
                                    act.wait_ge(maxed[1], HEADS * g + n + 1)
                                    w = len(win_tiles(qt)) * P
                                    act.activation(p[:, WIN0:WIN0 + w], win_bank[:, 0:w], ACT.Exp,
                                                   bias=nm[:, WIN:WIN + 1], accum_out=sm[:, WIN:WIN + 1])
                                    act.activation(p[:, CMP0:CMP0 + NB], win_bank[:, (WT + 1) * P:(WT + 1) * P + NB],
                                                   ACT.Exp, bias=nm[:, CMP:CMP + 1],
                                                   accum_out=sm[:, CMP:CMP + 1]).then_inc(exped[1], 1)
                                else:
                                    high(g, x)
                    take_upper(g, QT - 1)

            @block.vector
            def _(dve):
                dve.sem_inc(split, RING)
                dve.sem_inc(out_taken, ONE)
                for g in range(N_KV):
                    for half in range(2):
                        k = dve.tensor_copy(kc_dup[half * HD:(half + 1) * HD, g, :], kcp[g * HD:(g + 1) * HD, :])
                k.then_inc(kc_step, 1)
                dve.wait_ge(kc_step, 1)
                dve.tensor_copy(kc_hi[:], kc_dup[:]).then_inc(kc_step, 1)
                dve.wait_ge(kc_step, 2)
                dve.tensor_tensor(kc_lo[:], kc_dup[:], kc_hi[:].bitcast(F32), ALU.subtract).then_inc(kc_ready, 1)

                def low(g, x):
                    bank = turn_bank[at[x] % 2]
                    dve.wait_ge(hi_done, TURNS * g + at[x] + 1)
                    if x[0] == "k":
                        out = (slice(None), x[1], slice(x[2] * BANK, (x[2] + 1) * BANK))
                        last = dve.tensor_tensor(kT_lo[out], bank[:], kT_hi[out].bitcast(F32), ALU.subtract)
                    elif x[0] == "q":
                        low_half = q_split[HD:2 * HD, x[1] % 2]
                        last = dve.scalar_tensor_tensor(
                            low_half, bank[HD:2 * HD, :].rearrange("p (r n) -> p r n", r=GROUP), SCALE,
                            low_half.bitcast(F32), ALU.mult, ALU.subtract)
                    else:
                        v, rows = products[x], value_units(x[1])[x[2]][2]
                        last = dve.tensor_tensor(turned_lo[v % 2][0:rows, :], bank[0:rows, :],
                                                 turned_hi[v % 2][0:rows, :].bitcast(F32), ALU.subtract)
                    last.then_inc(split, 1)

                def factors(g, qt, pair):
                    for i in range(2):
                        dve.wait_ge(exped[i], HEADS * g + GROUP * qt + PAIR * (pair + 1) + ONE)
                    if qt >= 2:
                        dve.wait_ge(diag_ready, 2 * QT * g + 2 * (qt - 2) + pair + 1 + ONE)
                    else:
                        dve.wait_ge(diag_ready, 2 * QT * g + ONE)
                    heads = slice(PAIR * pair, PAIR * pair + PAIR)
                    f = factor[:, qt % 2, heads, :]
                    s0 = STEPS * g + (4 * qt + 2 * pair + 2 if qt else 3 * pair)
                    dve.tensor_scalar(f, sums[:, qt % 2, heads, :], 1e-30, None, ALU.max).then_inc(dve_step, 1)
                    dve.wait_ge(dve_step, s0 + 1)
                    dve.reciprocal(f, f).then_inc(dve_step, 1)
                    dve.wait_ge(dve_step, s0 + 2)
                    if qt == 0:
                        dve.tensor_scalar(f[:, :, CMP:CMP + 1], f[:, :, CMP:CMP + 1], K["has_block"][:], None,
                                          ALU.mult).then_inc(dve_step, 1)
                        dve.wait_ge(dve_step, s0 + 3)
                    dve.tensor_tensor(f, f, z[:, qt, bass.ds(OFF_GATE + g * 3 * GROUP + 3 * PAIR * pair, 3 * PAIR)]
                                      .rearrange("p (r b) -> p r b", b=3), ALU.mult).then_inc(factor_ready, 1)

                def take(g, t):
                    dve.wait_ge(upper_done, QT * g + t + 1)
                    for r in range(GROUP):
                        half = slice((r % 2) * HD, (r % 2 + 1) * HD)
                        cols = slice(r * P, (r + 1) * P)
                        last = dve.tensor_tensor(mixT[half, bass.ds(2 * g + r // 2, 1), t * P:(t + 1) * P],
                                                 out_bank[t % 2][0:HD, cols].unsqueeze(1), upper[:, cols].unsqueeze(1),
                                                 ALU.add)
                    last.then_inc(out_taken, 1)

                with dve.Fori(0, N_KV) as g:
                    for x in LEAD:
                        low(g, x)
                    dve.wait_ge(v_hi_done, g + 1)
                    for b, off in enumerate((OFF_SLC, OFF_WIN)):
                        dve.tensor_tensor(v_split[:, b, :, 1, :], z[:, 0:QT, bass.ds(off + N_KV * HD + g * HD, HD)],
                                          v_split[:, b, :, 0, :].bitcast(F32), ALU.subtract)
                    dve.tensor_tensor(vc_split[0:NB, 1, :], vcp[0:NB, bass.ds(g * HD, HD)],
                                      vc_split[0:NB, 0, :].bitcast(F32), ALU.subtract).then_inc(v_ready, 1)
                    for qt in range(QT + 1):
                        for r in range(GROUP):
                            if r == 1 and qt >= 2:
                                take(g, qt - 2)
                            n = GROUP * qt + r
                            nm = neg_max[:, qt % 2, r]
                            for x in steps(qt, r, *DVE_ORDER):
                                if x == "selected":
                                    dve.wait_ge(scored[0], HEADS * g + n + 1)
                                    dve.tensor_reduce(nm[:, SLC:SLC + 1], slc_bank[:, 0:(qt + 1) * P], AX.X, ALU.max,
                                                      negate=True).then_inc(maxed[0], 1)
                                elif x == "window":
                                    dve.wait_ge(scored[1], HEADS * g + n + 1)
                                    dve.tensor_reduce(nm[:, WIN:WIN + 1], win_bank[:, 0:len(win_tiles(qt)) * P], AX.X,
                                                      ALU.max, negate=True)
                                    dve.tensor_reduce(nm[:, CMP:CMP + 1], win_bank[:, (WT + 1) * P:(WT + 1) * P + NB],
                                                      AX.X, ALU.max, negate=True).then_inc(maxed[1], 1)
                                else:
                                    low(g, x)
                            if qt < QT and r >= 2:
                                factors(g, qt, r - 2)
                    take(g, QT - 1)

            @block.tensor
            def _(pe):
                pe.sem_inc(turned, ONE)
                pe.sem_inc(pv_done, RING)
                pe.wait_ge(kc_ready, 1)

                def turn(g, x):
                    n = TURNS * g + at[x]
                    bank = turn_bank[at[x] % 2]
                    pe.wait_ge(split, n - 1 + RING)
                    if x[0] == "v":
                        _, qt, u = x
                        branch, lo, rows, _ = value_units(qt)[u]
                        if u == 0:
                            pe.wait_ge(diag_ready, 2 * QT * g + 2 * (qt + 1) + ONE)
                        pe.nop(nofuse=True)
                        for h in range(GROUP):
                            tr = pe.matmul(bank[0:rows, h * P:(h + 1) * P], probs[qt % 2][:, h, lo:lo + rows],
                                           diag[:, qt % 2, h, branch, :], start=True, stop=True)
                    else:
                        pe.wait_ge(dup_ready, DUPS * g + dups[x] + 1)
                        pe.nop(nofuse=True)
                        for i in range(4):
                            tr = pe.transpose(bank[:, i * P:(i + 1) * P],
                                              dup[dups[x] % 2][:, i].rearrange("p c d -> p (c d)"), K["ident"][:])
                    tr.then_inc(turned, 1)

                def two_pass(out, q, keys_hi, keys_lo, last):
                    pe.matmul(out, q, keys_hi, start=True, stop=False)
                    return pe.matmul(out, q, keys_lo, start=False, stop=last)

                def selected_scores(g, qt, r):
                    n = GROUP * qt + r
                    q = q_split[:, qt % 2, r, :]
                    if r == 0:
                        pe.wait_ge(split, TURNS * g + at[("q", qt)] + 1 + RING)
                    pe.wait_ge(exped[0], HEADS * g + n + ONE)
                    pe.nop(nofuse=True)
                    for lo in range(0, (qt + 1) * P, BANK):
                        hi = min(lo + BANK, (qt + 1) * P)
                        diagonal = hi == (qt + 1) * P
                        mm = two_pass(slc_bank[:, lo:hi], q, kT_hi[:, 0, lo:hi], kT_lo[:, 0, lo:hi], not diagonal)
                        if diagonal:
                            mm = pe.matmul(slc_bank[:, hi - P:hi], K["ident16"][:], K["diagonal"][:],
                                           start=False, stop=True)
                    mm.then_inc(scored[0], 1)

                def window_scores(g, qt, r):
                    n = GROUP * qt + r
                    q = q_split[:, qt % 2, r, :]
                    pe.wait_ge(exped[1], HEADS * g + n + ONE)
                    pe.nop(nofuse=True)
                    keys = slice(max(0, qt - WT + 1) * P, (qt + 1) * P)
                    w = keys.stop - keys.start
                    two_pass(win_bank[:, 0:w], q, kT_hi[:, 1, keys], kT_lo[:, 1, keys], False)
                    pe.matmul(win_bank[:, w - P:w], K["ident16"][:], K["diagonal"][:], start=False, stop=True)
                    if qt >= WT:
                        keys = slice((qt - WT) * P, (qt - WT + 1) * P)
                        two_pass(win_bank[:, BANK:BANK + P], q, kT_hi[:, 1, keys], kT_lo[:, 1, keys], False)
                        pe.matmul(win_bank[:, BANK:BANK + P], K["ident16"][:], K["edge"][:], start=False, stop=True)
                    c = (WT + 1) * P
                    two_pass(win_bank[:, c:c + NB], q,
                             kc_hi[:, bass.ds(g, 1), :].rearrange("p a n -> p (a n)"),
                             kc_lo[:, bass.ds(g, 1), :].rearrange("p a n -> p (a n)"), False)
                    first = (SEQ - P) // CMP_STRIDE - qt * (P // CMP_STRIDE)
                    pe.matmul(win_bank[:, c:c + NB], K["ident16"][:], K["blocks"][:, first:first + NB], start=False,
                              stop=True).then_inc(scored[1], 1)

                def value_product(g, x):
                    _, qt, u = x
                    v = products[x]
                    _, _, rows, source = value_units(qt)[u]
                    pe.wait_ge(split, TURNS * g + at[x] + 1 + RING)
                    if v == 0:
                        pe.wait_ge(v_ready, g + 1)
                    if u == 0:
                        pe.wait_ge(out_taken, QT * g + max(0, qt - 1) + ONE)
                    pe.nop(nofuse=True)
                    values = (vc_split[0:rows] if source is None else v_split[:, source[0], source[1]]
                              ).rearrange("p c d -> p (c d)")
                    last = u == len(value_units(qt)) - 1
                    pe.matmul(out_bank[qt % 2][:], values, turned_hi[v % 2][0:rows, :], start=(u == 0), stop=False)
                    pe.matmul(out_bank[qt % 2][:], values, turned_lo[v % 2][0:rows, :], start=False,
                              stop=last).then_inc(pv_done, 1)
                    if last:
                        pe.wait_ge(pv_done, PRODUCTS * g + v + 1 + RING)
                        pe.nop().then_inc(out_done, 1)

                with pe.Fori(0, N_KV) as g:
                    for x in LEAD:
                        turn(g, x)
                    pending = None
                    for qt in range(QT + 1):
                        for r in range(GROUP):
                            for x in steps(qt, r, *PE_ORDER):
                                if x == "selected":
                                    selected_scores(g, qt, r)
                                    continue
                                if x == "window":
                                    window_scores(g, qt, r)
                                    continue
                                turn(g, x)
                                if x[0] == "v":
                                    if pending:
                                        value_product(g, pending)
                                    pending = x
                    value_product(g, pending)


def stage_attend_sample(nc, mem, K, z_s, pages, cache_slc, state_win, kc_dram, vc_dram, gates_dram, mixT):
    NP = PAST_LEN // PAGE
    HB = 2
    RQ = DEC_BATCH // HB
    ROWS = P // RQ
    NBLK = (PAST_LEN - CMP_BLOCK) // CMP_STRIDE + 1
    CB = PAST_LEN // CMP_STRIDE
    NSLC = PAST_LEN // SLC_BLOCK
    GP = BANK // P
    KG = NP // GP
    RING = 4
    WT = WINDOW // P
    NEW = N_SAMPLE
    SIDE = CB // P + WT + 1
    UNITS = SIDE + 1 + KG
    TURNS = RQ * (KG + 1)
    BPG = BANK // SLC_BLOCK
    with ExitStack() as scope:
        q_rows = mem.sb(scope, "as_q_rows", [N_SAMPLE, GROUP, N_KV, HD])
        q_diag = mem.sb(scope, "as_q_diag", [P, DEC_BATCH, N_KV, GROUP, DEC_SEQ])
        k_new = mem.sb(scope, "as_k_new", [P, 2, N_SAMPLE])
        kc = mem.sb(scope, "as_kc", [P, DEC_BATCH, CB])
        vc = mem.sb(scope, "as_vc", [P, DEC_BATCH, CB // P, P])
        state = [mem.sb(scope, f"as_state{i}", [P, RQ, WT, KV_WIDTH]) for i in range(HB)]
        gate = mem.sb(scope, "as_gate", [P, HB, 3])
        page_ring = [mem.sb(scope, f"as_pages{i}", [P, RQ, GP, KV_WIDTH]) for i in range(RING)]
        kT = [mem.sb(scope, f"as_kT{i}", [P, BANK]) for i in range(2)]
        pT = [mem.sb(scope, f"as_pT{i}", [P, BANK]) for i in range(2)]
        p_cmp = mem.sb(scope, "as_p_cmp", [P, CB])
        p_cmp_gated = mem.sb(scope, "as_p_cmp_gated", [P, CB])
        p_win = mem.sb(scope, "as_p_win", [P, WINDOW + NEW])
        p_new = mem.sb(scope, "as_p_new", [P, NEW])
        p_page = [mem.sb(scope, f"as_p_page{i}", [P, BANK]) for i in range(2)]
        grouped = mem.sb(scope, "as_grouped", [P, NSLC + 1, 4])
        score = [mem.sb(scope, f"as_score{i}", [P, NSLC + 1]) for i in range(2)]
        best = mem.sb(scope, "as_best", [P, 8])
        left_out = mem.sb(scope, "as_left_out", [P, NSLC])
        small = mem.sb(scope, "as_small", [P, 3, 3])
        neg_max = mem.sb(scope, "as_neg_max", [P, 4])
        group_max = mem.sb(scope, "as_group_max", [P, 1])
        shrink = mem.sb(scope, "as_shrink", [P, 4])
        group_sum = mem.sb(scope, "as_group_sum", [P, 4])
        total = mem.sb(scope, "as_total", [P, 1])
        acc = mem.sb(scope, "as_acc", [P, P])
        out_rows = mem.sb(scope, "as_out_rows", [P, P])
        kt_bank = [mem.ps(scope, f"as_kt_bank{i}") for i in range(2)]
        s_bank = [mem.ps(scope, f"as_s_bank{i}") for i in range(2)]
        c_bank = mem.ps(scope, "as_c_bank")
        pt_bank = [mem.ps(scope, f"as_pt_bank{i}") for i in range(2)]
        out_bank = mem.ps(scope, "as_out_bank")

        kc_landed, vc_landed, gate_in = mem.sem("as_kc_landed"), mem.sem("as_vc_landed"), mem.sem("as_gate_in")
        state_landed = [mem.sem(f"as_state_landed{i}") for i in range(HB)]
        pages_landed = [mem.sem(f"as_pages_landed{i}") for i in range(RING)]
        last_pages_landed = [mem.sem(f"as_last_pages_landed{i}") for i in range(RING)]
        q_packed, q_turned, q_ready, kn_ready = (mem.sem("as_q_packed"), mem.sem("as_q_turned"),
                                                 mem.sem("as_q_ready"), mem.sem("as_kn_ready"))
        c_done, kt_turned, kt_taken, s_done = (mem.sem("as_c_done"), mem.sem("as_kt_turned"),
                                               mem.sem("as_kt_taken"), mem.sem("as_s_done"))
        s_group, s_added = mem.sem("as_s_group"), mem.sem("as_s_added")
        maxed, exped = mem.sem("as_maxed"), mem.sem("as_exped")
        c_normed, g_done, win_ready = mem.sem("as_c_normed"), mem.sem("as_g_done"), mem.sem("as_win_ready")
        pt_turned, pt_taken, pv_done = mem.sem("as_pt_turned"), mem.sem("as_pt_taken"), mem.sem("as_pv_done")
        pv_group, acc_done = mem.sem("as_pv_group"), mem.sem("as_acc_done")
        out_ready, out_turned, out_taken = mem.sem("as_out_ready"), mem.sem("as_out_turned"), mem.sem("as_out_taken")
        dve_step, group_maxed = mem.sem("as_dve_step"), mem.sem("as_group_maxed")
        SOFT, BANKS, SUMS = 3 + KG, 1 + KG, 1 + KG
        S_TOKEN, ACC_TOKENS, RING_TOKENS = 1, RING, 2

        def load_pages(engine, kind, requests, landed_of_slot):
            for hb in range(HB):
                with engine.Fori(0, KG // RING) as i:
                    for s in range(RING):
                        engine.wait_ge(acc_done, SUMS * hb + (RING + 1) * i + s + 1)
                        for b in requests:
                            first = (RQ * hb + b) * NP + GP * RING * i + GP * s
                            _, numbers = nc.values_load_multi_w_load_instructions(
                                pages[0:1, bass.ds(first, GP)], [kind], min_val=0, max_val=cache_slc.shape[0] - 1)
                            for j, page in enumerate(numbers):
                                engine.dma_start(page_ring[s][:, b, j, :],
                                                 cache_slc[bass.ds(page, 1)].rearrange("a t n -> (a t) n")
                                                 ).then_inc(landed_of_slot[s], 16)

        with nc.Block() as block:
            @block.sync
            def _(sp):
                sp.dma_start(kc[:], kc_dram).then_inc(kc_landed, 16)
                sp.dma_start(vc[:], vc_dram).then_inc(vc_landed, 16)
                for b in range(DEC_BATCH):
                    sp.dma_start(gate[ROWS * (b % RQ):ROWS * (b % RQ + 1), b // RQ, :],
                                  gates_dram[DEC_SEQ * b:DEC_SEQ * b + DEC_SEQ, :].rearrange("t (h c) -> h t c", c=3)
                                  ).then_inc(gate_in, 16)
                load_pages(sp, mybir.EngineType.SP, range(RQ - 1), pages_landed)

            @block.gpsimd
            def _(pool):
                for b in range(RQ):
                    pool.dma_start(state[0][:, b], state_win[b].rearrange("(w p) n -> p w n", p=P)
                                   ).then_inc(state_landed[0], 16)
                for b in range(RQ):
                    pool.dma_start(state[1][:, b], state_win[RQ + b].rearrange("(w p) n -> p w n", p=P)
                                   ).then_inc(state_landed[1], 16)
                load_pages(pool, mybir.EngineType.Pool, [RQ - 1], last_pages_landed)

            @block.scalar
            def _(act):
                act.sem_inc(kt_taken, RING_TOKENS)
                act.sem_inc(pt_taken, RING_TOKENS)
                act.activation(q_rows[:], z_s[:, 0:NSA_WIDTH].rearrange("p (g r d) -> p r g d", g=N_KV, r=GROUP),
                               ACT.Copy, scale=SCALE).then_inc(q_packed, 1)
                act.wait_ge(q_turned, 2)
                act.activation(k_new[:], pt_bank[1][:, 0:2 * N_SAMPLE].rearrange("p (b n) -> p b n", b=2),
                               ACT.Copy).then_inc(kn_ready, 1)

                def take_kt(hb, group, b):
                    n = TURNS * hb + RQ * group + b
                    act.wait_ge(kt_turned, n + 1)
                    act.wait_ge(s_done, n + 1)
                    act.activation(kT[b % 2][:], kt_bank[b % 2][:], ACT.Copy).then_inc(kt_taken, 1)

                def take_pt(hb, n, i, rows, width=P):
                    act.wait_ge(pt_turned, UNITS * hb + n + 1)
                    act.wait_ge(pv_done, UNITS * hb + n + 1)
                    act.activation(pT[i][0:rows, 0:width], pt_bank[i][0:rows, 0:width], ACT.Copy).then_inc(pt_taken, 1)

                for hb in range(HB):
                    act.wait_ge(maxed, SOFT * hb + 1)
                    act.activation(p_cmp[:, 0:NBLK], c_bank[:, 0:NBLK], ACT.Exp, bias=small[:, 0, 0:1],
                                   accum_out=small[:, 1, 0:1]).then_inc(exped, 1)
                    for b in range(RQ):
                        take_kt(hb, 0, b)
                    act.wait_ge(maxed, SOFT * hb + 2)
                    act.activation(p_win[:], p_win[:], ACT.Exp, bias=small[:, 0, 2:3],
                                   accum_out=small[:, 1, 2:3]).then_inc(exped, 1)
                    act.wait_ge(maxed, SOFT * hb + 3)
                    act.activation(p_new[:], p_new[:], ACT.Exp, bias=neg_max[:, 3:4],
                                   accum_out=group_sum[:, 3:4]).then_inc(exped, 1)
                    for n in range(SIDE + 1):
                        take_pt(hb, n, n % 2, P if n < SIDE - 1 else NEW)
                    with act.Fori(0, KG // RING) as i:
                        for k in range(RING + 1):
                            g = RING * i + k
                            if k < RING:
                                take_kt(hb, g + 1, 0)
                            if k > 0:
                                take_pt(hb, SIDE + 1 + g - 1, (SIDE + k) % 2, P, BANK)
                            if k < RING:
                                for b in range(1, RQ):
                                    take_kt(hb, g + 1, b)
                                act.wait_ge(maxed, SOFT * hb + 4 + g)
                                act.activation(p_page[k % 2][:], p_page[k % 2][:], ACT.Exp, bias=neg_max[:, k:k + 1],
                                               accum_out=group_sum[:, k:k + 1])
                                before = (k + 3) % 4
                                act.activation(shrink[:, k:k + 1], neg_max[:, before:before + 1], ACT.Exp,
                                               bias=neg_max[:, k:k + 1], scale=-1.0).then_inc(exped, 1)

            @block.vector
            def _(dve):
                dve.sem_inc(s_added, S_TOKEN)
                dve.sem_inc(acc_done, ACC_TOKENS)
                step = Order(dve_step)
                step.did(dve.memset(q_diag[:], 0.0))
                step.did(dve.memset(grouped[:, 0, :], 0.0))
                step.did(dve.memset(p_cmp[:, NBLK:CB], 0.0))
                step.wait(dve)
                dve.wait_ge(q_turned, 1)
                for g in range(N_KV):
                    half = slice(g * HD, (g + 1) * HD)
                    qd = dve.tensor_copy(q_diag[half, :, g].rearrange("p b r t -> p r b t"),
                                         pt_bank[0][half, 0:GROUP * N_SAMPLE].rearrange(
                                             "p (r b t) -> p r b t", r=GROUP, t=DEC_SEQ))
                qd.then_inc(q_ready, 1)

                def factor(hb, branch, exponentials, gated=True):
                    f = small[:, 2, branch:branch + 1]
                    step.did(dve.tensor_scalar(f, exponentials, 1e-30, None, ALU.max))
                    step.wait(dve)
                    step.did(dve.reciprocal(f, f))
                    step.wait(dve)
                    if gated:
                        step.did(dve.tensor_tensor(f, f, gate[:, hb, branch:branch + 1], ALU.mult))
                        step.wait(dve)
                    return f

                def accumulate(hb, g, k):
                    dve.wait_ge(pv_group, SUMS * hb + g + 2)
                    dve.wait_ge(acc_done, ACC_TOKENS + SUMS * hb + g + 1)
                    dve.scalar_tensor_tensor(total[:], total[:], shrink[:, k:k + 1], group_sum[:, k:k + 1],
                                             ALU.mult, ALU.add)
                    dve.scalar_tensor_tensor(acc[:], acc[:], shrink[:, k:k + 1], out_bank[:, 0:P],
                                             ALU.mult, ALU.add).then_inc(acc_done, 1)

                for hb in range(HB):
                    dve.wait_ge(c_done, hb + 1)
                    step.did(dve.tensor_tensor(p_win[:, WINDOW:], c_bank[:, CB + NEW:CB + 2 * NEW],
                                               K["new_mask"][:, hb, :], ALU.add))
                    step.did(dve.tensor_tensor(p_new[:], c_bank[:, CB:CB + NEW], K["new_mask"][:, hb, :], ALU.add))
                    step.wait(dve)
                    dve.tensor_reduce(small[:, 0, 0:1], c_bank[:, 0:NBLK], AX.X, ALU.max,
                                      negate=True).then_inc(maxed, 1)
                    dve.wait_ge(s_group, BANKS * hb + 1)
                    dve.tensor_tensor(p_win[:, 0:WINDOW], s_bank[1][:], K["win_mask"][:], ALU.add).then_inc(s_added, 1)
                    dve.wait_ge(s_added, S_TOKEN + BANKS * hb + 1)
                    dve.tensor_reduce(small[:, 0, 2:3], p_win[:], AX.X, ALU.max, negate=True).then_inc(maxed, 1)
                    dve.tensor_reduce(neg_max[:, 3:4], p_new[:], AX.X, ALU.max, negate=True).then_inc(maxed, 1)
                    dve.wait_ge(exped, SOFT * hb + 1)
                    f = factor(hb, 0, small[:, 1, 0:1], False)
                    dve.tensor_scalar(p_cmp[:, 0:NBLK], p_cmp[:, 0:NBLK], f, None, ALU.mult).then_inc(c_normed, 1)
                    dve.wait_ge(c_normed, hb + 1)
                    dve.wait_ge(gate_in, 16 * DEC_BATCH)
                    step.did(dve.tensor_scalar(p_cmp_gated[:], p_cmp[:], gate[:, hb, 0:1], None, ALU.mult))
                    dve.wait_ge(exped, SOFT * hb + 2)
                    f = factor(hb, 2, small[:, 1, 2:3])
                    dve.tensor_scalar(p_win[:], p_win[:], f, None, ALU.mult).then_inc(win_ready, 1)
                    dve.wait_ge(g_done, hb + 1)
                    step.did(dve.tensor_copy(grouped[:, 1:, :], s_bank[0][:, 0:CB].rearrange("p (j c) -> p j c", c=4)))
                    step.wait(dve)
                    now, before = grouped[:, 1:, :], grouped[:, 0:NSLC, 3]
                    sc = score[0][:, 0:NSLC]
                    step.did(dve.tensor_tensor(sc, now[:, :, 0], now[:, :, 1], ALU.add))
                    step.wait(dve)
                    step.did(dve.tensor_tensor(sc, sc, now[:, :, 2], ALU.add))
                    step.wait(dve)
                    step.did(dve.scalar_tensor_tensor(sc, now[:, :, 3], 0.5, sc, ALU.mult, ALU.add))
                    step.wait(dve)
                    step.did(dve.scalar_tensor_tensor(sc, before, 0.5, sc, ALU.mult, ALU.add))
                    step.wait(dve)
                    step.did(dve.memset(score[0][:, 0:1], 1e4))
                    step.did(dve.memset(score[0][:, NSLC - 1:NSLC + 1], 1e4))
                    step.wait(dve)
                    for i in range(2):
                        step.did(dve.max(best[:], score[i][:]))
                        step.wait(dve)
                        step.did(dve.match_replace(score[1 - i][:], best[:], score[i][:], -1.0))
                        step.wait(dve)
                    step.did(dve.tensor_scalar(left_out[:], score[0][:, 0:NSLC], 0.0, NEG, ALU.is_ge, ALU.mult))
                    dve.wait_ge(pv_group, SUMS * hb + 1)
                    dve.wait_ge(exped, SOFT * hb + 3)
                    step.did(dve.tensor_copy(total[:], group_sum[:, 3:4]))
                    step.wait(dve)
                    dve.tensor_copy(acc[:], out_bank[:, 0:P]).then_inc(acc_done, 1)
                    with dve.Fori(0, KG // RING) as i:
                        for k in range(RING + 1):
                            g = RING * i + k
                            if k < RING:
                                dve.wait_ge(s_group, BANKS * hb + g + 2)
                                mask = left_out[:, bass.ds(BPG * g, BPG)].unsqueeze(2).to_broadcast(
                                    [P, BPG, SLC_BLOCK])
                                dve.tensor_tensor(p_page[k % 2][:].rearrange("p (j n) -> p j n", j=BPG),
                                                  s_bank[k % 2][:].rearrange("p (j n) -> p j n", j=BPG),
                                                  mask, ALU.add).then_inc(s_added, 1)
                                dve.wait_ge(s_added, S_TOKEN + BANKS * hb + g + 2)
                                dve.tensor_reduce(group_max[:], p_page[k % 2][:], AX.X, ALU.max,
                                                  negate=True).then_inc(group_maxed, 1)
                                dve.wait_ge(group_maxed, KG * hb + g + 1)
                                before = (k + 3) % 4
                                dve.tensor_tensor(neg_max[:, k:k + 1], neg_max[:, before:before + 1], group_max[:],
                                                  ALU.min).then_inc(maxed, 1)
                                dve.wait_ge(maxed, SOFT * hb + 4 + g)
                            if k > 0:
                                accumulate(hb, g - 1, k - 1)
                    dve.wait_ge(acc_done, ACC_TOKENS + SUMS * (hb + 1))
                    f = factor(hb, 1, total[:])
                    dve.scalar_tensor_tensor(out_rows[:], acc[:], f, c_bank[:, 0:P], ALU.mult,
                                             ALU.add).then_inc(out_ready, 1)
                    dve.wait_ge(out_turned, hb + 1)
                    src = kt_bank[0][:, 0:P].rearrange("p (b g r t) -> p b g r t", b=RQ, g=N_KV, r=GROUP)
                    for g in range(N_KV):
                        for r in range(GROUP):
                            half = slice((r % 2) * HD, (r % 2 + 1) * HD)
                            at = SEQ + RQ * DEC_SEQ * hb
                            last = dve.tensor_copy(
                                mixT[half, 2 * g + r // 2, at:at + RQ * DEC_SEQ].rearrange("p (b t) -> p b t", t=DEC_SEQ),
                                src[g * HD:(g + 1) * HD, :, g, r, :])
                    last.then_inc(out_taken, 1)

            @block.tensor
            def _(pe):
                pe.sem_inc(s_done, RING_TOKENS)
                pe.sem_inc(pv_done, RING_TOKENS)
                pe.wait_ge(q_packed, 1)
                for r in range(GROUP):
                    tr = pe.transpose(pt_bank[0][:, r * N_SAMPLE:(r + 1) * N_SAMPLE],
                                      q_rows[:, r].rearrange("p g d -> p (g d)"), K["ident"][0:N_SAMPLE, 0:N_SAMPLE])
                tr.then_inc(q_turned, 1)
                for i, off in enumerate((OFF_SLC, OFF_WIN)):
                    tr = pe.transpose(pt_bank[1][:, i * N_SAMPLE:(i + 1) * N_SAMPLE], z_s[:, off:off + P],
                                      K["ident"][0:N_SAMPLE, 0:N_SAMPLE])
                tr.then_inc(q_turned, 1)
                pe.wait_ge(kc_landed, 16)
                pe.wait_ge(q_ready, 1)
                pe.wait_ge(kn_ready, 1)

                def queries(b):
                    return q_diag[:, b].rearrange("p g r t -> p (g r t)")

                def turn_keys(hb, group, b, tiles):
                    n = TURNS * hb + RQ * group + b
                    pe.wait_ge(kt_taken, n + 1)
                    for j in range(GP):
                        tr = pe.transpose(kt_bank[b % 2][:, j * P:(j + 1) * P], tiles[j], K["ident"][:])
                    tr.then_inc(kt_turned, 1)

                def key_scores(hb, group, b, bank):
                    n = TURNS * hb + RQ * group + b
                    pe.wait_ge(kt_taken, n + RING_TOKENS + 1)
                    mm = pe.matmul(bank[ROWS * b:ROWS * (b + 1), :], queries(RQ * hb + b), kT[b % 2][:],
                                   start=True, stop=True)
                    mm.then_inc(s_done, 1)
                    if b == RQ - 1:
                        pe.wait_ge(s_done, n + RING_TOKENS + 1)
                        pe.nop().then_inc(s_group, 1)

                def key_group(hb, group, bank, tiles, behind_first=None):
                    for b in range(RQ + 1):
                        if b < RQ:
                            turn_keys(hb, group, b, tiles(b))
                        if b == 0 and behind_first:
                            behind_first()
                        if b > 0:
                            key_scores(hb, group, b - 1, bank)

                def turn_probs(hb, n, i, source, rows):
                    pe.wait_ge(pt_taken, UNITS * hb + n + 1)
                    pe.transpose(pt_bank[i][0:rows, 0:P], source, K["ident"][:]).then_inc(pt_turned, 1)

                def value_product(hb, n, i, rows, values, bank, first, last):
                    pe.wait_ge(pt_taken, UNITS * hb + n + RING_TOKENS + 1)
                    for b in range(RQ):
                        mm = pe.matmul(bank[ROWS * b:ROWS * (b + 1), 0:P], pT[i][0:rows, ROWS * b:ROWS * (b + 1)],
                                       values(b), start=first, stop=last)
                    mm.then_inc(pv_done, 1)

                def turn_group(hb, g, k):
                    n = SIDE + 1 + g
                    pe.wait_ge(exped, SOFT * hb + g + 4)
                    pe.wait_ge(pt_taken, UNITS * hb + n + 1)
                    for j in range(GP):
                        tr = pe.transpose(pt_bank[(SIDE + 1 + k) % 2][:, j * P:(j + 1) * P],
                                          p_page[k % 2][:, j * P:(j + 1) * P], K["ident"][:])
                    tr.then_inc(pt_turned, 1)

                def group_values(hb, g, k):
                    n = SIDE + 1 + g
                    pe.wait_ge(acc_done, ACC_TOKENS + SUMS * hb + g + 1)
                    pe.wait_ge(pt_taken, UNITS * hb + n + RING_TOKENS + 1)
                    for j in range(GP):
                        for b in range(RQ):
                            mm = pe.matmul(out_bank[ROWS * b:ROWS * (b + 1), 0:P],
                                           pT[(SIDE + 1 + k) % 2][:, j * P + ROWS * b:j * P + ROWS * (b + 1)],
                                           page_ring[k][:, b, j, P:2 * P], start=(j == 0), stop=(j == GP - 1))
                    mm.then_inc(pv_done, 1)
                    pe.wait_ge(pv_done, UNITS * hb + n + RING_TOKENS + 1)
                    pe.nop().then_inc(pv_group, 1)

                for hb in range(HB):
                    if hb:
                        pe.wait_ge(out_ready, hb)
                    for b in range(RQ):
                        rows = slice(ROWS * b, ROWS * (b + 1))
                        pe.matmul(c_bank[rows, 0:NBLK], queries(RQ * hb + b), kc[:, RQ * hb + b, 0:NBLK],
                                  start=True, stop=True)
                        for i in range(2):
                            mm = pe.matmul(c_bank[rows, CB + i * NEW:CB + (i + 1) * NEW], queries(RQ * hb + b),
                                           k_new[:, i, :], start=True, stop=True)
                    mm.then_inc(c_done, 1)
                    pe.wait_ge(state_landed[hb], 16 * RQ)
                    if hb:
                        pe.wait_ge(s_added, S_TOKEN + BANKS * hb)
                        pe.wait_ge(out_taken, hb)
                    key_group(hb, 0, s_bank[1], lambda b: [state[hb][:, b, j, 0:P] for j in range(WT)])
                    pe.wait_ge(c_normed, hb + 1)
                    pe.matmul(s_bank[0][:, 0:CB], K["head_sum"][:], p_cmp[:], start=True, stop=True).then_inc(g_done, 1)
                    units = [(p_cmp_gated[:, i * P:(i + 1) * P], P, lambda b, i=i: vc[:, RQ * hb + b, i, :])
                             for i in range(CB // P)]
                    units += [(p_win[:, i * P:(i + 1) * P], P, lambda b, i=i: state[hb][:, b, i, P:2 * P])
                              for i in range(WT)]
                    units += [(p_win[:, WINDOW:], NEW, lambda b: z_s[:, OFF_WIN + P:OFF_WIN + 2 * P])]
                    units += [(p_new[:], NEW, lambda b: z_s[:, OFF_SLC + P:OFF_SLC + 2 * P])]
                    pe.wait_ge(vc_landed, 16)
                    pe.wait_ge(win_ready, hb + 1)
                    for n in range(SIDE + 2):
                        if n < SIDE + 1:
                            if n == SIDE:
                                pe.wait_ge(exped, SOFT * hb + 3)
                            turn_probs(hb, n, n % 2, units[n][0], units[n][1])
                        if 0 < n <= SIDE:
                            value_product(hb, n - 1, (n - 1) % 2, units[n - 1][1], units[n - 1][2], c_bank,
                                          n == 1, n == SIDE)
                    value_product(hb, SIDE, SIDE % 2, NEW, units[SIDE][2], out_bank, True, True)
                    pe.wait_ge(pv_done, UNITS * hb + SIDE + 1 + RING_TOKENS)
                    pe.nop().then_inc(pv_group, 1)
                    with pe.Fori(0, KG // RING) as i:
                        for k in range(RING + 1):
                            g = RING * i + k
                            if k < RING:
                                pe.wait_ge(pages_landed[k], 16 * (RQ - 1) * GP * (KG // RING * hb + i + 1))
                                pe.wait_ge(last_pages_landed[k], 16 * GP * (KG // RING * hb + i + 1))
                                pe.wait_ge(s_added, S_TOKEN + BANKS * hb + g)
                                if k == 0:
                                    pe.wait_ge(acc_done, ACC_TOKENS + SUMS * hb + g + 1)
                                key_group(hb, g + 1, s_bank[k % 2],
                                          lambda b, k=k: [page_ring[k][:, b, j, 0:P] for j in range(GP)],
                                          (lambda g=g, k=k: turn_group(hb, g - 1, k - 1)) if k else None)
                            else:
                                turn_group(hb, g - 1, k - 1)
                            if k > 0:
                                group_values(hb, g - 1, k - 1)
                    pe.wait_ge(out_ready, hb + 1)
                    pe.transpose(kt_bank[0][:, 0:P], out_rows[:], K["ident"][:]).then_inc(out_turned, 1)


def stage_out_project(nc, mem, K, trunk, x_saved, w_out):
    mixT = xT = trunk
    w_view = w_out.rearrange("(k p) (m n) -> p m k n", p=P, n=P)
    with ExitStack() as scope:
        mix_hi = mem.sb(scope, "op_mix_hi", [P, KT, T], F32R)
        mix_lo = mem.sb(scope, "op_mix_lo", [P, KT, T], F32R)
        w_raw = [mem.sb(scope, f"op_w_raw{i}", [P, KT, P]) for i in range(2)]
        w_hi = [mem.sb(scope, f"op_w_hi{i}", [P, KT, P], F32R) for i in range(2)]
        w_lo = [mem.sb(scope, f"op_w_lo{i}", [P, KT, P], F32R) for i in range(2)]
        banks = [mem.ps(scope, f"op_bank{i}") for i in range(4)]
        x_in, w_landed = mem.sem("op_x_in"), [mem.sem(f"op_w_landed{i}") for i in range(2)]
        mix_hi_done, mix_split = mem.sem("op_mix_hi_done"), mem.sem("op_mix_split")
        w_hi_done, w_split = mem.sem("op_w_hi_done"), mem.sem("op_w_split")
        done, added = mem.sem("op_done"), mem.sem("op_added")

        with nc.Block() as block:
            @block.sync
            def _(sp):
                for m in range(KT):
                    if m >= 2:
                        sp.wait_ge(w_split, m - 1)
                    sp.dma_start(w_raw[m % 2][:], w_view[:, m]).then_inc(w_landed[m % 2], 16)
                    if m == 2:
                        sp.wait_ge(mix_split, CHUNKS)
                        sp.dma_start(xT[:], x_saved).then_inc(x_in, 16)

            @block.scalar
            def _(act):
                def high(m):
                    act.wait_ge(w_landed[m % 2], 16 * (m // 2) + 16)
                    if m >= 2:
                        act.wait_ge(done, CHUNKS * (m - 1))
                    act.activation(w_hi[m % 2][:], w_raw[m % 2][:], ACT.Copy).then_inc(w_hi_done, 1)

                for c in range(CHUNKS):
                    act.activation(mix_hi[:, :, chunk(c)], mixT[:, :, chunk(c)], ACT.Copy).then_inc(mix_hi_done, 1)
                    if c == 0:
                        high(0)
                for m in range(1, KT):
                    high(m)

            @block.vector
            def _(dve):
                def low(m):
                    dve.wait_ge(w_hi_done, m + 1)
                    dve.tensor_tensor(w_lo[m % 2][:], w_raw[m % 2][:], w_hi[m % 2][:].bitcast(F32),
                                      ALU.subtract).then_inc(w_split, 1)

                for c in range(CHUNKS):
                    if c == 1:
                        low(0)
                    dve.wait_ge(mix_hi_done, c + 1)
                    dve.tensor_tensor(mix_lo[:, :, chunk(c)], mixT[:, :, chunk(c)],
                                      mix_hi[:, :, chunk(c)].bitcast(F32), ALU.subtract).then_inc(mix_split, 1)
                dve.wait_ge(x_in, 16)
                for m in range(KT):
                    if m + 1 < KT:
                        low(m + 1)
                    for c in range(CHUNKS):
                        n = CHUNKS * m + c
                        dve.wait_ge(done, n + 1)
                        dve.tensor_tensor(xT[:, m, chunk(c)], xT[:, m, chunk(c)], banks[n % 4][:, 0:CH],
                                          ALU.add).then_inc(added, 1)

            @block.tensor
            def _(pe):
                for m in range(KT):
                    pe.wait_ge(w_split, m + 1)
                    for c in range(CHUNKS):
                        n = CHUNKS * m + c
                        if m == 0:
                            pe.wait_ge(mix_split, c + 1)
                        if n >= 4:
                            pe.wait_ge(added, n - 3)
                        for k in range(KT):
                            mm = product3(pe, banks[n % 4][:, 0:CH], w_hi[m % 2][:, k, :], w_lo[m % 2][:, k, :],
                                          mix_hi[:, k, chunk(c)], mix_lo[:, k, chunk(c)], k == 0, k == KT - 1)
                        mm.then_inc(done, 1)


def stage_finish(nc, mem, K, xT, gain, y_prompt, y_sample, states_copied, n_states_copied):
    with ExitStack() as scope:
        h = mem.sb(scope, "fin_h", [P, KT, T])
        y = [mem.sb(scope, f"fin_y{i}", [P, D_MODEL]) for i in range(3)]
        norm = Norm(mem, scope, K, "fin", split=False)
        banks = [mem.ps(scope, f"fin_bank{i}") for i in range(4)]
        sum_bank = mem.ps(scope, "fin_sum")
        turned, taken = mem.sem("fin_turned"), mem.sem("fin_taken")
        out_sem = [mem.sem(f"fin_out{i}") for i in range(3)]

        with nc.Block() as block:
            @block.sync
            def _(sp):
                norm.load(sp, gain)
                for t in range(TT):
                    sp.wait_ge(taken, 2 * t + 2)
                    target = y_prompt[t * P:(t + 1) * P, :] if t < TT - 1 else y_sample
                    n = P if t < TT - 1 else N_SAMPLE
                    sp.dma_start(target, y[t % 3][0:n, :]).then_inc(out_sem[t % 3], 16)
                sp.wait_ge(states_copied, n_states_copied)
                for i in range(3):
                    sp.wait_ge(out_sem[i], 16 * (TT // 3))

            @block.scalar
            def _(act):
                norm.scalar(act, xT, h)
                for t in range(TT):
                    n = P if t < TT - 1 else N_SAMPLE
                    if t >= 3:
                        act.wait_ge(out_sem[t % 3], 16 * (t // 3))
                    for half in range(2):
                        u = 2 * t + half
                        act.wait_ge(turned, u + 1)
                        act.activation(y[t % 3][0:n, half * BANK:(half + 1) * BANK], banks[u % 4][0:n, :],
                                       ACT.Copy).then_inc(taken, 1)

            @block.vector
            def _(dve):
                norm.vector(dve, xT, sum_bank, h, None)

            @block.tensor
            def _(pe):
                for c in range(CHUNKS):
                    norm.tensor(pe, sum_bank, c)
                for t in range(TT):
                    n = P if t < TT - 1 else N_SAMPLE
                    pe.wait_ge(norm.h_done, 2 * -(-(t * P + n) // CH))
                    for half in range(2):
                        u = 2 * t + half
                        if u >= 4:
                            pe.wait_ge(taken, u - 3)
                        for k in range(4):
                            tr = pe.transpose(banks[u % 4][0:n, k * P:(k + 1) * P],
                                              h[:, 4 * half + k, t * P:t * P + n], K["ident"][:])
                        tr.then_inc(turned, 1)


def stage_constants(nc, mem, targets, narrow=()):
    landed = mem.sem("const_landed")
    with nc.Block() as block:
        @block.sync
        def _(sp):
            for target, source in targets:
                sp.dma_start(target, source).then_inc(landed, 16)
            sp.wait_ge(landed, 16 * len(targets))

        @block.vector
        def _(dve):
            dve.wait_ge(landed, 16 * len(targets))
            for source, target in narrow:
                dve.tensor_copy(target, source)


def stage_copy(nc, mem, pairs):
    copied = mem.sem("copied")
    with nc.Block() as block:
        @block.sync
        def _(sp):
            for target, source in pairs:
                sp.dma_start(target, source).then_inc(copied, 16)
            sp.wait_ge(copied, 16 * len(pairs))


def trunk_step(nc, x_prompt, x_sample, cache_cmp, cache_slc, page_table, state_win, state_pool,
               n_ffn1, w1_gate, w1_up, w1_down, n_mix, w_in, w_cmp_k1, w_cmp_k2, pe_k, w_cmp_v1, w_cmp_v2, pe_v,
               w_pool, pool_scale, w_out, n_ffn2, w2_gate, w2_up, w2_down, n_final,
               c_ident, c_ones, c_cos, c_sin, c_inv_count, c_diagonal, c_edge, c_blocks, c_has_block, c_head_sum,
               c_new_mask, c_win_mask,
               y_prompt, y_sample, new_cmp_prompt, new_slc_prompt, new_win_prompt, new_pool_prompt,
               new_cmp_sample, new_slc_sample, new_win_sample, new_pool_sample):
    x_saved = nc.dram_tensor("x_saved", [P, KT, T], F32).ap()
    kc_saved = nc.dram_tensor("kc_saved", [P, DEC_BATCH, PAST_LEN // CMP_STRIDE], F32).ap()
    vc_saved = nc.dram_tensor("vc_saved", [P, DEC_BATCH, 2, P], F32).ap()
    gates_saved = nc.dram_tensor("gates_saved", [N_SAMPLE, 3 * N_HEADS], F32).ap()
    n_pages = PAST_LEN // PAGE
    BF16 = mybir.dt.bfloat16

    def flat(a):
        return a.rearrange("o b t c g d -> (o b t) (c g d)")

    cmp_weights = ((w_cmp_k1[0], w_cmp_v1[0]), (w_cmp_k2[0], w_cmp_v2[0]), (pe_k, pe_v))
    with ExitStack() as whole:
        mem = Mem(nc)
        K = {"ident": mem.sb(whole, "ident", [P, P]), "ones": mem.sb(whole, "ones", [P, P])}
        pages = mem.sb(whole, "pages", [1, DEC_BATCH * n_pages], I32)
        cmp_bias = mem.sb(whole, "cmp_bias", [P, 2 * CMP_HIDDEN // P])
        stage_constants(nc, mem, [(K["ident"][:], c_ident), (K["ones"][:], c_ones), (pages[:], page_table)])

        with ExitStack() as scope:
            kc = mem.sb(scope, "kc", [P, DEC_BATCH, PAST_LEN // CMP_STRIDE])
            vc = mem.sb(scope, "vc", [P, DEC_BATCH, 2, P])
            stage_compress(nc, mem, K, pages, cache_cmp[0].rearrange("a (c s) k g d -> a c (s k g d)", s=CMP_STRIDE),
                           n_pages, DEC_BATCH, PAST_LEN // CMP_STRIDE, *cmp_weights, kc, vc, "cs", cmp_bias)
            mem.end_stage()
            stage_copy(nc, mem, [(kc_saved, kc[:]), (vc_saved, vc[:])])

        trunk = mem.sb(whole, "trunk", [P, KT, T])
        win_rows = WINDOW - DEC_SEQ
        state_copies = [(new_win_sample[0, b].rearrange("t c g d -> t (c g d)")[0:win_rows, :],
                         state_win[0, b].rearrange("t c g d -> t (c g d)")[DEC_SEQ:WINDOW, :]) for b in range(DEC_BATCH)]
        state_copies.append((new_pool_sample[0, :, 0:POOL_STATE - DEC_SEQ, :], state_pool[0, :, DEC_SEQ:POOL_STATE, :]))
        states_copied = mem.lasting_sem("states_copied")
        stage_load_x(nc, mem, K, trunk, x_prompt[0], x_sample.rearrange("b t n -> (b t) n"))
        mem.end_stage()
        stage_ffn(nc, mem, K, trunk, n_ffn1, w1_gate[0], w1_up[0], w1_down[0], "f1",
                  state_copies, states_copied)
        mem.end_stage()

        with ExitStack() as mixer:
            z_sample = mem.sb(mixer, "z_sample", [N_SAMPLE, OFF_POOL])
            with ExitStack() as scope_z:
                z = mem.sb(scope_z, "z", [P, TT, OFF_POOL])
                with ExitStack() as scope:
                    for name, shape in (("cos", [P, TT, 8]), ("sin", [P, TT, 8]), ("inv_count", [P, 4, 16])):
                        K[name] = mem.sb(scope, name, shape)
                    stage_constants(nc, mem, [(K["cos"][:], c_cos), (K["sin"][:], c_sin),
                                              (K["inv_count"][:], c_inv_count)])
                    uT = mem.sb(scope, "uT", [P, 4, T])
                    outs = dict(cmp_prompt=flat(new_cmp_prompt), cmp_sample=flat(new_cmp_sample),
                                slc_prompt=flat(new_slc_prompt), slc_sample=flat(new_slc_sample),
                                win_prompt=flat(new_win_prompt), x=x_saved, gates=gates_saved)
                    stage_in_project(nc, mem, K, trunk, n_mix, w_in[0], z, z_sample, uT, outs)
                    mem.end_stage()
                    stage_pool(nc, mem, K, uT, trunk, state_pool[0], w_pool[0], pool_scale, new_pool_prompt[0, 0],
                               new_pool_sample[0])
                    mem.end_stage()
                kcp = mem.sb(scope_z, "kcp", [P, 1, SEQ // CMP_STRIDE])
                vcp = mem.sb(scope_z, "vcp", [P, 1, 1, P])
                spare = trunk[:, 0:4, :].rearrange("p k t -> p (k t)")[:, 0:CMP_STRIDE * KV_WIDTH]
                stage_compress(nc, mem, K, None, flat(new_cmp_prompt).rearrange("(c s) n -> c (s n)", s=CMP_STRIDE),
                               0, 1, SEQ // CMP_STRIDE, *cmp_weights, kcp, vcp, "cp", cmp_bias, True, spare)
                mem.end_stage()
                with ExitStack() as scope:
                    for name, width in (("ident16", P), ("diagonal", P), ("edge", P), ("blocks", 120)):
                        K[name] = mem.sb(scope, name, [P, width], BF16)
                    K["has_block"] = mem.sb(scope, "has_block", [P, 1])
                    with ExitStack() as wide_scope:
                        wide = {name: mem.sb(wide_scope, name + "_wide", [P, width])
                                for name, width in (("diagonal", P), ("edge", P), ("blocks", 120))}
                        stage_constants(nc, mem, [(wide["diagonal"][:], c_diagonal), (wide["edge"][:], c_edge),
                                                  (wide["blocks"][:], c_blocks), (K["has_block"][:], c_has_block)],
                                        [(K["ident"][:], K["ident16"][:])]
                                        + [(wide[name][:], K[name][:]) for name in wide])
                    stage_attend_prompt(nc, mem, K, z, kcp[:, 0], vcp[:, 0, 0], trunk)
                    mem.end_stage()
            for name, shape in (("head_sum", [P, P]), ("new_mask", [P, 2, N_SAMPLE]), ("win_mask", [P, WINDOW])):
                K[name] = mem.sb(mixer, name, shape)
            new_rows = [(new_win_sample[0, b].rearrange("t c g d -> t (c g d)")[win_rows:WINDOW, :],
                         z_sample[DEC_SEQ * b:DEC_SEQ * b + DEC_SEQ, OFF_WIN:OFF_GATE]) for b in range(DEC_BATCH)]
            stage_constants(nc, mem, [(K["head_sum"][:], c_head_sum), (K["new_mask"][:], c_new_mask),
                                      (K["win_mask"][:], c_win_mask)] + new_rows)
            stage_attend_sample(nc, mem, K, z_sample, pages, cache_slc[0].rearrange("a t c g d -> a t (c g d)"),
                                state_win[0].rearrange("b t c g d -> b t (c g d)"), kc_saved, vc_saved,
                                gates_saved, trunk)
            mem.end_stage()
        stage_out_project(nc, mem, K, trunk, x_saved, w_out[0])
        mem.end_stage()
        stage_ffn(nc, mem, K, trunk, n_ffn2, w2_gate[0], w2_up[0], w2_down[0], "f2")
        mem.end_stage()
        stage_finish(nc, mem, K, trunk, n_final, y_prompt[0], y_sample.rearrange("b t n -> (b t) n"),
                     states_copied, 16 * len(state_copies))
        mem.end_stage()


_INS = ["x_prompt", "x_sample", "cache_kv_cmp", "cache_kv_slc", "page_table", "state_kv_win", "state_pool",
        "n_ffn1", "w_ffn1_gate", "w_ffn1_up", "w_ffn1_down", "n_mix", "w_in", "w_cmp_k1", "w_cmp_k2", "pe_cmp_k",
        "w_cmp_v1", "w_cmp_v2", "pe_cmp_v", "w_pool", "pool_scale", "w_out", "n_ffn2", "w_ffn2_gate", "w_ffn2_up",
        "w_ffn2_down", "n_final"]
_KV = (2, N_KV, HD)
_OUTS = [(1, SEQ, D_MODEL), (DEC_BATCH, DEC_SEQ, D_MODEL), (1, 1, SEQ, *_KV), (1, 1, SEQ, *_KV), (1, 1, WINDOW, *_KV),
         (1, 1, POOL_STATE, POOL_WIDTH), (1, DEC_BATCH, DEC_SEQ, *_KV), (1, DEC_BATCH, DEC_SEQ, *_KV),
         (1, DEC_BATCH, WINDOW, *_KV), (1, DEC_BATCH, POOL_STATE, POOL_WIDTH)]


def shape_constants():
    f32 = np.float32
    inv = np.power(f32(500000.0), -np.arange(8, dtype=f32) / f32(8)).astype(f32)
    pos = np.concatenate([np.arange(SEQ), np.tile(PAST_LEN + np.arange(DEC_SEQ), DEC_BATCH),
                          np.zeros(TT * P - T)]).astype(f32)
    ang = pos[:, None] * inv
    tiles = lambda a: np.ascontiguousarray(a.reshape(TT, P, 8).transpose(1, 0, 2))
    inv_count = np.zeros((P, 4, 16), f32)
    for g, w in enumerate(POOL_WINDOWS):
        inv_count[:, g] = 1 / np.minimum(w, np.arange(16) + 1)
    row, col = np.arange(P)[:, None], np.arange(P)[None]
    starts = np.arange(120)[None] - 56
    req, kvh, tok = row // 32, (row // 16) % 2, row % 4
    new_mask = np.zeros((P, 2, N_SAMPLE), f32)
    key = np.arange(N_SAMPLE)[None]
    for half in range(2):
        new_mask[:, half] = np.where((key // DEC_SEQ == 4 * half + req) & (key % DEC_SEQ <= tok), 0, NEG)
    return dict(
        ident=np.eye(P, dtype=f32), ones=np.ones((P, P), f32), cos=tiles(np.cos(ang)), sin=tiles(np.sin(ang)),
        inv_count=inv_count, diagonal=np.where(col <= row, 0, NEG).astype(f32),
        edge=np.where(col >= row, 0, NEG).astype(f32),
        blocks=np.where(CMP_STRIDE * starts + CMP_BLOCK - 1 <= row, 0, NEG).astype(f32),
        has_block=(row >= CMP_BLOCK - 1).astype(f32),
        head_sum=((req == req.T) & (kvh == kvh.T) & (tok == tok.T)).astype(f32),
        new_mask=new_mask, win_mask=np.where(np.arange(WINDOW)[None] >= tok, 0, NEG).astype(f32))


def kernel(**inputs):
    import concourse.bacc as bacc
    from concourse.bass_utils import run_bass_kernel_spmd

    nc = bacc.Bacc("TRN2", target_bir_lowering=False, num_devices=1)

    def columns(a):
        return np.ascontiguousarray(a.reshape(-1, P).T)

    arrays, args = {}, []
    for name in _INS:
        a = np.ascontiguousarray(inputs[name])
        if name in ("n_ffn1", "n_mix", "n_ffn2", "n_final", "pool_scale", "pe_cmp_k", "pe_cmp_v"):
            a = columns(a)
        if name == "page_table":
            a = a.reshape(1, -1)
        arrays[f"in_{name}_dram"] = a
    for name, a in shape_constants().items():
        arrays[f"const_{name}_dram"] = a
    for name, a in arrays.items():
        args.append(nc.dram_tensor(name, a.shape, mybir.dt.from_np(a.dtype), kind="ExternalInput").ap())
    for i, shape in enumerate(_OUTS):
        args.append(nc.dram_tensor(f"out_{i}_dram", shape, F32, kind="ExternalOutput").ap())
    trunk_step(nc, *args)
    r = run_bass_kernel_spmd(nc, [arrays], core_ids=[0])
    return tuple(r.results[0][f"out_{i}_dram"] for i in range(len(_OUTS)))
```
